# Optimizing a Trainium2 kernel written in Bass

```python
import math
import jax, jax.numpy as jnp
from jax import lax
import numpy as np

D_MODEL = 1024
BATCH = 1
SEQ = 256
DEPTH = 2

EPS = 1e-6
A_HEADS = 8
A_DHEAD = 64
A_QK = A_HEADS * 2 * A_DHEAD
A_V = A_HEADS * 2 * A_DHEAD
Q_BLOCK = 128
M_HEADS = 8
M_DQK = 64
M_DV = 128
M_QK = M_HEADS * M_DQK
M_V = M_HEADS * M_DV
CONV_K = 4
CHUNK = 64
F_BIAS_OFFSET = 3.0
D_FF = 2816
FFN_SCALE = 0.5
SPLIT_SIZES = [A_QK, A_QK, A_V, M_QK, M_QK, M_V, M_V, M_HEADS, M_HEADS, 2 * D_MODEL]
SPLIT_IDX = [int(v) for v in np.cumsum(SPLIT_SIZES)[:-1]]
C_IN = int(sum(SPLIT_SIZES))


def rmsnorm(x, w):
    xf = x.astype(jnp.float32)
    y = xf * lax.rsqrt(jnp.mean(xf * xf, axis=-1, keepdims=True) + EPS)
    return (y * w.astype(jnp.float32)).astype(x.dtype)

def swiglu(h, w_gu, w_down):
    g, u = jnp.split(h @ w_gu, 2, axis=-1)
    return (jax.nn.silu(g) * u) @ w_down

def causal_depthwise_conv(x, w, b):
    c = x.shape[-1]
    y = lax.conv_general_dilated(x, w[:, None, :].astype(x.dtype), window_strides=(1,),
                                 padding=[(CONV_K - 1, 0)],
                                 dimension_numbers=('NWC', 'WIO', 'NWC'),
                                 feature_group_count=c)
    return y + b

def diff_attention(q, k, v, lam, lam_init, norm_w):
    b_, s_, _ = q.shape
    nb = s_ // Q_BLOCK
    scale = A_DHEAD ** -0.5
    qb = q.reshape(b_, nb, Q_BLOCK, A_HEADS, 2, A_DHEAD).transpose(1, 0, 3, 4, 2, 5)
    kh = k.reshape(b_, s_, A_HEADS, 2, A_DHEAD).transpose(0, 2, 3, 1, 4)
    vh = v.reshape(b_, s_, A_HEADS, 2 * A_DHEAD).transpose(0, 2, 1, 3)
    k_pos = jnp.arange(s_)
    lam32 = lam.astype(jnp.float32)

    def block(args):
        qblk, idx = args
        sc = jnp.einsum('bhmqd,bhmkd->bhmqk', qblk, kh).astype(jnp.float32) * scale
        q_pos = idx * Q_BLOCK + jnp.arange(Q_BLOCK)
        causal = k_pos[None, :] <= q_pos[:, None]
        sc = jnp.where(causal, sc, -jnp.inf)
        p = jax.nn.softmax(sc, axis=-1)
        a = p[:, :, 0] - lam32 * p[:, :, 1]
        return jnp.einsum('bhqk,bhkv->bhqv', a.astype(vh.dtype), vh)

    o = lax.map(block, (qb, jnp.arange(nb)))
    o = o.transpose(1, 0, 3, 2, 4).reshape(b_, s_, A_HEADS, 2 * A_DHEAD)
    o = rmsnorm(o, norm_w) * (1.0 - lam_init)
    return o.reshape(b_, s_, A_V)

def mlstm_chunkwise(q, k, v, ig, fg):
    b_, s_ = q.shape[:2]
    nc = s_ // CHUNK
    f32 = jnp.float32

    def chunk(t, d):
        return t.astype(f32).reshape(b_, nc, CHUNK, M_HEADS, d).transpose(0, 3, 1, 2, 4)

    qc = chunk(q, M_DQK) * (M_DQK ** -0.5)
    kc = chunk(k, M_DQK)
    vc = chunk(v, M_DV)
    igc = ig.astype(f32).reshape(b_, nc, CHUNK, M_HEADS).transpose(0, 3, 1, 2)
    logf = jax.nn.log_sigmoid(fg.astype(f32)).reshape(b_, nc, CHUNK, M_HEADS).transpose(0, 3, 1, 2)
    bcum = jnp.cumsum(logf, axis=-1)
    b_last = bcum[..., -1]

    a = b_last[..., None] - bcum + igc
    m_loc = jnp.max(a, axis=-1)
    w = jnp.exp(a - m_loc[..., None])
    c_loc = jnp.einsum('bhcl,bhcld,bhclv->bhcdv', w, kc, vc)
    n_loc = jnp.einsum('bhcl,bhcld->bhcd', w, kc)

    def step(carry, xs):
        c_st, n_st, m_st = carry
        bl, ml, cl, nl = xs
        m_new = jnp.maximum(bl + m_st, ml)
        sp = jnp.exp(bl + m_st - m_new)
        sl = jnp.exp(ml - m_new)
        c_new = sp[..., None, None] * c_st + sl[..., None, None] * cl
        n_new = sp[..., None] * n_st + sl[..., None] * nl
        return (c_new, n_new, m_new), (c_st, n_st, m_st)

    init = (jnp.zeros((b_, M_HEADS, M_DQK, M_DV), f32),
            jnp.zeros((b_, M_HEADS, M_DQK), f32),
            jnp.zeros((b_, M_HEADS), f32))
    xs = (jnp.moveaxis(b_last, 2, 0), jnp.moveaxis(m_loc, 2, 0),
          jnp.moveaxis(c_loc, 2, 0), jnp.moveaxis(n_loc, 2, 0))
    _, (c_prev, n_prev, m_prev) = lax.scan(step, init, xs)
    c_prev = jnp.moveaxis(c_prev, 0, 2)
    n_prev = jnp.moveaxis(n_prev, 0, 2)
    m_prev = jnp.moveaxis(m_prev, 0, 2)

    tril = jnp.tril(jnp.ones((CHUNK, CHUNK), dtype=bool))
    dmat = bcum[..., :, None] - bcum[..., None, :] + igc[..., None, :]
    dmat = jnp.where(tril, dmat, -jnp.inf)
    m_inter = bcum + m_prev[..., None]
    m_t = jnp.maximum(m_inter, jnp.max(dmat, axis=-1))
    sc_inter = jnp.exp(m_inter - m_t)
    p = jnp.exp(dmat - m_t[..., None]) * jnp.einsum('bhcld,bhcsd->bhcls', qc, kc)
    num = sc_inter[..., None] * jnp.einsum('bhcld,bhcdv->bhclv', qc, c_prev) + \
        jnp.einsum('bhcls,bhcsv->bhclv', p, vc)
    den = sc_inter * jnp.einsum('bhcld,bhcd->bhcl', qc, n_prev) + jnp.sum(p, axis=-1)
    h = num / jnp.maximum(jnp.abs(den), jnp.exp(-m_t))[..., None]
    h = h.transpose(0, 2, 3, 1, 4).reshape(b_, s_, M_HEADS, M_DV)
    return h.astype(q.dtype)

def first_inputs(seed: int = 0) -> dict:
    key = jax.random.key(seed)
    ks = iter(jax.random.split(key, 32))
    L = DEPTH

    def nrm(shape, scale):
        return scale * jax.random.normal(next(ks), shape, jnp.float32)

    def gain(shape):
        return 1.0 + nrm(shape, 0.05)

    return {
        "x": nrm((BATCH, SEQ, D_MODEL), 1.0),
        "ffn1_norm_pre": gain((L, D_MODEL)),
        "ffn1_w_gu": nrm((L, D_MODEL, 2 * D_FF), D_MODEL ** -0.5),
        "ffn1_w_down": nrm((L, D_FF, D_MODEL), D_FF ** -0.5),
        "ffn1_norm_post": gain((L, D_MODEL)),
        "mix_norm_pre": gain((L, D_MODEL)),
        "w_in": nrm((L, D_MODEL, C_IN), D_MODEL ** -0.5),
        "attn_lam_q1": nrm((L, A_DHEAD), 0.1),
        "attn_lam_k1": nrm((L, A_DHEAD), 0.1),
        "attn_lam_q2": nrm((L, A_DHEAD), 0.1),
        "attn_lam_k2": nrm((L, A_DHEAD), 0.1),
        "attn_norm_w": gain((L, 2 * A_DHEAD)),
        "conv_w": nrm((L, CONV_K, 2 * M_QK), CONV_K ** -0.5),
        "conv_b": nrm((L, 2 * M_QK), 0.02),
        "igate_b": nrm((L, M_HEADS), 0.1),
        "fgate_b": F_BIAS_OFFSET + nrm((L, M_HEADS), 0.5),
        "mlstm_norm_w": gain((L, M_HEADS, M_DV)),
        "w_proj_a": nrm((L, A_V, D_MODEL), A_V ** -0.5),
        "w_proj_m": nrm((L, M_V, D_MODEL), M_V ** -0.5),
        "gate_b": nrm((L, 2 * D_MODEL), 0.01),
        "w_out": nrm((L, D_MODEL, D_MODEL), D_MODEL ** -0.5),
        "mix_norm_post": gain((L, D_MODEL)),
        "ffn2_norm_pre": gain((L, D_MODEL)),
        "ffn2_w_gu": nrm((L, D_MODEL, 2 * D_FF), D_MODEL ** -0.5),
        "ffn2_w_down": nrm((L, D_FF, D_MODEL), D_FF ** -0.5),
        "ffn2_norm_post": gain((L, D_MODEL)),
    }

def first_block(x, ffn1_norm_pre, ffn1_w_gu, ffn1_w_down, ffn1_norm_post, mix_norm_pre, w_in,
              attn_lam_q1, attn_lam_k1, attn_lam_q2, attn_lam_k2, attn_norm_w, conv_w, conv_b,
              igate_b, fgate_b, mlstm_norm_w, w_proj_a, w_proj_m, gate_b, w_out, mix_norm_post,
              ffn2_norm_pre, ffn2_w_gu, ffn2_w_down, ffn2_norm_post):
    b_, s_, _ = x.shape
    for l in range(DEPTH):
        h = rmsnorm(x, ffn1_norm_pre[l])
        x = x + FFN_SCALE * rmsnorm(swiglu(h, ffn1_w_gu[l], ffn1_w_down[l]), ffn1_norm_post[l])

        h = rmsnorm(x, mix_norm_pre[l])
        z = h @ w_in[l]
        aq, ak, av, mq, mk, mv, mo, mi, mf, gl = jnp.split(z, SPLIT_IDX, axis=-1)

        lam_init = 0.8 - 0.6 * math.exp(-0.3 * l)
        lam = (jnp.exp(jnp.sum(attn_lam_q1[l] * attn_lam_k1[l]))
               - jnp.exp(jnp.sum(attn_lam_q2[l] * attn_lam_k2[l])) + lam_init)
        ya = diff_attention(aq, ak, av, lam, lam_init, attn_norm_w[l])

        mqk = jax.nn.silu(causal_depthwise_conv(jnp.concatenate([mq, mk], axis=-1), conv_w[l], conv_b[l]))
        mq_c, mk_c = jnp.split(mqk, 2, axis=-1)
        hm = mlstm_chunkwise(mq_c.reshape(b_, s_, M_HEADS, M_DQK),
                             mk_c.reshape(b_, s_, M_HEADS, M_DQK),
                             mv.reshape(b_, s_, M_HEADS, M_DV),
                             mi + igate_b[l], mf + fgate_b[l])
        ym = (jax.nn.sigmoid(mo) * rmsnorm(hm, mlstm_norm_w[l]).reshape(b_, s_, M_V))

        g_a, g_m = jnp.split(jax.nn.sigmoid(gl + gate_b[l]), 2, axis=-1)
        merged = g_a * (ya @ w_proj_a[l]) + g_m * (ym @ w_proj_m[l])
        x = x + rmsnorm(merged @ w_out[l], mix_norm_post[l])

        h = rmsnorm(x, ffn2_norm_pre[l])
        x = x + FFN_SCALE * rmsnorm(swiglu(h, ffn2_w_gu[l], ffn2_w_down[l]), ffn2_norm_post[l])
    return x


HEAD_DIM = 64
D_MIX = D_MODEL
GROUP_W = D_MIX // 4
N_HEADS_A = GROUP_W // HEAD_DIM
N_HEADS_B = GROUP_W // HEAD_DIM
N_GROUPS_C = 4
N_GROUPS_D = 4
MOBA_BLOCK = 256
MOBA_TOPK = 3
QBLOCK = 128
ROPE_THETA = 500000.0
ROPE_DIM = HEAD_DIM // 4
SGU_CHUNK = 128
POOL_WINDOWS = (2, 4, 8, 16)
CONV_WIDTH = 3
DN_ALPHA = (2 * DEPTH) ** 0.25
DN_BETA = (8 * DEPTH) ** -0.25
LN_EPS = 1e-5
IN_SIZES = (GROUP_W, GROUP_W, GROUP_W, GROUP_W, GROUP_W, GROUP_W, N_HEADS_B, GROUP_W, GROUP_W, GROUP_W)
IN_SPLITS = tuple(int(s) for s in np.cumsum(IN_SIZES)[:-1])
N_IN = int(sum(IN_SIZES))


def layer_norm(x, g, b):
    xf = x.astype(jnp.float32)
    mu = jnp.mean(xf, axis=-1, keepdims=True)
    var = jnp.mean(jnp.square(xf - mu), axis=-1, keepdims=True)
    return ((xf - mu) * lax.rsqrt(var + LN_EPS) * g.astype(jnp.float32) + b.astype(jnp.float32)).astype(x.dtype)

def to_heads(t, n_heads):
    b, s, _ = t.shape
    return t.reshape(b, s, n_heads, -1).transpose(0, 2, 1, 3)

def from_heads(t):
    b, h, s, d = t.shape
    return t.transpose(0, 2, 1, 3).reshape(b, s, h * d)

def rotary_tables(seq_len):
    pos = jnp.arange(seq_len, dtype=jnp.float32)
    inv_freq = ROPE_THETA ** (-jnp.arange(0, ROPE_DIM, 2, dtype=jnp.float32) / ROPE_DIM)
    ang = pos[:, None] * inv_freq[None, :]
    return jnp.cos(ang), jnp.sin(ang)

def partial_rotary(x, cos, sin):
    half = ROPE_DIM // 2
    cos = cos.astype(x.dtype)
    sin = sin.astype(x.dtype)
    x1 = x[..., :half]
    x2 = x[..., half:ROPE_DIM]
    return jnp.concatenate([x1 * cos - x2 * sin, x1 * sin + x2 * cos, x[..., ROPE_DIM:]], axis=-1)

def moba_attention(q, k, v):
    bsz, h, s, hd = q.shape
    s_pad = -(-s // MOBA_BLOCK) * MOBA_BLOCK
    pad = ((0, 0), (0, 0), (0, s_pad - s), (0, 0))
    q, k, v = jnp.pad(q, pad), jnp.pad(k, pad), jnp.pad(v, pad)
    nb = s_pad // MOBA_BLOCK
    n_sel = min(MOBA_TOPK, nb)
    scale = hd ** -0.5
    kb = k.reshape(bsz, h, nb, MOBA_BLOCK, hd)
    vb = v.reshape(bsz, h, nb, MOBA_BLOCK, hd)
    kbar = jnp.mean(kb.astype(jnp.float32), axis=3)
    gate = jnp.einsum('bhsd,bhnd->bhsn', q.astype(jnp.float32), kbar)
    q_blk = jnp.arange(s_pad) // MOBA_BLOCK
    fully_past = jnp.arange(nb)[None, :] < q_blk[:, None]
    gate = jnp.where(fully_past, gate, -jnp.inf)
    _, sel = lax.top_k(gate, n_sel)
    bi = jnp.arange(bsz)[:, None, None, None]
    hi = jnp.arange(h)[None, :, None, None]

    def one_chunk(n):
        start = n * QBLOCK
        blk = start // MOBA_BLOCK
        qc = lax.dynamic_slice_in_dim(q, start, QBLOCK, axis=2)
        selc = lax.dynamic_slice_in_dim(sel, start, QBLOCK, axis=2)
        valid = selc < blk
        ks = kb[bi, hi, selc]
        vs = vb[bi, hi, selc]
        s_sel = jnp.einsum('bhqd,bhqnjd->bhqnj', qc, ks).astype(jnp.float32) * scale
        s_sel = jnp.where(valid[..., None], s_sel, -jnp.inf).reshape(bsz, h, QBLOCK, n_sel * MOBA_BLOCK)
        k_own = lax.dynamic_slice_in_dim(k, blk * MOBA_BLOCK, MOBA_BLOCK, axis=2)
        v_own = lax.dynamic_slice_in_dim(v, blk * MOBA_BLOCK, MOBA_BLOCK, axis=2)
        s_own = jnp.einsum('bhqd,bhjd->bhqj', qc, k_own).astype(jnp.float32) * scale
        qpos = start + jnp.arange(QBLOCK)
        kpos = blk * MOBA_BLOCK + jnp.arange(MOBA_BLOCK)
        s_own = jnp.where(kpos[None, :] <= qpos[:, None], s_own, -jnp.inf)
        p = jax.nn.softmax(jnp.concatenate([s_sel, s_own], axis=-1), axis=-1)
        p_sel = p[..., :n_sel * MOBA_BLOCK].reshape(bsz, h, QBLOCK, n_sel, MOBA_BLOCK).astype(v.dtype)
        p_own = p[..., n_sel * MOBA_BLOCK:].astype(v.dtype)
        return (jnp.einsum('bhqnj,bhqnjd->bhqd', p_sel, vs)
                + jnp.einsum('bhqj,bhjd->bhqd', p_own, v_own))

    outs = lax.map(one_chunk, jnp.arange(s_pad // QBLOCK))
    out = outs.transpose(1, 2, 0, 3, 4).reshape(bsz, h, s_pad, hd)
    return out[:, :, :s]

def forgetting_attention(q, k, v, log_f):
    bsz, h, s, hd = q.shape
    scale = hd ** -0.5
    c = jnp.cumsum(log_f, axis=-1)
    kpos = jnp.arange(s)

    def one_block(n):
        start = n * QBLOCK
        qc = lax.dynamic_slice_in_dim(q, start, QBLOCK, axis=2)
        cq = lax.dynamic_slice_in_dim(c, start, QBLOCK, axis=2)
        logits = (jnp.einsum('bhqd,bhkd->bhqk', qc, k).astype(jnp.float32) * scale
                  + cq[..., :, None] - c[..., None, :])
        qpos = start + jnp.arange(QBLOCK)
        logits = jnp.where(kpos[None, :] <= qpos[:, None], logits, -jnp.inf)
        p = jax.nn.softmax(logits, axis=-1).astype(v.dtype)
        return jnp.einsum('bhqk,bhkd->bhqd', p, v)

    outs = lax.map(one_block, jnp.arange(s // QBLOCK))
    return outs.transpose(1, 2, 0, 3, 4).reshape(bsz, h, s, hd)

def causal_spatial_gating(u, v, ln_g, ln_b, w_s, b_s):
    bsz, s, width = v.shape
    g = N_GROUPS_C
    c = width // g
    vn = layer_norm(v.reshape(bsz, s, g, c), ln_g.reshape(g, c), ln_b.reshape(g, c))
    vc = vn.reshape(bsz, s // SGU_CHUNK, SGU_CHUNK, g, c)
    causal = jnp.tril(jnp.ones((SGU_CHUNK, SGU_CHUNK), dtype=bool))
    w = jnp.where(causal[None], w_s, jnp.zeros_like(w_s))
    mixed = jnp.einsum('gts,bnsgc->bntgc', w, vc) + b_s.T[None, None, :, :, None]
    return u * mixed.reshape(bsz, s, width)

def multiscale_pool(p, w_g, scale):
    bsz, s, width = p.shape
    g = len(POOL_WINDOWS)
    c = width // g
    pg = p.reshape(bsz, s, g, c).astype(jnp.float32)
    cs = jnp.concatenate([jnp.zeros((bsz, 1, g, c), jnp.float32), jnp.cumsum(pg, axis=1)], axis=1)
    t = jnp.arange(s)
    outs = []
    for gi, win in enumerate(POOL_WINDOWS):
        cs_g = cs[:, :, gi]
        lo = jnp.maximum(t + 1 - win, 0)
        window_sum = cs_g[:, 1:] - cs_g[:, lo]
        count = jnp.minimum(t + 1, win).astype(jnp.float32)
        outs.append(window_sum / count[None, :, None] - pg[:, :, gi])
    pooled = jnp.stack(outs, axis=2).astype(p.dtype)
    mixed = jnp.einsum('bsgc,gcd->bsgd', pooled, w_g)
    return mixed.reshape(bsz, s, width) * scale

def hybrid_mixer(x, w_in, b_forget, sgu_ln_g, sgu_ln_b, sgu_w, sgu_b, pool_w, pool_scale, w_o, cos, sin):
    z = x @ w_in
    aq, ak, av, bq, bk, bv, bf, cu, cv, dp = jnp.split(z, IN_SPLITS, axis=-1)
    ya = moba_attention(partial_rotary(to_heads(aq, N_HEADS_A), cos, sin),
                        partial_rotary(to_heads(ak, N_HEADS_A), cos, sin),
                        to_heads(av, N_HEADS_A))
    log_f = jax.nn.log_sigmoid((bf + b_forget).astype(jnp.float32)).transpose(0, 2, 1)
    yb = forgetting_attention(to_heads(bq, N_HEADS_B), to_heads(bk, N_HEADS_B),
                              to_heads(bv, N_HEADS_B), log_f)
    yc = causal_spatial_gating(jax.nn.gelu(cu, approximate=False), jax.nn.gelu(cv, approximate=False),
                               sgu_ln_g, sgu_ln_b, sgu_w, sgu_b)
    yd = multiscale_pool(dp, pool_w, pool_scale)
    y = jnp.concatenate([from_heads(ya), from_heads(yb), yc, yd], axis=-1)
    return y @ w_o

def conv_gated_ffn(x, w_up, conv_w, conv_b, w_down):
    h = x @ w_up
    h = lax.conv_general_dilated(h, conv_w[:, None, :], window_strides=(1,),
                                 padding=[(CONV_WIDTH - 1, 0)],
                                 dimension_numbers=('NWC', 'WIO', 'NWC'),
                                 feature_group_count=h.shape[-1]) + conv_b
    gate, val = jnp.split(h, 2, axis=-1)
    return (jax.nn.silu(gate) * val) @ w_down

def second_inputs(seed: int = 0) -> dict:
    key = jax.random.key(seed)
    ks = jax.random.split(key, 20)
    L = DEPTH
    nrm = jax.random.normal
    f32 = jnp.float32
    ch = GROUP_W // N_GROUPS_D
    return {
        'x': nrm(ks[0], (BATCH, SEQ, D_MODEL), f32),
        'w_in': nrm(ks[1], (L, D_MODEL, N_IN), f32) * D_MODEL ** -0.5,
        'b_forget': 3.0 + 0.1 * nrm(ks[2], (L, N_HEADS_B), f32),
        'sgu_ln_g': 1.0 + 0.05 * nrm(ks[3], (L, GROUP_W), f32),
        'sgu_ln_b': 0.02 * nrm(ks[4], (L, GROUP_W), f32),
        'sgu_w': nrm(ks[5], (L, N_GROUPS_C, SGU_CHUNK, SGU_CHUNK), f32) * SGU_CHUNK ** -0.5,
        'sgu_b': 1.0 + 0.1 * nrm(ks[6], (L, N_GROUPS_C, SGU_CHUNK), f32),
        'pool_w': nrm(ks[7], (L, N_GROUPS_D, ch, ch), f32) * ch ** -0.5,
        'pool_scale': 1.0 + 0.1 * nrm(ks[8], (L, GROUP_W), f32),
        'w_o': nrm(ks[9], (L, D_MIX, D_MODEL), f32) * D_MIX ** -0.5 * DN_BETA,
        'ln1_g': 1.0 + 0.05 * nrm(ks[10], (L, D_MODEL), f32),
        'ln1_b': 0.02 * nrm(ks[11], (L, D_MODEL), f32),
        'w_up': nrm(ks[12], (L, D_MODEL, 2 * D_FF), f32) * D_MODEL ** -0.5,
        'conv_w': nrm(ks[13], (L, CONV_WIDTH, 2 * D_FF), f32) * CONV_WIDTH ** -0.5,
        'conv_b': 0.02 * nrm(ks[14], (L, 2 * D_FF), f32),
        'w_down': nrm(ks[15], (L, D_FF, D_MODEL), f32) * D_FF ** -0.5 * DN_BETA,
        'ln2_g': 1.0 + 0.05 * nrm(ks[16], (L, D_MODEL), f32),
        'ln2_b': 0.02 * nrm(ks[17], (L, D_MODEL), f32),
    }

def second_block(x, w_in, b_forget, sgu_ln_g, sgu_ln_b, sgu_w, sgu_b, pool_w, pool_scale, w_o,
              ln1_g, ln1_b, w_up, conv_w, conv_b, w_down, ln2_g, ln2_b):
    cos, sin = rotary_tables(x.shape[1])
    for l in range(DEPTH):
        y = hybrid_mixer(x, w_in[l], b_forget[l], sgu_ln_g[l], sgu_ln_b[l], sgu_w[l], sgu_b[l],
                         pool_w[l], pool_scale[l], w_o[l], cos, sin)
        x = layer_norm(DN_ALPHA * x + y, ln1_g[l], ln1_b[l])
        y = conv_gated_ffn(x, w_up[l], conv_w[l], conv_b[l], w_down[l])
        x = layer_norm(DN_ALPHA * x + y, ln2_g[l], ln2_b[l])
    return x


def setup_inputs(seed=0):
    out = dict(first_inputs(seed))
    for name, value in second_inputs(seed + 1).items():
        if name != "x":
            out[name + "_2"] = value
    return out


def reference(
    x, ffn1_norm_pre, ffn1_w_gu, ffn1_w_down, ffn1_norm_post, mix_norm_pre, w_in, attn_lam_q1,
    attn_lam_k1, attn_lam_q2, attn_lam_k2, attn_norm_w, conv_w, conv_b, igate_b, fgate_b,
    mlstm_norm_w, w_proj_a, w_proj_m, gate_b, w_out, mix_norm_post, ffn2_norm_pre, ffn2_w_gu,
    ffn2_w_down, ffn2_norm_post, w_in_2, b_forget_2, sgu_ln_g_2, sgu_ln_b_2, sgu_w_2, sgu_b_2,
    pool_w_2, pool_scale_2, w_o_2, ln1_g_2, ln1_b_2, w_up_2, conv_w_2, conv_b_2, w_down_2,
    ln2_g_2, ln2_b_2,
):
    x = first_block(
        x, ffn1_norm_pre, ffn1_w_gu, ffn1_w_down, ffn1_norm_post, mix_norm_pre, w_in,
        attn_lam_q1, attn_lam_k1, attn_lam_q2, attn_lam_k2, attn_norm_w, conv_w, conv_b,
        igate_b, fgate_b, mlstm_norm_w, w_proj_a, w_proj_m, gate_b, w_out, mix_norm_post,
        ffn2_norm_pre, ffn2_w_gu, ffn2_w_down, ffn2_norm_post,
    )
    return second_block(
        x, w_in_2, b_forget_2, sgu_ln_g_2, sgu_ln_b_2, sgu_w_2, sgu_b_2, pool_w_2, pool_scale_2,
        w_o_2, ln1_g_2, ln1_b_2, w_up_2, conv_w_2, conv_b_2, w_down_2, ln2_g_2, ln2_b_2,
    )


_drawn_inputs = setup_inputs


def setup_inputs(seed=0):
    import zlib

    import numpy as np

    out = dict(_drawn_inputs(seed))
    spreads = {}
    factors = {'attn_lam_q2': 3.079,
     'conv_b': 2.716,
     'igate_b': 64.0,
     'gate_b': 8.0,
     'b_forget_2': 64.0,
     'sgu_ln_g_2': 8.0,
     'sgu_ln_b_2': 28.806,
     'sgu_b_2': 3.456,
     'pool_scale_2': 2.921,
     'conv_b_2': 6.679}
    for name, (base, spread) in spreads.items():
        noise = np.random.default_rng([zlib.crc32(name.encode()), seed]).standard_normal(out[name].shape)
        drawn = base * np.exp(spread * noise) if base else spread * noise
        out[name] = __import__('jax').numpy.asarray(drawn.astype(out[name].dtype))
    for name, factor in factors.items():
        out[name] = (out[name] * factor).astype(out[name].dtype)
    return out
```

```python
import concourse.bass as bass
from concourse import mybir
from contextlib import ExitStack

F32 = mybir.dt.float32
F32R = mybir.dt.float32r
ALU = mybir.AluOpType
ACT = mybir.ActivationFunctionType
AX = mybir.AxisListType

P = 128
T = 256
QT = T // P
D = 1024
KT = D // P
FF = 2816
NF = FF // P
DEPTH = 2
EPS = 1e-6
LN_EPS = 1e-5
ALPHA = (2 * DEPTH) ** 0.25
A_SCALE = 64 ** -0.5
HEADS = 8
NEG = -1e30

RING = 4
AHEAD = RING - 1
DOWN_PARTS = -(-NF // KT)
G_UP = 2 * NF // RING
G_DOWN = DOWN_PARTS * KT // RING
G_FFN = G_UP + G_DOWN
G_MIX = 22
G_L1 = 2 * G_FFN + G_MIX
G_MIX2 = 7
G_L2 = G_MIX2 + G_FFN
G_B2 = DEPTH * G_L1

C1 = {}
_at = 0
for _name, _n in (("ffn1_pre", KT), ("ffn1_post", KT), ("mix_pre", KT), ("mix_post", KT), ("ffn2_pre", KT),
                  ("ffn2_post", KT), ("attn_norm", 1), ("one_minus_lam_init", 1), ("lam_init", 1),
                  ("mlstm_norm", HEADS), ("conv_w", 32), ("conv_b", 8), ("gate_b", 16), ("lam", 4),
                  ("igate_b", 1), ("fgate_b", 1), ("w_gates", KT * 64)):
    C1[_name] = _at
    _at += _n
N1 = _at
C2 = {}
_at = 0
for _name, _n in (("ln1_g", KT), ("ln1_b", KT), ("ln2_g", KT), ("ln2_b", KT), ("conv_w", 3 * 2 * NF),
                  ("conv_b", 2 * NF), ("pool_scale", 2), ("b_forget", 1), ("w_forget", KT * 32),
                  ("sgu_w", 4 * P), ("pool_w", 2 * P), ("sgu_g", T), ("sgu_b_ln", T), ("sgu_b", P)):
    C2[_name] = _at
    _at += _n
N2 = _at
CC = {}
_at = 0
for _name, _n in (("ident", P), ("ones_model", P), ("ones_head", P), ("ones", P), ("mask_rows", 3 * P),
                  ("mask_cols", P), ("rot_cos", T), ("rot_sin", T), ("rot_swap", P), ("inv_count", 2 * T)):
    CC[_name] = _at
    _at += _n
NC = _at


def build(nc, x, consts, params1, params2, w_up1, w_down1, w_mix1, w_mix2, w_up2, w_down2, out):
    with ExitStack() as ctx:
        place = [(nc.sbuf_base + 63) // 64 * 64]

        def sb(name, shape, dt=F32, at=None):
            size = 4
            for n in shape[1:]:
                size *= n
            here = place[0] if at is None else at
            if at is None:
                place[0] += (size + 63) // 64 * 64
            return nc.alloc_sbuf_tensor_at(name, shape, dt, offset=here), here + (size + 63) // 64 * 64

        def sem(name):
            return ctx.enter_context(nc.semaphore(name))

        w_raw, _ = sb("w_raw", [P, RING, KT * P])
        w_hi, _ = sb("w_hi", [P, RING, KT * P], F32R)
        w_lo, _ = sb("w_lo", [P, RING, KT * P], F32R)
        xr, _ = sb("x_residual", [P, KT, T])
        y, _ = sb("y", [P, KT, T])
        h32, _ = sb("h32", [P, KT, T])
        h_hi, _ = sb("h_hi", [P, KT, T], F32R)
        h_lo, _ = sb("h_lo", [P, KT, T], F32R)
        cst, _ = sb("constants", [P, NC])
        par, _ = sb("params", [P, max(N1, N2)])
        acc, _ = sb("acc_squares", [P, T])
        y_sqr, _ = sb("y_squares", [P, 2, T])
        rs, _ = sb("rstd", [P, T])
        lnv, _ = sb("ln_variance", [P, T])
        eps1, _ = sb("eps1", [P, 1])
        eps2, _ = sb("eps2", [P, 1])
        wn, _ = sb("attn_norm_scaled", [P, 1])
        lamp, _ = sb("lam_products", [P, 2])
        lame, _ = sb("lam_exp", [P, 2])
        nlam, _ = sb("neg_lam", [P, 2])
        spare, _ = sb("credits", [P, 16])
        region = place[0]
        silu_g, _ = sb("silu_g", [P, 2, T])
        cbuf, _ = sb("conv_tiles", [P, RING, T])
        act32, _ = sb("act32", [P, 2, T])
        act_hi, _ = sb("act_hi", [P, NF, T], F32R)
        act_lo, _ = sb("act_lo", [P, NF, T], F32R)
        end_ffn = place[0]
        place[0] = region
        qk, _ = sb("qk", [P, 2 * HEADS, T])
        yms_hi, _ = sb("ym_hi", [P, KT, T], F32R, at=region)
        yms_lo, _ = sb("ym_lo", [P, KT, T], F32R, at=region + KT * T * 4)
        v_tok, _ = sb("v_tok", [P, HEADS, QT, P])
        shared2 = place[0]
        mv_tok, _ = sb("mv_tok", [P, HEADS, QT, P])
        gl, _ = sb("gates_merge", [P, 16, T])
        ya_hi, _ = sb("ya_hi", [P, KT, T], F32R)
        ya_lo, _ = sb("ya_lo", [P, KT, T], F32R)
        vT, _ = sb("vT", [P, 2, T])
        sm, _ = sb("scores", [P, 2, 3 * P])
        nmx, _ = sb("neg_max", [P, 4])
        den, _ = sb("row_sums", [P, 4])
        rden, _ = sb("row_scales", [P, 4])
        mx, _ = sb("row_max", [P, 4])
        ya32, _ = sb("ya32", [P, T])
        shared_heads = place[0]
        comb, _ = sb("combined", [P, 3 * P])
        aT, _ = sb("attn_T", [P, 3 * P])
        osq, _ = sb("o_squares", [P, T])
        o_rs, _ = sb("o_rstd", [P, T])
        zw, _ = sb("decay", [P, 3 * P])
        mp, _ = sb("mlstm_p", [P, 3 * P])
        mden, _ = sb("mlstm_den", [P, T])
        mrec, _ = sb("mlstm_rec", [P, T])
        hn, _ = sb("mlstm_h", [P, T])
        heads_end = place[0]
        row_i, _ = sb("row_i", [HEADS, T])
        row_abs, _ = sb("row_abs", [HEADS, T])
        row_l1, _ = sb("row_l1", [HEADS, T])
        row_min, _ = sb("row_min", [HEADS, T])
        scan_f, _ = sb("scan_f", [HEADS, 2, P + T])
        scan_m, _ = sb("scan_m", [HEADS, 2, P + T])
        neg_m, _ = sb("row_neg_m", [HEADS, T])
        row_fm, _ = sb("row_fm", [HEADS, T])
        row_e, _ = sb("row_e", [HEADS, T])
        gT, _ = sb("g_tok", [P, QT, HEADS])
        end_mix = place[0]
        place[0] = shared_heads
        gv, _ = sb("gelu_v", [P, 2, T])
        gu, _ = sb("gelu_u", [P, 2 * T])
        c32, _ = sb("c32", [P, 2 * T])
        r8, _ = sb("sgu_rstd", [P, 8])
        m8, _ = sb("sgu_mean", [P, 8])
        v8, _ = sb("sgu_var", [P, 8])
        assert place[0] <= heads_end
        place[0] = shared2
        aT8, _ = sb("attn_T8", [P, 8, 3 * P])
        xc, _ = sb("sgu_centred", [P, 2 * T])
        sqc, _ = sb("sgu_squares", [P, 2 * T])
        vn, _ = sb("sgu_normed", [P, 2 * T])
        pooled, _ = sb("pooled", [P, 2, T])
        end_mix2 = place[0]
        PAD = 16
        pda, _ = sb("pool_a", [P, 2, PAD + T], at=region + 8 * T * 4)
        pdb, _ = sb("pool_b", [P, 2, PAD + T], at=region + 8 * T * 4 + 2176 + 64)
        d32, _ = sb("d32", [P, 2, T], at=region + 8 * T * 4 + 2 * (2176 + 64))
        place[0] = max(end_ffn, end_mix, end_mix2)
        assert place[0] <= nc.sbuf_usable_end, (place[0], nc.sbuf_usable_end)

        ident = cst[:, CC["ident"]:CC["ident"] + P]
        ones_model = cst[:, CC["ones_model"]:CC["ones_model"] + P]
        ones_head = cst[:, CC["ones_head"]:CC["ones_head"] + P]
        ones = cst[:, CC["ones"]:CC["ones"] + P]
        mask_rows = cst[:, CC["mask_rows"]:CC["mask_rows"] + 3 * P]
        mask_cols = cst[:, CC["mask_cols"]:CC["mask_cols"] + P]

        def p1(name, k=0, n=1):
            return par[:, C1[name] + k:C1[name] + k + n]

        def p2(name, k=0, n=1):
            return par[:, C2[name] + k:C2[name] + k + n]

        bank = [ctx.enter_context(nc.psum_tensor(f"stream{i}", [P, 512], F32)) for i in range(4)]
        side = [ctx.enter_context(nc.psum_tensor(f"side{i}", [P, 512], F32)) for i in range(4)]
        stat = side[0][:, 0:T]
        o_tile = [bk[:, 0:T] for bk in bank]
        tr = bank[3]

        raw_full = [sem(f"raw_full{s}") for s in range(RING)]
        hi_ready = sem("hi_ready")
        split_done = sem("split_done")
        unit_done = sem("unit_done")
        consts_in = sem("consts_in")
        x_in = sem("x_in")
        par_in = sem("par_in")
        par_free = sem("par_free")
        init = sem("init")
        x_ready = sem("x_ready")
        sq_ready = sem("sq_ready")
        stat_ready = sem("stat_ready")
        lnv_ready = sem("lnv_ready")
        rstd_ready = sem("rstd_ready")
        h_ready = sem("h_ready")
        hi_act = sem("hi_act")
        h_split = sem("h_split")
        silu_done = sem("silu_done")
        gated = sem("gated")
        act_rounded = sem("act_rounded")
        act_split = sem("act_split")
        y_sq = sem("y_sq")
        acc_ready = sem("acc_ready")
        y_scaled = sem("y_scaled")
        mix_evict = sem("mix_evict")
        conv_step = sem("conv_step")
        conv_done = sem("conv_done")
        vt_ready = sem("vt_ready")
        vt_stored = sem("vt_stored")
        pads_ready = sem("pads_ready")
        gates_raw = sem("gates_raw")
        gate_act = sem("gate_act")
        gate_vec = sem("gate_vec")
        g_turned = sem("g_turned")
        g_tok_ready = sem("g_tok_ready")
        lam_step = sem("lam_step")
        lam_sum = sem("lam_sum")
        lam_exp = sem("lam_exp")
        lam_ready = sem("lam_ready")
        sc_ready = sem("sc_ready")
        sc_masked = sem("sc_masked")
        nmax_ready = sem("nmax_ready")
        p_ready = sem("p_ready")
        comb_step = sem("comb_step")
        comb_ready = sem("comb_ready")
        aT_ready = sem("aT_ready")
        aT_stored = sem("aT_stored")
        o_ready = sem("o_ready")
        osq_ready = sem("osq_ready")
        ostat_ready = sem("ostat_ready")
        oln_ready = sem("oln_ready")
        orstd_ready = sem("orstd_ready")
        o_normed = sem("o_normed")
        side_rounded = sem("side_rounded")
        ya_split = sem("ya_split")
        sig_ready = sem("sig_ready")
        ms_ready = sem("ms_ready")
        mz_ready = sem("mz_ready")
        mw_ready = sem("mw_ready")
        mwm_ready = sem("mwm_ready")
        mp_ready = sem("mp_ready")
        nd_ready = sem("nd_ready")
        dabs_ready = sem("dabs_ready")
        mmax_ready = sem("mmax_ready")
        mrec_ready = sem("mrec_ready")
        hn_ready = sem("hn_ready")
        hsq_ready = sem("hsq_ready")
        hstat_ready = sem("hstat_ready")
        hln_ready = sem("hln_ready")
        hrstd_ready = sem("hrstd_ready")
        ym_step = sem("ym_step")
        ym_ready = sem("ym_ready")
        ym_split = sem("ym_split")
        proj_done = sem("proj_done")
        conv2_base = sem("conv2_base")
        conv2_step = sem("conv2_step")
        conv2_done = sem("conv2_done")
        z_ready = sem("z_ready")
        centred = sem("centred")
        scaled2 = sem("scaled2")
        m2_evict = sem("m2_evict")
        f_raw = sem("f_raw")
        f_act = sem("f_act")
        f_vec = sem("f_vec")
        gv_turned = sem("gv_turned")
        sgu_vec = sem("sgu_vec")
        sgu_sq = sem("sgu_sq")
        sgu_var = sem("sgu_var")
        sgu_ln = sem("sgu_ln")
        sgu_rs = sem("sgu_rs")
        sgu_xn = sem("sgu_xn")
        sgu_w_masked = sem("sgu_w_masked")
        sgu_step = sem("sgu_step")
        vn_ready = sem("vn_ready")
        sgu_mixed = sem("sgu_mixed")
        c_ready = sem("c_ready")
        pool_step = sem("pool_step")
        d_mixed = sem("d_mixed")
        d_ready = sem("d_ready")
        cd_rounded = sem("cd_rounded")
        cd_split = sem("cd_split")
        swapped = sem("swapped")
        rot_step = sem("rot_step")
        rot_done = sem("rot_done")
        s2_ready = sem("s2_ready")
        s2_masked = sem("s2_masked")
        n2_ready = sem("n2_ready")
        e2_ready = sem("e2_ready")
        q2_step = sem("q2_step")
        q2_ready = sem("q2_ready")
        a2_turned = sem("a2_turned")
        a2_stored = sem("a2_stored")
        v2_turned = sem("v2_turned")
        v2_stored = sem("v2_stored")
        o2_ready = sem("o2_ready")
        o2_hi = sem("o2_hi")
        ab_split = sem("ab_split")
        stored = sem("stored")

        block = ctx.enter_context(nc.Block())

        def ahead(g, s):
            return (g, s + AHEAD) if s + AHEAD < RING else (g + 1, s + AHEAD - RING)

        U_Q, U_K, U_V, U_MQK, U_MO, U_MV, U_GL, U_PA, U_PM, U_OUT = 0, 8, 16, 24, 32, 40, 48, 64, 72, 80
        A0 = 17
        M0 = A0 + 3 * HEADS + 1

        V_CV, V_CU, V_DP, V_AQ, V_AK, V_BQ, V_BK, V_AV, V_BV, V_NONE, V_OUT = 0, 2, 4, 6, 8, 10, 12, 14, 16, 18, 20
        S2 = V_BQ

        H0 = 4 * DEPTH * KT
        X0 = KT * (1 + 3 * DEPTH)
        Q0 = 3 * DEPTH * KT
        E0 = 6 * DEPTH
        Y0 = 3 * DEPTH * (KT + 1)
        K_OUT = (4, 5, 6, 7, 0, 1, 2, 3)

        @block.sync
        def _(sp):
            sp.dma_start(cst[:], consts).then_inc(consts_in, 16)
            sp.dma_start(xr[:], x).then_inc(x_in, 16)

            def stream(g0, groups, src):
                with sp.Fori(0, groups) as i:
                    for s in range(RING):
                        sp.wait_ge(split_done, RING * (g0 + i) + s + 1)
                        sp.dma_start(w_raw[:, s], src(RING * i + s)).then_inc(raw_full[s], 16)

            def rows(w, first):
                return lambda u: w[bass.ds(first + u, 1)].rearrange("a p n -> (a p) n")

            def ffn(g0, w_up, w_down, f):
                stream(g0, G_UP, rows(w_up, f * (2 * NF)))
                stream(g0 + G_UP, G_DOWN, rows(w_down, f * (DOWN_PARTS * KT)))

            with sp.Fori(0, DEPTH) as l:
                g = l * G_L1
                ffn(g, w_up1, w_down1, l * 2)
                stream(g + G_FFN, G_MIX, rows(w_mix1, l * (G_MIX * RING)))
                ffn(g + G_FFN + G_MIX, w_up1, w_down1, l * 2 + 1)
            with sp.Fori(0, DEPTH) as l:
                g = l * G_L2 + G_B2
                stream(g, G_MIX2, rows(w_mix2, l * (G_MIX2 * RING)))
                ffn(g + G_MIX2, w_up2, w_down2, l)
            for s in range(AHEAD):
                sp.wait_ge(split_done, RING * (G_B2 + DEPTH * G_L2) + s + 1)
                sp.dma_start(w_raw[:, s], w_up1[s]).then_inc(raw_full[s], 16)
            sp.wait_ge(x_ready, X0 + 2 * DEPTH * KT)
            sp.dma_start(out, xr[:]).then_inc(stored, 16)
            sp.wait_ge(stored, 16)

        @block.scalar
        def _(act):
            def exp_set():
                nc.scalar.preload_act_table_set("natural_log_exp_and_others")

            def hi_split(g, s, first=False):
                act.wait_ge(raw_full[s], 16 * (g + 1))
                if not first:
                    act.wait_ge(unit_done, RING * g + (s - AHEAD))
                nc.scalar.activation(w_hi[:, s], w_raw[:, s], ACT.Copy).then_inc(hi_ready, 1)

            def rstd(e, eps, dst, src):
                act.wait_ge(stat_ready, e + 1)
                nc.scalar.activation(lnv[:], src, ACT.Ln, bias=eps).then_inc(lnv_ready, 1)
                act.wait_ge(lnv_ready, e + 1)
                nc.scalar.activation(dst, lnv[:], ACT.Exp, scale=-0.5).then_inc(rstd_ready, 1)

            def pre_norm(l, i):
                for m in range(KT):
                    act.wait_ge(x_ready, (l * 3 + i) * KT + m + 1)
                    nc.scalar.activation(h32[:, m], xr[:, m], ACT.Square).then_inc(sq_ready, 1)
                rstd(l * 6 + 2 * i, eps1[:], rs[:], stat)
                hb = (l * 4 + (0, 1, 3)[i]) * KT
                nb = (l * 3 + i) * KT
                for m in range(KT):
                    act.wait_ge(h_ready, nb + m + 1)
                    nc.scalar.activation(h_hi[:, m], h32[:, m], ACT.Copy).then_inc(hi_act, 1)

            def y_tile(yb, m, b, w, slot):
                nc.scalar.activation(y[:, bass.ds(m, 1)].rearrange("p a t -> p (a t)"), o_tile[b],
                                     ACT.Identity, scale=w)
                act.wait_ge(acc_ready, yb * (KT + 1) + m)
                nc.scalar.activation(y_sqr[:, slot], o_tile[b], ACT.Square).then_inc(y_sq, 1)

            def ffn(l, w, g0):
                i_sub = 2 * w
                f = l * 2 + w
                pre_norm(l, i_sub)
                nc.scalar.preload_act_table_set("silu_and_others")
                with act.Fori(0, G_UP) as i:
                    g = g0 + i
                    for p in range(2):
                        hi_split(*ahead(g, 2 * p))
                        act.wait_ge(gated, f * NF + i * 2 + p + 1)
                        act.wait_ge(unit_done, g * RING + 2 * p + 1)
                        nc.scalar.activation(silu_g[:, p], o_tile[2 * p], ACT.Silu).then_inc(silu_done, 1)
                        hi_split(*ahead(g, 2 * p + 1))
                exp_set()
                yb = l * 3 + i_sub
                with act.Fori(0, 2) as i:
                    for mm in range(4):
                        for part in range(DOWN_PARTS):
                            q = DOWN_PARTS * mm + part
                            hi_split(*ahead(g0 + G_UP + i * DOWN_PARTS + q // RING, q % RING))
                        act.wait_ge(unit_done, (g0 + G_UP + i * DOWN_PARTS) * RING + DOWN_PARTS * (mm + 1))
                        m = i * 4 + mm
                        y_tile(yb, m, mm, par[:, bass.ds(m + C1[f"ffn{w + 1}_post"], 1)], mm % 2)
                rstd(l * 6 + 2 * i_sub + 1, eps1[:], rs[:], stat)

            def mixer(l, g0):
                pre_norm(l, 1)
                n64 = l * 64
                act.wait_ge(lam_sum, l + 1)
                nc.scalar.activation(lame[:], side[1][:, 0:2], ACT.Exp).then_inc(lam_exp, 1)

                def attn_exp(h):
                    act.wait_ge(nmax_ready, l * HEADS + h + 1)
                    for k, (m, qt) in enumerate(((0, 0), (0, 1), (1, 0), (1, 1))):
                        s = sm[:, m, 0:P] if qt == 0 else sm[:, m, P:3 * P]
                        i = nc.scalar.activation(s, s, ACT.Exp, bias=nmx[:, 2 * m + qt:2 * m + qt + 1],
                                                 scale=A_SCALE, accum_out=den[:, 2 * m + qt:2 * m + qt + 1])
                    i.then_inc(p_ready, 1)

                def attn_square(h):
                    act.wait_ge(o_ready, l * HEADS + h + 1)
                    nc.scalar.activation(osq[:], side[3][:, 0:T], ACT.Square).then_inc(osq_ready, 1)

                def attn_rstd(h):
                    act.wait_ge(ostat_ready, l * HEADS + h + 1)
                    nc.scalar.activation(lnv[:], side[2][:, 0:T], ACT.Ln, bias=eps1[:]).then_inc(oln_ready, 1)
                    act.wait_ge(oln_ready, l * HEADS + h + 1)
                    if h > 0:
                        act.wait_ge(o_normed, l * HEADS + h)
                    nc.scalar.activation(o_rs[:], lnv[:], ACT.Exp, scale=-0.5).then_inc(orstd_ready, 1)

                def gates():
                    act.wait_ge(gates_raw, l + 1)
                    nc.scalar.activation(row_i[:], side[2][0:HEADS, 0:T], ACT.Identity,
                                         bias=p1("igate_b")[0:HEADS]).then_inc(gate_act, 1)
                    nc.scalar.activation(row_abs[:], side[2][32:32 + HEADS, 0:T], ACT.Abs,
                                         bias=p1("fgate_b")[32:32 + HEADS]).then_inc(gate_act, 1)
                    act.wait_ge(gate_act, l * 5 + 2)
                    nc.scalar.activation(row_abs[:], row_abs[:], ACT.Exp, scale=-1.0).then_inc(gate_act, 1)
                    act.wait_ge(gate_act, l * 5 + 3)
                    nc.scalar.activation(row_l1[:], row_abs[:], ACT.Ln, bias=1.0).then_inc(gate_act, 1)

                def gate_e():
                    act.wait_ge(gate_vec, l * 22 + 21)
                    nc.scalar.activation(row_e[:], row_fm[:], ACT.Exp, scale=-1.0).then_inc(gate_act, 1)

                def mlstm_exp(h):
                    act.wait_ge(mz_ready, l * HEADS + h + 1)
                    nc.scalar.activation(zw[:], zw[:], ACT.Exp).then_inc(mw_ready, 1)

                def mlstm_abs(h):
                    act.wait_ge(nd_ready, l * HEADS + h + 1)
                    if h > 0:
                        act.wait_ge(mrec_ready, l * HEADS + h)
                    nc.scalar.activation(mden[:], side[3][:, 0:T], ACT.Abs).then_inc(dabs_ready, 1)

                def mlstm_square(h):
                    act.wait_ge(hn_ready, l * HEADS + h + 1)
                    nc.scalar.activation(osq[:], hn[:], ACT.Square).then_inc(hsq_ready, 1)

                def mlstm_rstd(h):
                    act.wait_ge(hstat_ready, l * HEADS + h + 1)
                    nc.scalar.activation(lnv[:], side[3][:, 0:T], ACT.Ln, bias=eps1[:]).then_inc(hln_ready, 1)
                    act.wait_ge(hln_ready, l * HEADS + h + 1)
                    nc.scalar.activation(o_rs[:], lnv[:], ACT.Exp, scale=-0.5).then_inc(hrstd_ready, 1)

                def evict(i):
                    b = o_tile[i % 3]
                    act.wait_ge(unit_done, g0 * RING + i + 1)
                    if i < U_V:
                        r = nc.scalar.activation(qk[:, i], b, ACT.Copy)
                    elif i < U_MQK or U_MV <= i < U_GL:
                        n = i - U_V if i < U_MQK else i - U_MV + 8
                        act.wait_ge(vt_ready, l * 16 + n + 1)
                        r = nc.scalar.activation(vT[:, n % 2], b, ACT.Copy)
                    elif i < U_MO:
                        n = i - U_MQK
                        r = nc.scalar.activation(y[:, n], b, ACT.Identity, scale=p1("conv_w", 3 * 8 + n),
                                                 bias=p1("conv_b", n))
                    elif i < U_MV:
                        r = nc.scalar.activation(h32[:, i - U_MO], b, ACT.Copy)
                    else:
                        r = nc.scalar.activation(gl[:, i - U_GL], b, ACT.Identity,
                                                 bias=p1("gate_b", i - U_GL))
                    r.then_inc(mix_evict, 1)

                for i in range(G_MIX * RING):
                    hi_split(*ahead(g0 + i // RING, i % RING))
                    if i == 2:
                        gates()
                    if i == 6:
                        gate_e()
                    k, h = (i - A0) % 3, (i - A0) // 3
                    if i >= A0:
                        if k == 0 and h < HEADS:
                            attn_exp(h)
                        if k == 1 and 1 <= h <= HEADS:
                            attn_square(h - 1)
                        if k == 2 and 1 <= h <= HEADS:
                            attn_rstd(h - 1)
                    k, h = (i - M0) % 3, (i - M0) // 3
                    if i >= M0:
                        if k == 0 and h < HEADS:
                            mlstm_exp(h)
                        if k == 2 and h < HEADS:
                            mlstm_abs(h)
                        if k == 0 and 1 <= h <= HEADS:
                            mlstm_square(h - 1)
                        if k == 1 and 1 <= h <= HEADS:
                            mlstm_rstd(h - 1)
                    if i < U_PA:
                        evict(i)
                    if i == U_MO + 1:
                        act.wait_ge(conv_done, l * 16 + 16)
                        nc.scalar.activation(y[:], y[:], ACT.Silu).then_inc(sig_ready, 1)
                        exp_set()
                    if i == U_MV:
                        act.wait_ge(mix_evict, n64 + U_MV)
                        nc.scalar.activation(h32[:], h32[:], ACT.Sigmoid).then_inc(sig_ready, 1)
                        exp_set()
                    if i == U_GL + 15:
                        act.wait_ge(mix_evict, n64 + 64)
                        nc.scalar.activation(gl[:], gl[:], ACT.Sigmoid).then_inc(sig_ready, 1)
                        exp_set()
                    if U_PM <= i < U_OUT:
                        m = i - U_PM
                        act.wait_ge(proj_done, l * 24 + 8 + 2 * (m + 1))
                        nc.scalar.activation(h_hi[:, m], gl[:, m], ACT.Copy).then_inc(hi_act, 1)
                    if i >= U_OUT:
                        act.wait_ge(unit_done, g0 * RING + i + 1)
                        m = i - U_OUT
                        y_tile(l * 3 + 1, m, i % 3, p1("mix_post", m), m % 2)
                rstd(l * 6 + 3, eps1[:], rs[:], stat)

            def layer_norm(l, i, g, b):
                e = l * 2 + i
                for m in range(KT):
                    act.wait_ge(centred, e * KT + m + 1)
                    nc.scalar.activation(h32[:, m], y[:, m], ACT.Square).then_inc(sq_ready, 1)
                act.wait_ge(stat_ready, E0 + 2 + 2 * e)
                nc.scalar.activation(lnv[:], side[1][:, 0:T], ACT.Ln, bias=eps2[:]).then_inc(lnv_ready, 1)
                act.wait_ge(lnv_ready, E0 + 1 + e)
                nc.scalar.activation(rs[:], lnv[:], ACT.Exp, scale=-0.5).then_inc(rstd_ready, 1)
                for m in range(KT):
                    act.wait_ge(scaled2, e * KT + m + 1)
                    nc.scalar.activation(xr[:, m], y[:, m], ACT.Identity, bias=p2(b, m)).then_inc(x_ready, 1)
                    nc.scalar.activation(h_hi[:, m], y[:, m], ACT.Identity, bias=p2(b, m)).then_inc(hi_act, 1)

            def conv_ffn(l, g0):
                f = l + 4
                nc.scalar.preload_act_table_set("silu_and_others")
                with act.Fori(0, G_UP) as i:
                    g = g0 + i
                    for p in range(2):
                        act.wait_ge(gated, f * NF + i * 2 + p + 1)
                        for half in range(2):
                            s = 2 * p + half
                            hi_split(*ahead(g, s))
                            act.wait_ge(unit_done, g * RING + s + 1)
                            w = par[:, bass.ds(i * 2 + (C2["conv_w"] + 2 * 2 * NF + half * NF + p), 1)]
                            b = par[:, bass.ds(i * 2 + (C2["conv_b"] + half * NF + p), 1)]
                            nc.scalar.activation(cbuf[:, s], o_tile[s], ACT.Identity, scale=w,
                                                 bias=b).then_inc(conv2_base, 1)
                        act.wait_ge(conv2_done, l * (2 * NF) + i * 4 + 2 * p + 5)
                        nc.scalar.activation(silu_g[:, p], cbuf[:, 2 * p], ACT.Silu).then_inc(silu_done, 1)
                exp_set()
                with act.Fori(0, 2) as i:
                    for q in range(4 * DOWN_PARTS):
                        hi_split(*ahead(g0 + G_UP + i * DOWN_PARTS + q // RING, q % RING))
                layer_norm(l, 1, "ln2_g", "ln2_b")

            def mixer2(l, g0):
                n28 = l * 18

                def forget():
                    act.wait_ge(f_raw, l + 1)
                    nc.scalar.activation(row_abs[0:4], side[1][0:4, 0:T], ACT.Abs,
                                         bias=p2("b_forget")[0:4]).then_inc(f_act, 1)

                def forget_ln():
                    act.wait_ge(f_act, l * 3 + 1)
                    nc.scalar.activation(row_abs[0:4], row_abs[0:4], ACT.Exp, scale=-1.0).then_inc(f_act, 1)
                    act.wait_ge(f_act, l * 3 + 2)
                    nc.scalar.activation(row_l1[0:4], row_abs[0:4], ACT.Ln, bias=1.0).then_inc(f_act, 1)

                def sgu_square():
                    act.wait_ge(sgu_vec, l * 3 + 3)
                    nc.scalar.activation(sqc[:], xc[:], ACT.Square).then_inc(sgu_sq, 1)

                def sgu_rstd():
                    act.wait_ge(sgu_var, l + 1)
                    nc.scalar.activation(v8[:], v8[:], ACT.Ln, bias=eps2[:], scale=1.0 / 64).then_inc(sgu_ln, 1)
                    act.wait_ge(sgu_ln, l + 1)
                    nc.scalar.activation(r8[:], v8[:], ACT.Exp, scale=-0.5).then_inc(sgu_rs, 1)

                def attn_exp(h):
                    act.wait_ge(n2_ready, l * 8 + h + 1)
                    b = h % 2
                    for qt in range(2):
                        s = sm[:, b, 0:P] if qt == 0 else sm[:, b, P:3 * P]
                        k = 2 * b + qt
                        i = nc.scalar.activation(s, s, ACT.Exp, bias=nmx[:, k:k + 1], scale=A_SCALE,
                                                 accum_out=den[:, k:k + 1])
                    i.then_inc(e2_ready, 1)

                def pool_scale():
                    act.wait_ge(d_mixed, l + 1)
                    for ct in range(2):
                        r = nc.scalar.activation(d32[:, ct], side[3][:, ct * T:(ct + 1) * T], ACT.Copy,
                                                 scale=p2("pool_scale", ct))
                    r.then_inc(d_ready, 1)

                def value_hi(j):
                    act.wait_ge(o2_ready, l * 4 + j + 1)
                    nc.scalar.activation(ya_hi[:, j], side[3 if j % 2 == 0 else 0][:, 0:T],
                                         ACT.Copy).then_inc(o2_hi, 1)

                def evict(i):
                    b = o_tile[i % 3]
                    act.wait_ge(unit_done, g0 * RING + i + 1)
                    if i < V_CU:
                        r = nc.scalar.activation(gv[:, i], b, ACT.Gelu)
                    elif i < V_DP:
                        r = nc.scalar.activation(gu[:, (i - V_CU) * T:(i - V_CU + 1) * T], b, ACT.Gelu)
                    elif i < V_AQ:
                        r = nc.scalar.activation(pda[:, i - V_DP, PAD:], b, ACT.Copy)
                    elif i < V_AV:
                        r = nc.scalar.activation(qk[:, i - V_AQ], b, ACT.Copy)
                    else:
                        n = i - V_AV
                        if n >= 2:
                            act.wait_ge(v2_turned, l * 4 + n - 1)
                        r = nc.scalar.activation(vT[:, n % 2], b, ACT.Copy)
                    r.then_inc(m2_evict, 1)

                for i in range(G_MIX2 * RING):
                    hi_split(*ahead(g0 + i // RING, i % RING))
                    if i == 1:
                        forget()
                    if i < V_NONE:
                        evict(i)
                    if i == 3:
                        exp_set()
                        sgu_square()
                        forget_ln()
                    if i == 4:
                        sgu_rstd()
                    if S2 <= i < S2 + 8:
                        attn_exp(i - S2)
                    if i == 13:
                        pool_scale()
                    if V_NONE <= i <= V_NONE + 1:
                        value_hi(i - V_NONE)
                    if i == V_OUT:
                        value_hi(2)
                        value_hi(3)
                layer_norm(l, 0, "ln1_g", "ln1_b")

            act.wait_ge(init, 2)
            for s in range(AHEAD):
                hi_split(0, s, first=True)
            with act.Fori(0, DEPTH) as l:
                exp_set()
                act.wait_ge(par_in, l * 16 + 16)
                g = l * G_L1
                ffn(l, 0, g)
                mixer(l, g + G_FFN)
                ffn(l, 1, g + G_FFN + G_MIX)
            for m in range(KT):
                act.wait_ge(x_ready, X0 - KT + m + 1)
                nc.scalar.activation(h_hi[:, m], xr[:, m], ACT.Copy).then_inc(hi_act, 1)
            with act.Fori(0, DEPTH) as l:
                nc.scalar.preload_act_table_set("gelu_and_others")
                act.wait_ge(par_in, l * 16 + 16 * (DEPTH + 1))
                g = l * G_L2 + G_B2
                mixer2(l, g)
                conv_ffn(l, g + G_MIX2)

        @block.vector
        def _(dve):
            def lo_split(g, s):
                dve.wait_ge(hi_ready, g * RING + s + 1)
                nc.vector.tensor_tensor(w_lo[:, s], w_raw[:, s], w_hi[:, s].bitcast(F32),
                                        ALU.subtract).then_inc(split_done, 1)

            def pre_norm(l, i, w):
                dve.wait_ge(rstd_ready, l * 6 + 2 * i + 1)
                hb = (l * 4 + (0, 1, 3)[i]) * KT
                nb = (l * 3 + i) * KT

                def rest(m):
                    dve.wait_ge(hi_act, hb + m + 1)
                    nc.vector.tensor_tensor(h_lo[:, m], h32[:, m], h_hi[:, m].bitcast(F32),
                                            ALU.subtract).then_inc(h_split, 1)

                for m in range(KT):
                    nc.vector.scalar_tensor_tensor(out=h32[:, m], in0=xr[:, m], scalar=p1(w, m), in1=rs[:],
                                                   op0=ALU.mult, op1=ALU.mult).then_inc(h_ready, 1)
                    if m > 0:
                        rest(m - 1)
                rest(KT - 1)

            def clear_acc(yb):
                nc.vector.memset(acc[:], 0.0).then_inc(acc_ready, 1)

            def add_squares(yb, m, slot):
                dve.wait_ge(y_sq, yb * KT + m + 5)
                dve.wait_ge(acc_ready, yb * (KT + 1) + m + 1)
                nc.vector.tensor_tensor(acc[:], acc[:], y_sqr[:, slot], ALU.add).then_inc(acc_ready, 1)

            def post_norm(l, i, scale):
                dve.wait_ge(rstd_ready, l * 6 + 2 * i + 2)
                yb = (l * 3 + i) * KT

                def update(m):
                    dve.wait_ge(y_scaled, yb + m + 1)
                    nc.vector.scalar_tensor_tensor(out=xr[:, m], in0=y[:, m], scalar=scale, in1=xr[:, m],
                                                   op0=ALU.mult, op1=ALU.add).then_inc(x_ready, 1)

                for m in range(KT):
                    nc.vector.tensor_tensor(y[:, m], y[:, m], rs[:], ALU.mult).then_inc(y_scaled, 1)
                    if m > 0:
                        update(m - 1)
                update(KT - 1)

            def ffn(l, w, g0):
                i_sub = 2 * w
                f = l * 2 + w
                pre_norm(l, i_sub, f"ffn{w + 1}_pre")
                with dve.Fori(0, G_UP) as i:
                    g = g0 + i
                    for p in range(2):
                        lo_split(*ahead(g, 2 * p))
                        lo_split(*ahead(g, 2 * p + 1))
                        dve.wait_ge(act_split, f * NF + i * 2 + p + 1)
                        dve.wait_ge(silu_done, f * NF + i * 2 + p + 3)
                        dve.wait_ge(unit_done, g * RING + 2 * p + 2)
                        nc.vector.tensor_tensor(act32[:, p], silu_g[:, p], o_tile[2 * p + 1],
                                                ALU.mult).then_inc(gated, 1)
                yb = l * 3 + i_sub
                clear_acc(yb)
                with dve.Fori(0, 2) as i:
                    for mm in range(4):
                        for part in range(DOWN_PARTS):
                            q = DOWN_PARTS * mm + part
                            lo_split(*ahead(g0 + G_UP + i * DOWN_PARTS + q // RING, q % RING))
                        add_squares(yb, i * 4 + mm, mm % 2)
                post_norm(l, i_sub, 0.5)

            def mixer(l, g0):
                pre_norm(l, 1, "mix_pre")
                n8 = l * HEADS
                nc.vector.tensor_tensor(lamp[:, 0:1], p1("lam", 0), p1("lam", 1), ALU.mult)
                nc.vector.tensor_tensor(lamp[:, 1:2], p1("lam", 2), p1("lam", 3), ALU.mult)
                nc.vector.tensor_tensor(wn[:], p1("attn_norm"), p1("one_minus_lam_init"),
                                        ALU.mult).then_inc(lam_step, 1)
                dve.wait_ge(lam_exp, l + 1)
                nc.vector.scalar_tensor_tensor(out=nlam[:, 0:1], in0=lame[:, 1:2], scalar=lame[:, 0:1],
                                               in1=p1("lam_init"), op0=ALU.subtract,
                                               op1=ALU.subtract).then_inc(lam_ready, 1)

                def gates():
                    n = [l * 22, 0]

                    def link(ins):
                        n[1] += 1
                        ins.then_inc(gate_vec, 1)
                        dve.wait_ge(gate_vec, n[0] + n[1])

                    dve.wait_ge(gate_act, l * 5 + 4)
                    dve.wait_ge(pads_ready, l + 1)
                    link(nc.vector.tensor_scalar(row_min[:], side[2][32:32 + HEADS, 0:T],
                                                 p1("fgate_b")[32:32 + HEADS], 0.0, ALU.add, ALU.min))
                    link(nc.vector.tensor_tensor(scan_f[:, 0, P:], row_min[:], row_l1[:], ALU.subtract))
                    k, at = 1, 0
                    while k < T:
                        link(nc.vector.tensor_tensor(scan_f[:, 1 - at, P:], scan_f[:, at, P:],
                                                     scan_f[:, at, P - k:P + T - k], ALU.add))
                        k, at = 2 * k, 1 - at
                    link(nc.vector.tensor_tensor(scan_m[:, 0, P:], row_i[:], scan_f[:, at, P:], ALU.subtract))
                    link(nc.vector.tensor_copy(row_min[:], scan_m[:, 0, P:]))
                    k, am = 1, 0
                    while k < T:
                        link(nc.vector.tensor_tensor(scan_m[:, 1 - am, P:], scan_m[:, am, P:],
                                                     scan_m[:, am, P - k:P + T - k], ALU.max))
                        k, am = 2 * k, 1 - am
                    nc.vector.tensor_tensor(row_fm[:], scan_m[:, am, P:], scan_f[:, at, P:],
                                            ALU.add).then_inc(gate_vec, 1)
                    nc.vector.tensor_scalar(neg_m[:], scan_m[:, am, P:], -1.0, None, ALU.mult).then_inc(gate_vec, 1)

                def g_tok():
                    dve.wait_ge(g_turned, l + 1)
                    nc.vector.tensor_copy(gT[:], side[3][:, 0:QT * HEADS].rearrange("p (a h) -> p a h", a=QT)) \
                        .then_inc(g_tok_ready, 1)

                def store_v(n):
                    dve.wait_ge(vt_ready, l * 16 + n + 3)
                    dst = (v_tok if n < 8 else mv_tok)[:, n % 8]
                    nc.vector.tensor_copy(dst, tr[:, 0:T].rearrange("p (a d) -> p a d", a=QT)) \
                        .then_inc(vt_stored, 1)

                def conv(i):
                    n = i - U_MQK
                    b = o_tile[i % 3]
                    dve.wait_ge(mix_evict, l * 64 + i + 1)
                    for back in (1, 2, 3):
                        r = nc.vector.scalar_tensor_tensor(
                            out=y[:, n, back:], in0=b[:, 0:T - back], scalar=p1("conv_w", (3 - back) * 8 + n),
                            in1=y[:, n, back:], op0=ALU.mult, op1=ALU.add)
                        if back == 1:
                            r.then_inc(conv_step, 1)
                            dve.wait_ge(conv_step, (l * 8 + n) * 2 + 1)
                        if back == 2:
                            r.then_inc(conv_step, 1)
                            dve.wait_ge(conv_step, (l * 8 + n) * 2 + 2)
                    r.then_inc(conv_done, 2)

                def attn_mask(h):
                    for m in range(2):
                        dve.wait_ge(sc_ready, (n8 + h) * 2 + m + 1)
                        nc.vector.memset(spare[:, 13 + m:14 + m], 0.0)
                        dve.wait_ge(consts_in, 16)
                        for qt, (a, b) in enumerate(((0, P), (P, 3 * P))):
                            r = nc.vector.tensor_tensor_reduce(
                                out=sm[:, m, a:b], in0=side[m][:, a:b], in1=mask_rows[:, a:b], scale=1.0,
                                scalar=-3e38, op0=ALU.add, op1=ALU.max,
                                accum_out=mx[:, 2 * m + qt:2 * m + qt + 1])
                        r.then_inc(sc_masked, 1)
                    dve.wait_ge(sc_masked, (n8 + h) * 2 + 2)
                    nc.vector.tensor_scalar(nmx[:], mx[:], -A_SCALE, None, ALU.mult).then_inc(nmax_ready, 1)

                def attn_combine(h):
                    dve.wait_ge(p_ready, n8 + h + 1)
                    nc.vector.reciprocal(rden[:], den[:]).then_inc(comb_step, 1)
                    dve.wait_ge(comb_step, (n8 + h) * 3 + 1)
                    nc.vector.tensor_scalar(rden[:, 2:4], rden[:, 2:4], nlam[:, 0:1], None,
                                            ALU.mult).then_inc(comb_step, 1)
                    if h > 0:
                        dve.wait_ge(aT_ready, n8 + h)
                    nc.vector.tensor_scalar(comb[:, 0:P], sm[:, 0, 0:P], rden[:, 0:1], None, ALU.mult)
                    nc.vector.tensor_scalar(comb[:, P:], sm[:, 0, P:], rden[:, 1:2], None,
                                            ALU.mult).then_inc(comb_step, 1)
                    dve.wait_ge(comb_step, (n8 + h) * 3 + 3)
                    nc.vector.scalar_tensor_tensor(out=comb[:, 0:P], in0=sm[:, 1, 0:P], scalar=rden[:, 2:3],
                                                   in1=comb[:, 0:P], op0=ALU.mult, op1=ALU.add)
                    nc.vector.scalar_tensor_tensor(out=comb[:, P:], in0=sm[:, 1, P:], scalar=rden[:, 3:4],
                                                   in1=comb[:, P:], op0=ALU.mult,
                                                   op1=ALU.add).then_inc(comb_ready, 1)

                def attn_store(h):
                    dve.wait_ge(aT_ready, n8 + h + 1)
                    if h > 0:
                        dve.wait_ge(o_ready, n8 + h)
                    nc.vector.tensor_copy(aT[:], side[2][:, 0:3 * P]).then_inc(aT_stored, 1)

                def attn_norm(h):
                    dve.wait_ge(orstd_ready, n8 + h + 1)
                    if h > 0:
                        dve.wait_ge(ya_split, n8 + h)
                    nc.vector.scalar_tensor_tensor(out=ya32[:], in0=side[3][:, 0:T], scalar=wn[:], in1=o_rs[:],
                                                   op0=ALU.mult, op1=ALU.mult).then_inc(o_normed, 1)

                def mlstm_z(h):
                    dve.wait_ge(ms_ready, n8 + h + 1)
                    if h > 0:
                        dve.wait_ge(mp_ready, n8 + h)
                    nc.vector.tensor_scalar(zw[:, 0:T], side[1][:, 0:T], gT[:, 0, h:h + 1], 0.0, ALU.add, ALU.min)
                    nc.vector.tensor_scalar(zw[:, T:], side[1][:, P:T], gT[:, 1, h:h + 1], 0.0, ALU.add,
                                            ALU.min).then_inc(mz_ready, 1)

                def mlstm_p(h):
                    dve.wait_ge(mwm_ready, (n8 + h) * 2 + 2)
                    if h > 0:
                        dve.wait_ge(nd_ready, n8 + h)
                    nc.vector.scalar_tensor_tensor(out=mp[:], in0=side[0][:, 0:3 * P], scalar=A_SCALE, in1=zw[:],
                                                   op0=ALU.mult, op1=ALU.mult).then_inc(mp_ready, 1)

                def mlstm_h(h):
                    dve.wait_ge(dabs_ready, n8 + h + 1)
                    nc.vector.tensor_tensor(mden[:], mden[:], side[1][:, T:2 * T], ALU.max).then_inc(mmax_ready, 1)
                    dve.wait_ge(mmax_ready, n8 + h + 1)
                    nc.vector.reciprocal(mrec[:], mden[:]).then_inc(mrec_ready, 1)
                    dve.wait_ge(mrec_ready, n8 + h + 1)
                    nc.vector.tensor_tensor(hn[:], mrec[:], side[2][:, 0:T], ALU.mult).then_inc(hn_ready, 1)

                def mlstm_norm(h):
                    dve.wait_ge(hrstd_ready, n8 + h + 1)
                    nc.vector.scalar_tensor_tensor(out=hn[:], in0=hn[:], scalar=p1("mlstm_norm", h), in1=o_rs[:],
                                                   op0=ALU.mult, op1=ALU.mult).then_inc(ym_step, 1)
                    dve.wait_ge(ym_step, n8 + h + 1)
                    dve.wait_ge(sig_ready, l * 3 + 2)
                    dve.wait_ge(ym_split if h > 0 else ya_split, n8 + (h or HEADS))
                    nc.vector.tensor_tensor(ya32[:], hn[:], h32[:, h], ALU.mult).then_inc(ym_ready, 1)

                def proj(i):
                    b = o_tile[i % 3]
                    if i == U_PA:
                        dve.wait_ge(sig_ready, l * 3 + 3)
                    dve.wait_ge(unit_done, g0 * RING + i + 1)
                    n = i - U_PA
                    nc.vector.tensor_tensor(gl[:, n], gl[:, n], b, ALU.mult).then_inc(proj_done, 1)
                    if i >= U_PM:
                        m = i - U_PM
                        dve.wait_ge(proj_done, l * 24 + 8 + 2 * m + 1)
                        nc.vector.tensor_tensor(gl[:, m], gl[:, m], gl[:, 8 + m], ALU.add).then_inc(proj_done, 1)
                        dve.wait_ge(hi_act, (l * 4 + 2) * KT + m + 1)
                        nc.vector.tensor_tensor(h_lo[:, m], gl[:, m], h_hi[:, m].bitcast(F32),
                                                ALU.subtract).then_inc(h_split, 1)

                for i in range(G_MIX * RING):
                    lo_split(*ahead(g0 + i // RING, i % RING))
                    if i == 2:
                        gates()
                    if i == 6:
                        g_tok()
                    if U_V + 1 < i <= U_MQK + 1:
                        store_v(i - U_V - 2)
                    if U_MV + 1 < i <= U_GL + 1:
                        store_v(i - U_MV - 2 + 8)
                    k, h = (i - A0) % 3, (i - A0) // 3
                    if i >= A0:
                        if k == 0 and h < HEADS:
                            attn_mask(h)
                        if k == 0 and 1 <= h <= HEADS:
                            attn_store(h - 1)
                        if k == 2 and h < HEADS:
                            attn_combine(h)
                        if k == 2 and 1 <= h <= HEADS:
                            attn_norm(h - 1)
                    k, h = (i - M0) % 3, (i - M0) // 3
                    if i >= M0:
                        if k == 0 and h < HEADS:
                            mlstm_z(h)
                        if k == 1 and h < HEADS:
                            mlstm_p(h)
                        if k == 1 and 1 <= h <= HEADS:
                            mlstm_norm(h - 1)
                        if k == 2 and h < HEADS:
                            mlstm_h(h)
                    if U_MQK <= i < U_MO:
                        conv(i)
                    if U_PA <= i < U_OUT:
                        proj(i)
                    if i == U_OUT:
                        clear_acc(l * 3 + 1)
                    if i >= U_OUT:
                        add_squares(l * 3 + 1, i - U_OUT, (i - U_OUT) % 2)
                post_norm(l, 1, 1.0)

            def add_residual(l, i, m, b):
                z = xr[:, bass.ds(m, 1)].rearrange("p a t -> p (a t)")
                nc.vector.scalar_tensor_tensor(out=z, in0=z, scalar=ALPHA, in1=b, op0=ALU.mult,
                                               op1=ALU.add).then_inc(z_ready, 1)
                dve.wait_ge(z_ready, l * (2 * KT) + (i * KT + 5) + m)
                dve.wait_ge(acc_ready, (l * 2 + i) * (KT + 1) + (Y0 + 1) + m)
                nc.vector.tensor_tensor(acc[:], acc[:], z, ALU.add).then_inc(acc_ready, 1)

            def layer_norm(l, i, g):
                e = l * 2 + i
                dve.wait_ge(stat_ready, E0 + 1 + 2 * e)
                for m in range(KT):
                    nc.vector.tensor_tensor(y[:, m], xr[:, m], stat, ALU.subtract).then_inc(centred, 1)
                dve.wait_ge(rstd_ready, E0 + 1 + e)

                def rest(m):
                    dve.wait_ge(hi_act, H0 + KT + e * KT + m + 1)
                    nc.vector.tensor_tensor(h_lo[:, m], xr[:, m], h_hi[:, m].bitcast(F32),
                                            ALU.subtract).then_inc(h_split, 1)

                for m in range(KT):
                    nc.vector.scalar_tensor_tensor(out=y[:, m], in0=y[:, m], scalar=p2(g, m), in1=rs[:],
                                                   op0=ALU.mult, op1=ALU.mult).then_inc(scaled2, 1)
                    if m > 1:
                        rest(m - 2)
                rest(KT - 2)
                rest(KT - 1)

            def conv_ffn(l, g0):
                f = l + 4
                with dve.Fori(0, G_UP) as i:
                    g = g0 + i
                    for p in range(2):
                        for half in range(2):
                            s = 2 * p + half
                            lo_split(*ahead(g, s))
                            n = l * (2 * NF) + i * 4 + s
                            dve.wait_ge(conv2_base, n + 1)
                            for back in (1, 2):
                                w = par[:, bass.ds(i * 2 + (C2["conv_w"] + (2 - back) * 2 * NF + half * NF + p), 1)]
                                r = nc.vector.scalar_tensor_tensor(
                                    out=cbuf[:, s, back:], in0=o_tile[s][:, 0:T - back], scalar=w,
                                    in1=cbuf[:, s, back:], op0=ALU.mult, op1=ALU.add)
                                if back == 1:
                                    r.then_inc(conv2_step, 1)
                                    dve.wait_ge(conv2_step, n + 1)
                            r.then_inc(conv2_done, 1)
                        dve.wait_ge(act_split, f * NF + i * 2 + p + 1)
                        dve.wait_ge(conv2_done, l * (2 * NF) + i * 4 + 2 * p + 6)
                        dve.wait_ge(silu_done, f * NF + i * 2 + p + 3)
                        nc.vector.tensor_tensor(act32[:, p], silu_g[:, p], cbuf[:, 2 * p + 1],
                                                ALU.mult).then_inc(gated, 1)
                nc.vector.memset(acc[:], 0.0).then_inc(acc_ready, 1)
                with dve.Fori(0, 2) as i:
                    for mm in range(4):
                        for part in range(DOWN_PARTS):
                            q = DOWN_PARTS * mm + part
                            lo_split(*ahead(g0 + G_UP + i * DOWN_PARTS + q // RING, q % RING))
                        dve.wait_ge(unit_done, (g0 + G_UP + i * DOWN_PARTS) * RING + DOWN_PARTS * (mm + 1))
                        add_residual(l, 1, i * 4 + mm, o_tile[mm])
                layer_norm(l, 1, "ln2_g")

            def mixer2(l, g0):
                def forget():
                    n = [l * 11, 0]

                    def link(ins):
                        n[1] += 1
                        ins.then_inc(f_vec, 1)
                        dve.wait_ge(f_vec, n[0] + n[1])

                    dve.wait_ge(f_act, l * 3 + 1)
                    nc.vector.tensor_scalar(row_min[0:4], side[1][0:4, 0:T], p2("b_forget")[0:4], 0.0, ALU.add,
                                            ALU.min).then_inc(f_vec, 1)
                    n[1] += 1
                    dve.wait_ge(f_act, l * 3 + 3)
                    dve.wait_ge(f_vec, n[0] + n[1])
                    dve.wait_ge(pads_ready, DEPTH + l + 1)
                    link(nc.vector.tensor_tensor(scan_f[0:4, 0, P:], row_min[0:4], row_l1[0:4], ALU.subtract))
                    k, at = 1, 0
                    while k < T:
                        link(nc.vector.tensor_tensor(scan_f[0:4, 1 - at, P:], scan_f[0:4, at, P:],
                                                     scan_f[0:4, at, P - k:P + T - k], ALU.add))
                        k, at = 2 * k, 1 - at
                    nc.vector.tensor_scalar(neg_m[0:4], scan_f[0:4, at, P:], -1.0 / A_SCALE, None,
                                            ALU.mult).then_inc(f_vec, 1)

                def groups(ap):
                    return ap.rearrange("p (g c) -> p g c", c=64)

                def sgu_centre():
                    dve.wait_ge(gv_turned, l + 1)
                    nc.vector.tensor_reduce(m8[:], groups(side[3][:, 0:2 * T]), AX.X, ALU.add).then_inc(sgu_vec, 1)
                    dve.wait_ge(sgu_vec, l * 3 + 1)
                    nc.vector.tensor_scalar(m8[:], m8[:], 1.0 / 64, None, ALU.mult).then_inc(sgu_vec, 1)
                    dve.wait_ge(sgu_vec, l * 3 + 2)
                    nc.vector.tensor_tensor(groups(xc[:]), groups(side[3][:, 0:2 * T]),
                                            m8[:].unsqueeze(2).to_broadcast([P, 8, 64]),
                                            ALU.subtract).then_inc(sgu_vec, 1)

                def sgu_variance():
                    dve.wait_ge(sgu_sq, l + 1)
                    nc.vector.tensor_reduce(v8[:], groups(sqc[:]), AX.X, ALU.add).then_inc(sgu_var, 1)

                def sgu_scale():
                    dve.wait_ge(sgu_rs, l + 1)
                    nc.vector.tensor_tensor(groups(xc[:]), groups(xc[:]),
                                            r8[:].unsqueeze(2).to_broadcast([P, 8, 64]),
                                            ALU.mult).then_inc(sgu_xn, 1)

                def sgu_gate():
                    dve.wait_ge(sgu_mixed, l + 1)
                    nc.vector.tensor_tensor(c32[:], gu[:], side[3][:, 0:2 * T], ALU.mult).then_inc(c_ready, 1)

                def rotate(n):
                    dve.wait_ge(swapped, l * 4 + n + 1)
                    t = ya32[:]
                    nc.vector.tensor_tensor(t, cst[:, CC["rot_sin"]:CC["rot_sin"] + T], side[2][:, 0:T], ALU.mult)
                    nc.vector.tensor_tensor(qk[:, n], qk[:, n], cst[:, CC["rot_cos"]:CC["rot_cos"] + T],
                                            ALU.mult).then_inc(rot_step, 1)
                    dve.wait_ge(rot_step, l * 4 + n + 1)
                    nc.vector.tensor_tensor(qk[:, n], qk[:, n], t, ALU.add).then_inc(rot_done, 1)

                def attn_mask(h):
                    b = h % 2
                    dve.wait_ge(s2_ready, l * 8 + h + 1)
                    if h >= 2:
                        dve.wait_ge(a2_turned, l * 8 + h - 1)
                    nc.vector.memset(spare[:, 13 + b:14 + b], 0.0)
                    dve.wait_ge(consts_in, 16)
                    for qt, (lo, hi) in enumerate(((0, P), (P, 3 * P))):
                        r = nc.vector.tensor_tensor_reduce(
                            out=sm[:, b, lo:hi], in0=side[b][:, lo:hi], in1=mask_rows[:, lo:hi], scale=1.0,
                            scalar=-3e38, op0=ALU.add, op1=ALU.max,
                            accum_out=mx[:, 2 * b + qt:2 * b + qt + 1])
                    r.then_inc(s2_masked, 1)
                    dve.wait_ge(s2_masked, l * 8 + h + 1)
                    nc.vector.tensor_scalar(nmx[:, 2 * b:2 * b + 2], mx[:, 2 * b:2 * b + 2], -A_SCALE, None,
                                            ALU.mult).then_inc(n2_ready, 1)

                def attn_scale(h):
                    b = h % 2
                    dve.wait_ge(e2_ready, l * 8 + h + 1)
                    nc.vector.reciprocal(rden[:, 2 * b:2 * b + 2], den[:, 2 * b:2 * b + 2]).then_inc(q2_step, 1)
                    dve.wait_ge(q2_step, l * 8 + h + 1)
                    nc.vector.tensor_scalar(sm[:, b, 0:P], sm[:, b, 0:P], rden[:, 2 * b:2 * b + 1], None, ALU.mult)
                    nc.vector.tensor_scalar(sm[:, b, P:], sm[:, b, P:], rden[:, 2 * b + 1:2 * b + 2], None,
                                            ALU.mult).then_inc(q2_ready, 1)

                def attn_store(h):
                    dve.wait_ge(a2_turned, l * 8 + h + 1)
                    nc.vector.tensor_copy(aT8[:, h], side[2][:, 0:3 * P]).then_inc(a2_stored, 1)

                def store_v(n):
                    dve.wait_ge(v2_turned, l * 4 + n + 1)
                    nc.vector.tensor_copy(v_tok[:, n], tr[:, 0:T].rearrange("p (a d) -> p a d", a=QT))                         .then_inc(v2_stored, 1)

                def value_lo(j):
                    dve.wait_ge(o2_hi, l * 4 + j + 1)
                    nc.vector.tensor_tensor(ya_lo[:, j], side[3 if j % 2 == 0 else 0][:, 0:T],
                                            ya_hi[:, j].bitcast(F32), ALU.subtract).then_inc(ab_split, 1)

                for i in range(G_MIX2 * RING):
                    lo_split(*ahead(g0 + i // RING, i % RING))
                    if i == 2:
                        sgu_centre()
                    if i == 4:
                        sgu_variance()
                    if i == 5:
                        forget()
                        sgu_scale()
                    if V_AQ + 1 <= i <= V_AQ + 4:
                        rotate(i - V_AQ - 1)
                    if i == 8:
                        sgu_gate()
                    if S2 <= i < S2 + 8:
                        attn_mask(i - S2)
                    if S2 + 2 <= i < S2 + 10:
                        attn_store(i - S2 - 2)
                    if S2 <= i < S2 + 8:
                        attn_scale(i - S2)
                    if V_AV + 2 <= i < V_AV + 6:
                        store_v(i - V_AV - 2)
                    if V_NONE <= i <= V_NONE + 1:
                        value_lo(i - V_NONE)
                    if i == V_OUT:
                        value_lo(2)
                        value_lo(3)
                        nc.vector.memset(acc[:], 0.0).then_inc(acc_ready, 1)
                    if i >= V_OUT:
                        dve.wait_ge(unit_done, g0 * RING + i + 1)
                        add_residual(l, 0, i - V_OUT, o_tile[i % 3])
                layer_norm(l, 0, "ln1_g")

            nc.vector.memset(eps1[:], EPS).then_inc(init, 1)
            nc.vector.memset(eps2[:], LN_EPS).then_inc(init, 1)
            nc.vector.memset(spare[:, 15:16], 0.0).then_inc(par_free, 1)
            nc.vector.memset(spare[:, 8:9], 0.0).then_inc(y_sq, 4)
            nc.vector.memset(spare[:, 11:12], 0.0).then_inc(z_ready, 4)
            nc.vector.memset(spare[:, 12:13], 0.0).then_inc(conv2_done, 4)
            dve.wait_ge(x_in, 16)
            nc.vector.memset(spare[:, 9:10], 0.0).then_inc(x_ready, KT)
            for s in range(AHEAD):
                lo_split(0, s)
            with dve.Fori(0, DEPTH) as l:
                dve.wait_ge(par_in, l * 16 + 16)
                g = l * G_L1
                ffn(l, 0, g)
                mixer(l, g + G_FFN)
                ffn(l, 1, g + G_FFN + G_MIX)
                nc.vector.memset(spare[:, 10:11], 0.0).then_inc(par_free, 1)
            for m in range(KT):
                dve.wait_ge(hi_act, H0 + m + 1)
                nc.vector.tensor_tensor(h_lo[:, m], xr[:, m], h_hi[:, m].bitcast(F32),
                                        ALU.subtract).then_inc(h_split, 1)
            with dve.Fori(0, DEPTH) as l:
                dve.wait_ge(par_in, l * 16 + 16 * (DEPTH + 1))
                g = l * G_L2 + G_B2
                mixer2(l, g)
                conv_ffn(l, g + G_MIX2)
                dve.wait_ge(x_ready, X0 + (l + 1) * (2 * KT))
                nc.vector.memset(spare[:, 10:11], 0.0).then_inc(par_free, 1)

        @block.gpsimd
        def _(pool):
            credits = ((split_done, RING), (silu_done, 2), (gated, 2), (act_split, 2), (vt_ready, 2), (vt_stored, 1))
            for k, (s, n) in enumerate(credits):
                nc.gpsimd.memset(spare[:, k:k + 1], 0.0).then_inc(s, n)

            def split(src, hi, lo, rounded, n, done):
                nc.gpsimd.tensor_tensor(hi, src, ones_t, ALU.mult).then_inc(rounded, 1)
                pool.wait_ge(rounded, n)
                nc.gpsimd.tensor_tensor(lo, src, hi.bitcast(F32), ALU.subtract).then_inc(done, 1)

            ones_t = ones.unsqueeze(1).to_broadcast([P, 2, P])

            def halves(ap):
                return ap.rearrange("p (a b) -> p a b", a=2)

            def ffn(l, w):
                f = l * 2 + w
                with pool.Fori(0, G_UP) as i:
                    for p in range(2):
                        pool.wait_ge(gated, f * NF + i * 2 + p + 3)
                        j = i * 2 + p
                        hi = act_hi[:, bass.ds(j, 1)].rearrange("p a (b t) -> p (a b) t", b=2)
                        lo = act_lo[:, bass.ds(j, 1)].rearrange("p a (b t) -> p (a b) t", b=2)
                        split(halves(act32[:, p]), hi, lo, act_rounded, f * NF + j + 1, act_split)

            def mixer(l):
                n8 = l * HEADS
                nc.gpsimd.tensor_tensor(scan_f[:, :, 0:P], ones[0:HEADS].unsqueeze(1).to_broadcast([HEADS, 2, P]),
                                        ones[0:HEADS].unsqueeze(1).to_broadcast([HEADS, 2, P]), ALU.subtract)
                nc.gpsimd.memset(scan_m[:, :, 0:P], 0.0).then_inc(pads_ready, 1)
                for h in range(HEADS):
                    pool.wait_ge(o_normed, n8 + h + 1)
                    split(halves(ya32[:]), halves(ya_hi[:, h]), halves(ya_lo[:, h]), side_rounded,
                          n8 * 2 + h + 1, ya_split)
                for h in range(HEADS):
                    pool.wait_ge(mw_ready, n8 + h + 1)
                    nc.gpsimd.tensor_tensor(zw[:, 0:P], zw[:, 0:P], mask_cols, ALU.mult).then_inc(mwm_ready, 1)
                    nc.gpsimd.tensor_tensor(zw[:, T:], zw[:, T:], mask_cols, ALU.mult).then_inc(mwm_ready, 1)
                    if h > 0:
                        ym(n8, h - 1)
                ym(n8, HEADS - 1)

            def ym(n8, h):
                pool.wait_ge(ym_ready, n8 + h + 1)
                split(halves(ya32[:]), halves(yms_hi[:, h]), halves(yms_lo[:, h]), side_rounded,
                      n8 * 2 + HEADS + h + 1, ym_split)

            def conv_ffn(l):
                f = l + 4
                with pool.Fori(0, G_UP) as i:
                    for p in range(2):
                        pool.wait_ge(gated, f * NF + i * 2 + p + 3)
                        j = i * 2 + p
                        hi = act_hi[:, bass.ds(j, 1)].rearrange("p a (b t) -> p (a b) t", b=2)
                        lo = act_lo[:, bass.ds(j, 1)].rearrange("p a (b t) -> p (a b) t", b=2)
                        split(halves(act32[:, p]), hi, lo, act_rounded, f * NF + j + 1, act_split)

            def mixer2(l):
                nc.gpsimd.tensor_tensor(scan_f[0:4, :, 0:P], ones[0:4].unsqueeze(1).to_broadcast([4, 2, P]),
                                        ones[0:4].unsqueeze(1).to_broadcast([4, 2, P]),
                                        ALU.subtract).then_inc(pads_ready, 1)
                nc.gpsimd.memset(pda[:, :, 0:PAD], 0.0)
                nc.gpsimd.memset(pdb[:, :, 0:PAD], 0.0).then_inc(pool_step, 1)
                w = p2("sgu_w", 0, 4 * P).rearrange("p (g t) -> p g t", g=4)
                nc.gpsimd.tensor_tensor(w, w, mask_cols.unsqueeze(1).to_broadcast([P, 4, P]),
                                        ALU.mult).then_inc(sgu_w_masked, 1)
                pool.wait_ge(sgu_xn, l + 1)
                two = xc[:].rearrange("p (a c) -> p a c", a=2)
                out2 = vn[:].rearrange("p (a c) -> p a c", a=2)
                nc.gpsimd.tensor_tensor(two, two, p2("sgu_g", 0, T).unsqueeze(1).to_broadcast([P, 2, T]),
                                        ALU.mult).then_inc(sgu_step, 1)
                pool.wait_ge(sgu_step, l + 1)
                nc.gpsimd.tensor_tensor(out2, two, p2("sgu_b_ln", 0, T).unsqueeze(1).to_broadcast([P, 2, T]),
                                        ALU.add).then_inc(vn_ready, 1)
                n = [l * 10 + 1]

                def link(ins):
                    n[0] = n[0] + 1
                    ins.then_inc(pool_step, 1)
                    pool.wait_ge(pool_step, n[0])

                pool.wait_ge(m2_evict, l * 18 + V_AQ)
                pool.wait_ge(pool_step, l * 10 + 1)

                def doubled(rows, ct, src, dst, back):
                    link(nc.gpsimd.tensor_tensor(dst[rows, ct, PAD:], src[rows, ct, PAD:],
                                                 src[rows, ct, PAD - back:PAD + T - back], ALU.add))

                everything, upper, lower = slice(0, P), slice(64, P), slice(0, 64)
                link(nc.gpsimd.tensor_tensor(pooled[:], pda[:, :, PAD:],
                                             ones[:, 0:1].unsqueeze(1).to_broadcast([P, 2, T]), ALU.mult))
                doubled(everything, 0, pda, pdb, 1)
                doubled(upper, 0, pdb, pda, 2)
                doubled(everything, 1, pda, pdb, 1)
                doubled(everything, 1, pdb, pda, 2)
                doubled(everything, 1, pda, pdb, 4)
                doubled(upper, 1, pdb, pda, 8)
                inv = cst[:, CC["inv_count"]:CC["inv_count"] + 2 * T].rearrange("p (a t) -> p a t", a=2)
                nc.gpsimd.tensor_tensor(pda[upper, :, PAD:], pda[upper, :, PAD:], inv[upper], ALU.mult)
                link(nc.gpsimd.tensor_tensor(pda[lower, :, PAD:], pdb[lower, :, PAD:], inv[lower], ALU.mult))
                link(nc.gpsimd.tensor_tensor(pooled[:], pda[:, :, PAD:], pooled[:], ALU.subtract))
                pool.wait_ge(c_ready, l + 1)
                for ct in range(2):
                    split(halves(c32[:, ct * T:(ct + 1) * T]), halves(ya_hi[:, 4 + ct]), halves(ya_lo[:, 4 + ct]),
                          cd_rounded, l * 4 + ct + 1, cd_split)
                pool.wait_ge(d_ready, l + 1)
                for ct in range(2):
                    split(halves(d32[:, ct]), halves(ya_hi[:, 6 + ct]), halves(ya_lo[:, 6 + ct]),
                          cd_rounded, l * 4 + ct + 3, cd_split)

            pool.wait_ge(consts_in, 16)
            with pool.Fori(0, DEPTH) as l:
                pool.wait_ge(par_free, l + 1)
                pool.dma_start(par[:, 0:N1], params1[bass.ds(l, 1)].rearrange("a p n -> (a p) n")) \
                    .then_inc(par_in, 16)
                ffn(l, 0)
                pool.wait_ge(consts_in, 16)
                pool.wait_ge(unit_done, (l * G_L1 + G_FFN) * RING)
                mixer(l)
                ffn(l, 1)
            with pool.Fori(0, DEPTH) as l:
                pool.wait_ge(par_free, l + DEPTH + 1)
                pool.dma_start(par[:, 0:N2], params2[bass.ds(l, 1)].rearrange("a p n -> (a p) n")) \
                    .then_inc(par_in, 16)
                pool.wait_ge(consts_in, 16)
                pool.wait_ge(unit_done, (l * G_L2 + G_B2) * RING)
                pool.wait_ge(par_in, l * 16 + 16 * (DEPTH + 1))
                mixer2(l)
                conv_ffn(l)

        @block.tensor
        def _(pe):
            def product(dst, s, k, hi, lo, first, last):
                w = slice(k * P, (k + 1) * P)
                nc.tensor.matmul(dst, w_hi[:, s, w], hi, start=first, stop=False)
                nc.tensor.matmul(dst, w_hi[:, s, w], lo, start=False, stop=False)
                return nc.tensor.matmul(dst, w_lo[:, s, w], hi, start=False, stop=last)

            def unit(g, s):
                pe.wait_ge(split_done, g * RING + (s + 1 + RING))

            def model_unit(dst, s, hi, lo, waits=None):
                for k in range(KT):
                    if waits:
                        waits(k)
                    r = product(dst, s, k, hi[:, k], lo[:, k], k == 0, k == KT - 1)
                r.then_inc(unit_done, 1)

            def pre_norm(l, i):
                for m in range(KT):
                    pe.wait_ge(sq_ready, (l * 3 + i) * KT + m + 1)
                    r = nc.tensor.matmul(stat, ones_model, h32[:, m], start=(m == 0), stop=(m == KT - 1))
                r.then_inc(stat_ready, 1)

            def post_norm(yb):
                pe.wait_ge(acc_ready, yb * (KT + 1) + KT + 1)
                nc.tensor.matmul(stat, ones_model, acc[:], start=True, stop=True).then_inc(stat_ready, 1)

            def ffn(l, w, g0):
                i_sub = 2 * w
                f = l * 2 + w
                pre_norm(l, i_sub)
                hb = (l * 4 + 3 * w) * KT
                with pe.Fori(0, G_UP) as i:
                    for s in range(RING):
                        unit(g0 + i, s)
                        pe.wait_ge(gated if s % 2 else silu_done, f * NF + i * 2 + s // 2 + 1)
                        model_unit(o_tile[s], s, h_hi, h_lo,
                                   (lambda k: pe.wait_ge(h_split, hb + k + 1)) if s == 0 else None)
                yb = l * 3 + i_sub
                with pe.Fori(0, 2) as i:
                    for mm in range(4):
                        pe.wait_ge(y_sq, yb * KT + i * 4 + mm + 1)
                        pe.wait_ge(gated if mm % 2 else silu_done, f * NF + NF + 1 + mm // 2)
                        for part in range(DOWN_PARTS):
                            q = DOWN_PARTS * mm + part
                            s = q % RING
                            unit(g0 + G_UP + i * DOWN_PARTS + q // RING, s)
                            ks = range(KT * part, min(KT * (part + 1), NF))
                            pe.wait_ge(act_split, f * NF + ks[-1] + 3)
                            for k in ks:
                                r = product(o_tile[mm], s, k - KT * part, act_hi[:, k], act_lo[:, k], k == 0,
                                            k == NF - 1)
                            r.then_inc(unit_done, 1)
                post_norm(yb)

            def mixer(l, g0):
                pre_norm(l, 1)
                n8 = l * HEADS
                hb = (l * 4 + 1) * KT
                pe.wait_ge(lam_step, l + 1)
                nc.tensor.matmul(side[1][:, 0:2], ones, lamp[:], start=True, stop=True).then_inc(lam_sum, 1)

                def gates():
                    wg = par[:, C1["w_gates"]:C1["w_gates"] + KT * 64].rearrange("p (k n) -> p k n", k=KT)
                    for k in range(KT):
                        r = nc.tensor.matmul(side[2][0:64, 0:T], wg[:, k], h32[:, k], start=(k == 0),
                                             stop=(k == KT - 1))
                    r.then_inc(gates_raw, 1)

                def g_tok():
                    pe.wait_ge(consts_in, 16)
                    pe.wait_ge(gate_vec, l * 22 + 12)
                    for a in range(QT):
                        r = nc.tensor.matmul(side[3][:, a * HEADS:(a + 1) * HEADS], row_min[:, a * P:(a + 1) * P],
                                             ident[0:HEADS, 0:HEADS], start=True, stop=True)
                    r.then_inc(g_turned, 1)

                def turn_v(n):
                    i = U_V + n if n < 8 else U_MV + n - 8
                    pe.wait_ge(mix_evict, l * 64 + i + 1)
                    pe.wait_ge(vt_stored, l * 16 + n + 1)
                    for a in range(QT):
                        r = nc.tensor.transpose(tr[:, a * P:(a + 1) * P], vT[:, n % 2, a * P:(a + 1) * P], ident)
                    r.then_inc(vt_ready, 1)

                def scores(h):
                    if h == 0:
                        pe.wait_ge(mix_evict, l * 64 + 16)
                        pe.wait_ge(lam_exp, l + 1)
                    for m in range(2):
                        if h > 0:
                            pe.wait_ge(sc_masked, (n8 + h) * 2 - 1 + m)
                        r = slice(64 * m, 64 * m + 64)
                        nc.tensor.matmul(side[m][:, 0:P], qk[r, h, 0:P], qk[r, 8 + h, 0:P], start=True, stop=True)
                        nc.tensor.matmul(side[m][:, P:3 * P], qk[r, h, P:T], qk[r, 8 + h, :], start=True,
                                         stop=True).then_inc(sc_ready, 1)

                def turn_a(h):
                    pe.wait_ge(comb_ready, n8 + h + 1)
                    if h > 0:
                        pe.wait_ge(orstd_ready, n8 + h)
                    else:
                        pe.wait_ge(gate_vec, l * 22 + 1)
                    for b in range(3):
                        r = nc.tensor.transpose(side[2][:, b * P:(b + 1) * P], comb[:, blk(b)], ident)
                    r.then_inc(aT_ready, 1)

                def values(h):
                    pe.wait_ge(aT_stored, n8 + h + 1)
                    pe.wait_ge(vt_stored, l * 16 + h + 2)
                    if h == 0:
                        pe.wait_ge(g_tok_ready, l + 1)
                    else:
                        pe.wait_ge(o_normed, n8 + h)
                    nc.tensor.matmul(side[3][:, 0:T], v_tok[:, h, 0], aT[:, 0:T], start=True, stop=False)
                    nc.tensor.matmul(side[3][:, P:T], v_tok[:, h, 1], aT[:, T:], start=False,
                                     stop=True).then_inc(o_ready, 1)

                def head_mean(h):
                    pe.wait_ge(osq_ready, n8 + h + 1)
                    nc.tensor.matmul(side[2][:, 0:T], ones_head, osq[:], start=True,
                                     stop=True).then_inc(ostat_ready, 1)

                def row(h):
                    return ident[0:HEADS, h:h + 1].to_broadcast([HEADS, P])

                def mlstm_scores(h):
                    if h == 0:
                        pe.wait_ge(sig_ready, l * 3 + 1)
                        pe.wait_ge(sc_masked, (n8 + HEADS) * 2)
                        pe.wait_ge(gate_act, l * 5 + 5)
                        pe.wait_ge(gate_vec, l * 22 + 22)
                    else:
                        pe.wait_ge(mp_ready, n8 + h)
                        pe.wait_ge(mmax_ready, n8 + h)
                    r = slice(64 * (h % 2), 64 * (h % 2) + 64)
                    q, k = y[r, h // 2], y[r, 4 + h // 2]
                    nc.tensor.matmul(side[0][:, 0:T], k[:, 0:P], q, start=True, stop=True)
                    nc.tensor.matmul(side[0][:, T:3 * P], k[:, P:T], q[:, P:T], start=True, stop=True)
                    nc.tensor.matmul(side[1][:, 0:T], row(h), neg_m[:], start=True, stop=True)
                    nc.tensor.matmul(side[1][:, T:2 * T], row(h), row_e[:], start=True,
                                     stop=True).then_inc(ms_ready, 1)

                def mlstm_values(h):
                    pe.wait_ge(mp_ready, n8 + h + 1)
                    pe.wait_ge(vt_stored, l * 16 + 8 + h + 2)
                    if h == 0:
                        pe.wait_ge(orstd_ready, n8 + HEADS)
                        pe.wait_ge(o_normed, n8 + HEADS)
                    else:
                        pe.wait_ge(hn_ready, n8 + h)
                        pe.wait_ge(hrstd_ready, n8 + h)
                    nc.tensor.matmul(side[2][:, 0:T], mv_tok[:, h, 0], mp[:, 0:T], start=True, stop=False)
                    nc.tensor.matmul(side[2][:, P:T], mv_tok[:, h, 1], mp[:, T:], start=False, stop=True)
                    nc.tensor.matmul(side[3][:, 0:T], ones, mp[:, 0:T], start=True, stop=False)
                    nc.tensor.matmul(side[3][:, P:T], ones, mp[:, T:], start=False, stop=True).then_inc(nd_ready, 1)

                def mlstm_mean(h):
                    pe.wait_ge(hsq_ready, n8 + h + 1)
                    nc.tensor.matmul(side[3][:, 0:T], ones_head, osq[:], start=True,
                                     stop=True).then_inc(hstat_ready, 1)

                def waits(i):
                    if i < 3:
                        pass
                    elif i - 3 < U_PA:
                        pe.wait_ge(mix_evict, l * 64 + i - 2)
                    elif i - 3 < U_PM:
                        pe.wait_ge(proj_done, l * 24 + i - 3 - U_PA + 1)
                    elif i - 3 < U_OUT:
                        pe.wait_ge(proj_done, l * 24 + 8 + 2 * (i - 3 - U_PM) + 1)
                    else:
                        pe.wait_ge(y_sq, (l * 3 + 1) * KT + 4 + i - 3 - U_OUT + 1)
                    if U_MQK <= i - 3 < U_MO:
                        pe.wait_ge(conv_done, l * 16 + 2 * (i - 3 - U_MQK + 1))

                for i in range(G_MIX * RING):
                    k, h = (i - A0) % 3, (i - A0) // 3
                    if U_V + 1 < i <= U_MQK + 1:
                        turn_v(i - U_V - 2)
                    if U_MV + 1 < i <= U_GL + 1:
                        turn_v(i - U_MV - 2 + 8)
                    if i >= A0:
                        if k == 0 and 1 <= h <= HEADS:
                            turn_a(h - 1)
                        if k == 0 and h < HEADS:
                            scores(h)
                        if k == 1 and 1 <= h <= HEADS:
                            values(h - 1)
                        if k == 2 and 1 <= h <= HEADS:
                            head_mean(h - 1)
                    k, h = (i - M0) % 3, (i - M0) // 3
                    if i >= M0:
                        if k == 0 and h < HEADS:
                            mlstm_scores(h)
                        if k == 1 and 1 <= h <= HEADS:
                            mlstm_mean(h - 1)
                        if k == 2 and h < HEADS:
                            mlstm_values(h)
                    g, s = g0 + i // RING, i % RING
                    unit(g, s)
                    waits(i)
                    if i < U_PA:
                        model_unit(o_tile[i % 3], s, h_hi, h_lo,
                                   (lambda k: pe.wait_ge(h_split, hb + k + 1)) if i == 0 else None)
                    elif i < U_PM:
                        model_unit(o_tile[i % 3], s, ya_hi, ya_lo,
                                   (lambda k: pe.wait_ge(ya_split, n8 + k + 1)) if i == U_PA else None)
                    elif i < U_OUT:
                        model_unit(o_tile[i % 3], s, yms_hi, yms_lo,
                                   (lambda k: pe.wait_ge(ym_split, n8 + k + 1)) if i == U_PM else None)
                    else:
                        model_unit(o_tile[i % 3], s, h_hi, h_lo,
                                   (lambda k: pe.wait_ge(h_split, hb + KT + k + 1)) if i == U_OUT else None)
                    if i == 1:
                        gates()
                    if i == 5:
                        g_tok()
                post_norm(l * 3 + 1)

            def blk(b):
                return slice(b * P, (b + 1) * P)

            def layer_norm(l, i):
                e = l * 2 + i
                pe.wait_ge(acc_ready, e * (KT + 1) + Y0 + KT + 1)
                nc.tensor.matmul(stat, ones_model, acc[:], start=True, stop=True).then_inc(stat_ready, 1)
                for m in range(KT):
                    pe.wait_ge(sq_ready, Q0 + e * KT + m + 1)
                    r = nc.tensor.matmul(side[1][:, 0:T], ones_model, h32[:, m], start=(m == 0), stop=(m == KT - 1))
                r.then_inc(stat_ready, 1)

            def conv_ffn(l, g0):
                f = l + 4
                hb = H0 + (l * 2 + 1) * KT
                with pe.Fori(0, G_UP) as i:
                    for s in range(RING):
                        unit(g0 + i, s)
                        pe.wait_ge(conv2_done, l * (2 * NF) + i * 4 + s + 1)
                        model_unit(o_tile[s], s, h_hi, h_lo,
                                   (lambda k: pe.wait_ge(h_split, hb + k + 1)) if s == 0 else None)
                with pe.Fori(0, 2) as i:
                    for mm in range(4):
                        pe.wait_ge(z_ready, l * (2 * KT) + KT + i * 4 + mm + 1)
                        pe.wait_ge(conv2_done, l * (2 * NF) + 2 * NF + mm + 1)
                        for part in range(DOWN_PARTS):
                            q = DOWN_PARTS * mm + part
                            s = q % RING
                            unit(g0 + G_UP + i * DOWN_PARTS + q // RING, s)
                            ks = range(KT * part, min(KT * (part + 1), NF))
                            pe.wait_ge(act_split, f * NF + ks[-1] + 3)
                            for k in ks:
                                r = product(o_tile[mm], s, k - KT * part, act_hi[:, k], act_lo[:, k], k == 0,
                                            k == NF - 1)
                            r.then_inc(unit_done, 1)
                layer_norm(l, 1)

            def mixer2(l, g0):
                hb = H0 + l * 2 * KT

                def forget():
                    wf = p2("w_forget", 0, KT * 32).rearrange("p (k n) -> p k n", k=KT)
                    for k in range(KT):
                        r = nc.tensor.matmul(side[1][0:32, 0:T], wf[:, k], xr[:, k], start=(k == 0),
                                             stop=(k == KT - 1))
                    r.then_inc(f_raw, 1)

                def turn_gv():
                    pe.wait_ge(m2_evict, l * 18 + 2)
                    pe.wait_ge(consts_in, 16)
                    for a in range(QT):
                        for ct in range(2):
                            r = nc.tensor.transpose(side[3][:, a * T + ct * P:a * T + (ct + 1) * P],
                                                    gv[:, ct, a * P:(a + 1) * P], ident)
                    r.then_inc(gv_turned, 1)

                def spatial():
                    pe.wait_ge(sgu_w_masked, l + 1)
                    pe.wait_ge(vn_ready, l + 1)
                    for g in range(4):
                        rows, ct = slice(64 * (g % 2), 64 * (g % 2) + 64), g // 2
                        for a in range(QT):
                            dst = side[3][rows, ct * T + a * P:ct * T + (a + 1) * P]
                            nc.tensor.matmul(dst, vn[:, a * T + 64 * g:a * T + 64 * g + 64], p2("sgu_w", g * P, P),
                                             start=True, stop=False)
                            r = nc.tensor.matmul(dst, ident[0:4, g:g + 1].to_broadcast([4, 64]),
                                                 p2("sgu_b", 0, P)[0:4], start=False, stop=True)
                    r.then_inc(sgu_mixed, 1)

                def pooling():
                    pe.wait_ge(pool_step, l * 10 + 10)
                    pe.wait_ge(c_ready, l + 1)
                    for ct in range(2):
                        r = nc.tensor.matmul(side[3][:, ct * T:(ct + 1) * T], p2("pool_w", ct * P, P),
                                             pooled[:, ct], start=True, stop=True)
                    r.then_inc(d_mixed, 1)

                def swap(n):
                    pe.wait_ge(m2_evict, l * 18 + V_AQ + n + 1)
                    if n > 0:
                        pe.wait_ge(rot_done, l * 4 + n)
                    nc.tensor.matmul(side[2][:, 0:T], cst[:, CC["rot_swap"]:CC["rot_swap"] + P], qk[:, n],
                                     start=True, stop=True).then_inc(swapped, 1)

                def scores(h):
                    b = side[h % 2]
                    forgets = h >= 4
                    r = slice(64 * (h % 2), 64 * (h % 2) + 64)
                    q, k = (4 if forgets else 0) + (h % 4) // 2, (6 if forgets else 2) + (h % 4) // 2
                    if h == 0:
                        pe.wait_ge(f_vec, l * 11 + 1)
                    if h >= 2:
                        pe.wait_ge(s2_masked, l * 8 + h - 1)
                    if forgets:
                        pe.wait_ge(m2_evict, l * 18 + V_AQ + k + 1)
                        pe.wait_ge(f_vec, l * 11 + 11)
                    else:
                        pe.wait_ge(rot_done, l * 4 + k + 1)
                    for qs, ks, dst in ((slice(0, P), P, b[:, 0:P]), (slice(P, T), T, b[:, P:3 * P])):
                        i = nc.tensor.matmul(dst, qk[r, q, qs], qk[r, k, 0:ks], start=True, stop=not forgets)
                        if forgets:
                            i = nc.tensor.matmul(dst, ident[0:4, h - 4:h - 3].to_broadcast([4, P]),
                                                 neg_m[0:4, 0:ks], start=False, stop=True)
                    i.then_inc(s2_ready, 1)

                def turn_a(h):
                    pe.wait_ge(q2_ready, l * 8 + h + 1)
                    if h > 0:
                        pe.wait_ge(a2_stored, l * 8 + h)
                    else:
                        pe.wait_ge(rot_done, l * 4 + 4)
                    for b in range(3):
                        r = nc.tensor.transpose(side[2][:, blk(b)], sm[:, h % 2, blk(b)], ident)
                    r.then_inc(a2_turned, 1)

                def turn_v(n):
                    pe.wait_ge(m2_evict, l * 18 + V_AV + n + 1)
                    if n > 0:
                        pe.wait_ge(v2_stored, l * 4 + n)
                    for a in range(QT):
                        r = nc.tensor.transpose(tr[:, a * P:(a + 1) * P], vT[:, n % 2, a * P:(a + 1) * P], ident)
                    r.then_inc(v2_turned, 1)

                def values(j):
                    dst = side[3 if j % 2 == 0 else 0]
                    pe.wait_ge(v2_stored, l * 4 + j + 1)
                    pe.wait_ge(a2_stored, l * 8 + 2 * j + 2)
                    if j == 0:
                        pe.wait_ge(d_ready, l + 1)
                    elif j == 1:
                        pe.wait_ge(s2_masked, l * 8 + 8)
                    else:
                        pe.wait_ge(ab_split, l * 4 + j - 1)
                    for h in (2 * j, 2 * j + 1):
                        r = slice(64 * (h % 2), 64 * (h % 2) + 64)
                        nc.tensor.matmul(dst[r, 0:T], v_tok[:, j, 0, r], aT8[:, h, 0:T], start=True, stop=False)
                        i = nc.tensor.matmul(dst[r, P:T], v_tok[:, j, 1, r], aT8[:, h, T:], start=False, stop=True)
                    i.then_inc(o2_ready, 1)

                for i in range(G_MIX2 * RING):
                    if i == 3:
                        turn_gv()
                    if V_AQ + 1 <= i <= V_AQ + 4:
                        swap(i - V_AQ - 1)
                    if i == 8:
                        spatial()
                    if i == 13:
                        pooling()
                    if S2 + 2 <= i < S2 + 10:
                        turn_a(i - S2 - 2)
                    if S2 <= i < S2 + 8:
                        scores(i - S2)
                    if V_AV + 2 <= i < V_AV + 6:
                        turn_v(i - V_AV - 2)
                    if V_NONE <= i <= V_NONE + 1:
                        values(i - V_NONE)
                    if i == V_OUT:
                        values(2)
                        values(3)
                    if V_NONE <= i < V_OUT:
                        continue
                    g, s = g0 + i // RING, i % RING
                    unit(g, s)
                    if i < V_NONE:
                        if i >= 3:
                            pe.wait_ge(m2_evict, l * 18 + i - 2)
                        for k in range(KT):
                            if i == 0:
                                pe.wait_ge(h_split, hb + k + 1)
                            r = product(o_tile[i % 3], s, k, h_hi[:, k], h_lo[:, k], k == 0, k == KT - 1)
                        r.then_inc(unit_done, V_OUT - V_NONE + 1 if i == V_NONE - 1 else 1)
                        if i == 0:
                            forget()
                    else:
                        m = i - V_OUT
                        if m >= 3:
                            pe.wait_ge(z_ready, l * (2 * KT) + 4 + m - 2)
                        else:
                            pe.wait_ge(m2_evict, l * 18 + 18)
                        for n, k in enumerate(K_OUT):
                            if i == V_OUT:
                                pe.wait_ge(cd_split if k >= 4 else ab_split, l * 4 + k % 4 + 1)
                            r = product(o_tile[i % 3], s, k, ya_hi[:, k], ya_lo[:, k], n == 0, n == KT - 1)
                        r.then_inc(unit_done, 1)
                layer_norm(l, 0)

            pe.wait_ge(consts_in, 16)
            with pe.Fori(0, DEPTH) as l:
                pe.wait_ge(par_in, l * 16 + 16)
                g = l * G_L1
                ffn(l, 0, g)
                mixer(l, g + G_FFN)
                ffn(l, 1, g + G_FFN + G_MIX)
            with pe.Fori(0, DEPTH) as l:
                pe.wait_ge(par_in, l * 16 + 16 * (DEPTH + 1))
                g = l * G_L2 + G_B2
                mixer2(l, g)
                conv_ffn(l, g + G_MIX2)


def cols(a):
    import numpy as np
    return np.ascontiguousarray(a.reshape(-1, P).T)


def tiles(w):
    import numpy as np
    k, m = w.shape
    return np.ascontiguousarray(w.reshape(k // P, P, m // P, P).transpose(2, 1, 0, 3)).reshape(m // P, P, k)


def down_units(w):
    import numpy as np
    t = tiles(w).reshape(KT, P, NF, P)
    t = np.concatenate([t, np.zeros((KT, P, DOWN_PARTS * KT - NF, P), t.dtype)], axis=2)
    t = t.reshape(KT, P, DOWN_PARTS, KT * P).transpose(0, 2, 1, 3)
    return np.ascontiguousarray(t).reshape(KT * DOWN_PARTS, P, KT * P)


def constants():
    import numpy as np
    c = np.zeros((P, NC), np.float32)

    def put(name, a):
        c[:, CC[name]:CC[name] + a.shape[1]] = a

    put("ident", np.eye(P, dtype=np.float32))
    put("ones_model", np.full((P, P), 1.0 / D, np.float32))
    put("ones_head", np.full((P, P), 1.0 / P, np.float32))
    put("ones", np.ones((P, P), np.float32))
    tri = np.where(np.arange(P)[None, :] <= np.arange(P)[:, None], 0.0, NEG).astype(np.float32)
    put("mask_rows", np.concatenate([tri, np.zeros((P, P), np.float32), tri], axis=1))
    put("mask_cols", (np.arange(P)[:, None] <= np.arange(P)[None, :]).astype(np.float32))
    inv_freq = np.float32(500000.0) ** (-np.arange(0, 16, 2, dtype=np.float32) / np.float32(16))
    ang = np.arange(T, dtype=np.float32)[None, :] * inv_freq[:, None]
    cos, sin, swap = np.ones((P, T), np.float32), np.zeros((P, T), np.float32), np.zeros((P, P), np.float32)
    for head in (0, 64):
        for d in range(8):
            cos[head + d] = cos[head + 8 + d] = np.cos(ang[d])
            sin[head + d] = sin[head + 8 + d] = np.sin(ang[d])
            swap[head + 8 + d, head + d] = -1.0
            swap[head + d, head + 8 + d] = 1.0
    put("rot_cos", cos)
    put("rot_sin", sin)
    put("rot_swap", swap)
    inv = np.stack([np.repeat(1.0 / np.minimum(np.arange(T) + 1, w)[None, :], 64, axis=0) for w in (2, 4, 8, 16)])
    put("inv_count", inv.reshape(2, P, T).transpose(1, 0, 2).reshape(P, 2 * T).astype(np.float32))
    return c


def pack1(v, l):
    import math
    import numpy as np
    c = np.zeros((P, N1), np.float32)

    def put(name, a):
        c[:a.shape[0], C1[name]:C1[name] + a.shape[1]] = a

    for name, key in (("ffn1_pre", "ffn1_norm_pre"), ("ffn1_post", "ffn1_norm_post"), ("mix_pre", "mix_norm_pre"),
                      ("mix_post", "mix_norm_post"), ("ffn2_pre", "ffn2_norm_pre"),
                      ("ffn2_post", "ffn2_norm_post"), ("attn_norm", "attn_norm_w"),
                      ("mlstm_norm", "mlstm_norm_w"), ("conv_b", "conv_b"), ("gate_b", "gate_b")):
        put(name, cols(v[key][l]))
    lam_init = 0.8 - 0.6 * math.exp(-0.3 * l)
    put("lam_init", np.full((P, 1), lam_init, np.float32))
    put("one_minus_lam_init", np.full((P, 1), 1.0 - lam_init, np.float32))
    put("conv_w", cols(v["conv_w"][l]))
    put("lam", np.stack([v[f"attn_lam_{n}"][l] for n in ("q1", "k1", "q2", "k2")], axis=1))
    c[0:HEADS, C1["igate_b"]] = v["igate_b"][l]
    c[32:32 + HEADS, C1["fgate_b"]] = v["fgate_b"][l]
    at = 6144
    g = v["w_in"][l][:, at:at + 2 * HEADS].reshape(KT, P, 2, HEADS).transpose(1, 0, 2, 3)
    w = np.zeros((P, KT, 2, 32), np.float32)
    w[:, :, :, 0:HEADS] = g
    put("w_gates", w.reshape(P, KT * 64))
    return c


def mix1(v, l):
    import numpy as np
    w = v["w_in"][l]
    q, k, va, mqk, mv, mo, gl = (w[:, a:b] for a, b in ((0, 1024), (1024, 2048), (2048, 3072), (3072, 4096),
                                                        (4096, 5120), (5120, 6144), (6160, 8208)))
    return np.concatenate([tiles(a) for a in (q, k, va, mqk, mo, mv, gl, v["w_proj_a"][l], v["w_proj_m"][l],
                                              v["w_out"][l])])


def up_units(w):
    import numpy as np
    t = tiles(w).reshape(2, NF, P, D)
    return np.ascontiguousarray(t.transpose(1, 0, 2, 3)).reshape(2 * NF, P, D)


def model_in(x):
    import numpy as np
    return np.ascontiguousarray(x.reshape(T, KT, P).transpose(2, 1, 0))


def model_out(a):
    import numpy as np
    return np.ascontiguousarray(a.transpose(2, 1, 0)).reshape(1, T, D)


def pack2(v, l):
    import numpy as np
    c = np.zeros((P, N2), np.float32)

    def put(name, a):
        c[:a.shape[0], C2[name]:C2[name] + a.shape[1]] = a

    for name, key in (("ln1_g", "ln1_g_2"), ("ln1_b", "ln1_b_2"), ("ln2_g", "ln2_g_2"), ("ln2_b", "ln2_b_2"),
                      ("conv_w", "conv_w_2"), ("conv_b", "conv_b_2"), ("pool_scale", "pool_scale_2")):
        put(name, cols(v[key][l]))
    put("b_forget", v["b_forget_2"][l][:, None])
    w = np.zeros((P, KT, 32), np.float32)
    w[:, :, 0:4] = v["w_in_2"][l][:, 1536:1540].reshape(KT, P, 4).transpose(1, 0, 2)
    put("w_forget", w.reshape(P, KT * 32))
    put("sgu_w", v["sgu_w_2"][l].transpose(2, 0, 1).reshape(P, 4 * P))
    w = np.zeros((P, 2, P), np.float32)
    for g in range(4):
        r = slice(64 * (g % 2), 64 * (g % 2) + 64)
        w[r, g // 2, r] = v["pool_w_2"][l][g]
    put("pool_w", w.reshape(P, 2 * P))
    put("sgu_g", np.broadcast_to(v["sgu_ln_g_2"][l], (P, T)))
    put("sgu_b_ln", np.broadcast_to(v["sgu_ln_b_2"][l], (P, T)))
    put("sgu_b", v["sgu_b_2"][l])
    return c


def mix2(v, l):
    import numpy as np
    w = v["w_in_2"][l]
    aq, ak, av, bq, bk, bv, cu, cv, dp = (w[:, a:a + 256] for a in (0, 256, 512, 768, 1024, 1280, 1540, 1796, 2052))
    none = np.zeros((2, P, D), np.float32)
    return np.concatenate([tiles(a) for a in (cv, cu, dp, aq, ak, bq, bk, av, bv)] + [none, tiles(v["w_o_2"][l])])


_INS = ["x", "consts", "params1", "params2", "w_up1", "w_down1", "w_mix1", "w_mix2", "w_up2", "w_down2"]


def layout(v):
    import numpy as np
    ffns = [(v[n + "_w_gu"][l], v[n + "_w_down"][l]) for l in range(DEPTH) for n in ("ffn1", "ffn2")]
    both = range(DEPTH)
    return {
        "x": model_in(v["x"][0]),
        "consts": constants(),
        "params1": np.stack([pack1(v, l) for l in both]),
        "params2": np.stack([pack2(v, l) for l in both]),
        "w_up1": np.concatenate([up_units(a) for a, _ in ffns]),
        "w_down1": np.concatenate([down_units(b) for _, b in ffns]),
        "w_mix1": np.concatenate([mix1(v, l) for l in both]),
        "w_mix2": np.concatenate([mix2(v, l) for l in both]),
        "w_up2": np.concatenate([up_units(v["w_up_2"][l]) for l in both]),
        "w_down2": np.concatenate([down_units(v["w_down_2"][l]) for l in both]),
    }


def kernel(**inputs):
    import numpy as np
    import concourse.bacc as bacc
    from concourse.bass_utils import run_bass_kernel_spmd

    arrays = layout({k: np.asarray(a) for k, a in inputs.items()})
    nc = bacc.Bacc("TRN2", target_bir_lowering=False, num_devices=1)
    args = [nc.dram_tensor("in_" + n, arrays[n].shape, F32, kind="ExternalInput").ap() for n in _INS]
    args.append(nc.dram_tensor("out_x", (P, KT, T), F32, kind="ExternalOutput").ap())
    build(nc, *args)
    r = run_bass_kernel_spmd(nc, [{"in_" + n: arrays[n] for n in _INS}], core_ids=[0])
    return model_out(r.results[0]["out_x"])
```

```python
import concourse.bass as bass
import math
from concourse import mybir
from contextlib import ExitStack

F32 = mybir.dt.float32
F32R = mybir.dt.float32r
ALU = mybir.AluOpType
ACT = mybir.ActivationFunctionType
AX = mybir.AxisListType

P = 128
T = 256
QT = T // P
D = 1024
KT = D // P
FF = 2816
NF = FF // P
DEPTH = 2
EPS = 1e-6
LN_EPS = 1e-5
ALPHA = (2 * DEPTH) ** 0.25
A_SCALE = 64 ** -0.5
HEADS = 8
NEG = -1e30

RING = 4
AHEAD = RING - 1
DOWN_PARTS = -(-NF // KT)
G_UP = 2 * NF // RING
G_DOWN = DOWN_PARTS * KT // RING
G_FFN = G_UP + G_DOWN
G_MIX = 22
G_L1 = 2 * G_FFN + G_MIX
G_MIX2 = 7
G_L2 = G_MIX2 + G_FFN
G_B2 = DEPTH * G_L1

C1 = {}
_at = 0
for _name, _n in (("mix_pre", KT), ("mix_post", KT), ("attn_norm", 1), ("one_minus_lam_init", 1), ("lam_init", 1),
                  ("mlstm_norm", HEADS), ("conv_w", 32), ("conv_b", 8), ("gate_b", 16), ("lam", 4),
                  ("igate_b", 1), ("fgate_b", 1), ("w_gates", KT * 64)):
    C1[_name] = _at
    _at += _n
N1 = _at
C2 = {}
_at = 0
for _name, _n in (("conv_w", 3 * 2 * NF),
                  ("conv_b", 2 * NF), ("pool_scale", 2), ("b_forget", 1), ("w_forget", KT * 32),
                  ("sgu_w", 4 * P), ("pool_w", 2 * P), ("sgu_g", T), ("sgu_b_ln", T), ("sgu_b", P)):
    C2[_name] = _at
    _at += _n
N2 = _at
NPAR = max(N1, N2)
GAINS1 = ("ffn1_pre", "ffn1_post", "ffn2_pre", "ffn2_post")
GAINS2 = ("ln1_g", "ln1_b", "ln2_g", "ln2_b")
G_ONE = DEPTH * len(GAINS1) * KT
G_SECOND = G_ONE + KT
NG = G_SECOND + DEPTH * len(GAINS2) * KT
X_DVE = 5
X_POOL = KT - X_DVE
CC = {}
_at = 0
for _name, _n in (("ones_model", P), ("ones", P), ("ident", P), ("ones_head", P), ("mask_rows", 3 * P),
                  ("mask_cols", P), ("rot_cos", T), ("rot_sin", T), ("rot_swap", P), ("inv_count", 2 * T)):
    CC[_name] = _at
    _at += _n
NC = _at


def build(nc, x, consts, gains, params, w_up1, w_down1, w_mix1, w_mix2, w_up2, w_down2, out):
    with ExitStack() as ctx:
        place = [(nc.sbuf_base + 63) // 64 * 64]

        def sb(name, shape, dt=F32, at=None):
            size = 4
            for n in shape[1:]:
                size *= n
            here = place[0] if at is None else at
            if at is None:
                place[0] += (size + 63) // 64 * 64
            return nc.alloc_sbuf_tensor_at(name, shape, dt, offset=here), here + (size + 63) // 64 * 64

        def sem(name):
            return ctx.enter_context(nc.semaphore(name))

        w_raw, _ = sb("w_raw", [P, RING, KT * P])
        w_hi, _ = sb("w_hi", [P, RING, KT * P], F32R)
        w_lo, _ = sb("w_lo", [P, RING, KT * P], F32R)
        xr, _ = sb("x_residual", [P, KT, T])
        y, _ = sb("y", [P, KT, T])
        h32, _ = sb("h32", [P, KT, T])
        h_hi, _ = sb("h_hi", [P, KT, T], F32R)
        h_lo, _ = sb("h_lo", [P, KT, T], F32R)
        cst, _ = sb("constants", [P, NC])
        gn, _ = sb("gains", [P, NG])
        par, _ = sb("params", [P, NPAR])
        acc, _ = sb("acc_squares", [P, T])
        y_sqr, _ = sb("y_squares", [P, 2, T])
        rs, _ = sb("rstd", [P, T])
        lnv, _ = sb("ln_variance", [P, T])
        eps1, _ = sb("eps1", [P, 1])
        eps2, _ = sb("eps2", [P, 1])
        ln_half, _ = sb("ln_half", [P, 1])
        wn, _ = sb("attn_norm_scaled", [P, 1])
        lamp, _ = sb("lam_products", [P, 2])
        lame, _ = sb("lam_exp", [P, 2])
        nlam, _ = sb("neg_lam", [P, 2])
        spare, _ = sb("credits", [P, 32])
        region = place[0]
        silu_g, _ = sb("silu_g", [P, 2, T])
        cbuf, _ = sb("conv_tiles", [P, RING, T])
        act32, _ = sb("act32", [P, 2, T])
        act_hi, _ = sb("act_hi", [P, NF, T], F32R)
        act_lo, _ = sb("act_lo", [P, NF, T], F32R)
        end_ffn = place[0]
        place[0] = region
        qk, _ = sb("qk", [P, 2 * HEADS, T])
        yms_hi, _ = sb("ym_hi", [P, KT, T], F32R, at=region)
        yms_lo, _ = sb("ym_lo", [P, KT, T], F32R, at=region + KT * T * 4)
        v_tok, _ = sb("v_tok", [P, HEADS, QT, P])
        shared2 = place[0]
        mv_tok, _ = sb("mv_tok", [P, HEADS, QT, P])
        gl, _ = sb("gates_merge", [P, 16, T])
        ya_hi, _ = sb("ya_hi", [P, KT, T], F32R)
        ya_lo, _ = sb("ya_lo", [P, KT, T], F32R)
        vT, _ = sb("vT", [P, 2, T])
        sm, _ = sb("scores", [P, 2, 3 * P])
        nmx, _ = sb("neg_max", [P, 4])
        den, _ = sb("row_sums", [P, 4])
        rden, _ = sb("row_scales", [P, 4])
        mx, _ = sb("row_max", [P, 4])
        ya32, _ = sb("ya32", [P, T])
        shared_heads = place[0]
        comb, _ = sb("combined", [P, 3 * P])
        aT, _ = sb("attn_T", [P, 3 * P])
        osq, _ = sb("o_squares", [P, T])
        o_rs, _ = sb("o_rstd", [P, T])
        zw, _ = sb("decay", [P, 3 * P])
        mp, _ = sb("mlstm_p", [P, 3 * P])
        mden, _ = sb("mlstm_den", [P, T])
        mrec, _ = sb("mlstm_rec", [P, T])
        hn, _ = sb("mlstm_h", [P, T])
        heads_end = place[0]
        row_i, _ = sb("row_i", [HEADS, T])
        row_abs, _ = sb("row_abs", [HEADS, T])
        row_l1, _ = sb("row_l1", [HEADS, T])
        row_min, _ = sb("row_min", [HEADS, T])
        scan_f, _ = sb("scan_f", [HEADS, 2, P + T])
        scan_m, _ = sb("scan_m", [HEADS, 2, P + T])
        neg_m, _ = sb("row_neg_m", [HEADS, T])
        row_fm, _ = sb("row_fm", [HEADS, T])
        row_e, _ = sb("row_e", [HEADS, T])
        gT, _ = sb("g_tok", [P, QT, HEADS])
        end_mix = place[0]
        place[0] = shared_heads
        gv, _ = sb("gelu_v", [P, 2, T])
        gu, _ = sb("gelu_u", [P, 2 * T])
        c32, _ = sb("c32", [P, 2 * T])
        r8, _ = sb("sgu_rstd", [P, 8])
        m8, _ = sb("sgu_mean", [P, 8])
        v8, _ = sb("sgu_var", [P, 8])
        assert place[0] <= heads_end
        place[0] = shared2
        aT8, _ = sb("attn_T8", [P, 8, 3 * P])
        xc, _ = sb("sgu_centred", [P, 2 * T])
        sqc, _ = sb("sgu_squares", [P, 2 * T])
        vn, _ = sb("sgu_normed", [P, 2 * T])
        pooled, _ = sb("pooled", [P, 2, T])
        end_mix2 = place[0]
        PAD = 16
        pda, _ = sb("pool_a", [P, 2, PAD + T], at=region + 8 * T * 4)
        pdb, _ = sb("pool_b", [P, 2, PAD + T], at=region + 8 * T * 4 + 2176 + 64)
        d32, _ = sb("d32", [P, 2, T], at=region + 8 * T * 4 + 2 * (2176 + 64))
        place[0] = max(end_ffn, end_mix, end_mix2)
        assert place[0] <= nc.sbuf_usable_end, (place[0], nc.sbuf_usable_end)

        ident = cst[:, CC["ident"]:CC["ident"] + P]
        ones_model = cst[:, CC["ones_model"]:CC["ones_model"] + P]
        ones_head = cst[:, CC["ones_head"]:CC["ones_head"] + P]
        ones = cst[:, CC["ones"]:CC["ones"] + P]
        mask_rows = cst[:, CC["mask_rows"]:CC["mask_rows"] + 3 * P]
        mask_cols = cst[:, CC["mask_cols"]:CC["mask_cols"] + P]

        def p1(name, k=0, n=1):
            return par[:, C1[name] + k:C1[name] + k + n]

        def p2(name, k=0, n=1):
            return par[:, C2[name] + k:C2[name] + k + n]

        def g1(l, name, m):
            return gn[:, bass.ds(l * (len(GAINS1) * KT) + m + GAINS1.index(name) * KT, 1)]

        def g2(l, name, m):
            return gn[:, bass.ds(l * (len(GAINS2) * KT) + m + (G_SECOND + GAINS2.index(name) * KT), 1)]

        bank = [ctx.enter_context(nc.psum_tensor(f"stream{i}", [P, 512], F32)) for i in range(4)]
        side = [ctx.enter_context(nc.psum_tensor(f"side{i}", [P, 512], F32)) for i in range(4)]
        stat = side[0][:, 0:T]
        o_tile = [bk[:, 0:T] for bk in bank]
        tr = bank[3]

        raw_full = [sem(f"raw_full{s}") for s in range(RING)]
        hi_ready = sem("hi_ready")
        split_done = sem("split_done")
        unit_done = sem("unit_done")
        consts_in = sem("consts_in")
        ones_in = sem("ones_in")
        gains_in = sem("gains_in")
        x_in = [sem(f"x_in{q}") for q in range(4)]
        par_in = sem("par_in")
        par_free = sem("par_free")
        init = sem("init")
        x_ready = sem("x_ready")
        x_pool = sem("x_pool")
        sq_ready = sem("sq_ready")
        stat_ready = sem("stat_ready")
        lnv_ready = sem("lnv_ready")
        rstd_ready = sem("rstd_ready")
        raw_act = sem("raw_act")
        raw_split = sem("raw_split")
        h_ready = sem("h_ready")
        hi_act = sem("hi_act")
        h_split = sem("h_split")
        silu_done = sem("silu_done")
        gate_scaled = sem("gate_scaled")
        up_scaled = sem("up_scaled")
        gated = sem("gated")
        act_rounded = sem("act_rounded")
        act_split = sem("act_split")
        y_sq = sem("y_sq")
        y_taken = sem("y_taken")
        acc_ready = sem("acc_ready")
        y_scaled = sem("y_scaled")
        y_pool = sem("y_pool")
        mix_evict = sem("mix_evict")
        conv_step = sem("conv_step")
        conv_done = sem("conv_done")
        vt_ready = sem("vt_ready")
        vt_stored = sem("vt_stored")
        pads_ready = sem("pads_ready")
        gates_raw = sem("gates_raw")
        gate_act = sem("gate_act")
        gate_vec = sem("gate_vec")
        g_turned = sem("g_turned")
        g_tok_ready = sem("g_tok_ready")
        lam_step = sem("lam_step")
        lam_sum = sem("lam_sum")
        lam_exp = sem("lam_exp")
        lam_ready = sem("lam_ready")
        sc_ready = sem("sc_ready")
        sc_masked = sem("sc_masked")
        nmax_ready = sem("nmax_ready")
        p_ready = sem("p_ready")
        comb_step = sem("comb_step")
        comb_ready = sem("comb_ready")
        aT_ready = sem("aT_ready")
        aT_stored = sem("aT_stored")
        o_ready = sem("o_ready")
        osq_ready = sem("osq_ready")
        ostat_ready = sem("ostat_ready")
        oln_ready = sem("oln_ready")
        orstd_ready = sem("orstd_ready")
        o_normed = sem("o_normed")
        side_rounded = sem("side_rounded")
        ya_split = sem("ya_split")
        sig_ready = sem("sig_ready")
        ms_ready = sem("ms_ready")
        mz_ready = sem("mz_ready")
        mw_ready = sem("mw_ready")
        mwm_ready = sem("mwm_ready")
        mp_ready = sem("mp_ready")
        nd_ready = sem("nd_ready")
        dabs_ready = sem("dabs_ready")
        mmax_ready = sem("mmax_ready")
        mrec_ready = sem("mrec_ready")
        hn_ready = sem("hn_ready")
        hsq_ready = sem("hsq_ready")
        hstat_ready = sem("hstat_ready")
        hln_ready = sem("hln_ready")
        hrstd_ready = sem("hrstd_ready")
        ym_step = sem("ym_step")
        ym_ready = sem("ym_ready")
        ym_split = sem("ym_split")
        proj_done = sem("proj_done")
        conv2_base = sem("conv2_base")
        conv2_step = sem("conv2_step")
        conv2_done = sem("conv2_done")
        z_ready = sem("z_ready")
        centred = sem("centred")
        scaled2 = sem("scaled2")
        m2_evict = sem("m2_evict")
        f_raw = sem("f_raw")
        f_act = sem("f_act")
        f_vec = sem("f_vec")
        gv_turned = sem("gv_turned")
        sgu_vec = sem("sgu_vec")
        sgu_sq = sem("sgu_sq")
        sgu_var = sem("sgu_var")
        sgu_ln = sem("sgu_ln")
        sgu_rs = sem("sgu_rs")
        sgu_xn = sem("sgu_xn")
        sgu_w_masked = sem("sgu_w_masked")
        sgu_step = sem("sgu_step")
        vn_ready = sem("vn_ready")
        sgu_mixed = sem("sgu_mixed")
        c_ready = sem("c_ready")
        pool_step = sem("pool_step")
        d_mixed = sem("d_mixed")
        d_ready = sem("d_ready")
        cd_rounded = sem("cd_rounded")
        cd_split = sem("cd_split")
        swapped = sem("swapped")
        rot_step = sem("rot_step")
        rot_done = sem("rot_done")
        s2_ready = sem("s2_ready")
        s2_masked = sem("s2_masked")
        n2_ready = sem("n2_ready")
        e2_ready = sem("e2_ready")
        q2_step = sem("q2_step")
        q2_ready = sem("q2_ready")
        a2_turned = sem("a2_turned")
        a2_stored = sem("a2_stored")
        v2_turned = sem("v2_turned")
        v2_stored = sem("v2_stored")
        o2_ready = sem("o2_ready")
        o2_hi = sem("o2_hi")
        ab_split = sem("ab_split")
        stored = sem("stored")

        block = ctx.enter_context(nc.Block())

        def ahead(g, s):
            return (g, s + AHEAD) if s + AHEAD < RING else (g + 1, s + AHEAD - RING)

        U_MO, U_MQK, U_MV, U_GL, U_PA, U_PM, U_OUT = 24, 32, 40, 48, 64, 72, 80
        U_RAW = 3
        A0 = 6
        M0 = U_MV + 5

        V_CV, V_CU, V_DP, V_AQ, V_AK, V_BQ, V_BK, V_AV, V_BV, V_NONE, V_OUT = 0, 2, 4, 6, 8, 10, 12, 14, 16, 18, 20
        S2 = V_BQ

        H0 = 4 * DEPTH * KT
        X0 = X_DVE * (1 + 3 * DEPTH)
        Q0 = (3 * DEPTH + 1) * KT
        E0 = 6 * DEPTH
        Y0 = 3 * DEPTH * (KT + 1)
        K_OUT = (4, 5, 6, 7, 0, 1, 2, 3)

        @block.sync
        def _(sp):
            sp.dma_start(gn[:], gains).then_inc(gains_in, 16)
            sp.dma_start(xr[:, 0:2], x[:, 0:2]).then_inc(x_in[0], 16)

            def stream(g0, groups, src):
                with sp.Fori(0, groups) as i:
                    for s in range(RING):
                        sp.wait_ge(split_done, RING * (g0 + i) + s + 1)
                        sp.dma_start(w_raw[:, s], src(RING * i + s)).then_inc(raw_full[s], 16)

            def rows(w, first):
                return lambda u: w[bass.ds(first + u, 1)].rearrange("a p n -> (a p) n")

            def ffn(g0, w_up, w_down, f):
                stream(g0, G_UP, rows(w_up, f * (2 * NF)))
                stream(g0 + G_UP, G_DOWN, rows(w_down, f * (DOWN_PARTS * KT)))

            with sp.Fori(0, DEPTH) as l:
                g = l * G_L1
                ffn(g, w_up1, w_down1, l * 2)
                stream(g + G_FFN, G_MIX, rows(w_mix1, l * (G_MIX * RING)))
                ffn(g + G_FFN + G_MIX, w_up1, w_down1, l * 2 + 1)
            with sp.Fori(0, DEPTH) as l:
                g = l * G_L2 + G_B2
                stream(g, G_MIX2, rows(w_mix2, l * (G_MIX2 * RING)))
                ffn(g + G_MIX2, w_up2, w_down2, l)
            for s in range(AHEAD):
                sp.wait_ge(split_done, RING * (G_B2 + DEPTH * G_L2) + s + 1)
                sp.dma_start(w_raw[:, s], w_up1[s]).then_inc(raw_full[s], 16)
            for q in range(4):
                sp.wait_ge(x_ready, X0 + (2 * DEPTH - 1) * KT + 2 * q + 2)
                sp.dma_start(out[:, 2 * q:2 * q + 2], xr[:, 2 * q:2 * q + 2]).then_inc(stored, 16)
            sp.wait_ge(stored, 4 * 16)

        @block.scalar
        def _(act):
            def exp_set():
                nc.scalar.preload_act_table_set("natural_log_exp_and_others")

            def hi_split(g, s, first=False):
                act.wait_ge(raw_full[s], 16 * (g + 1))
                if not first:
                    act.wait_ge(unit_done, RING * g + (s - AHEAD))
                nc.scalar.activation(w_hi[:, s], w_raw[:, s], ACT.Copy).then_inc(hi_ready, 1)

            def rstd(e, eps, dst, src, ln_scale=None):
                act.wait_ge(stat_ready, e + 1)
                nc.scalar.activation(lnv[:], src, ACT.Ln, bias=eps).then_inc(lnv_ready, 1)
                act.wait_ge(lnv_ready, e + 1)
                nc.scalar.activation(dst, lnv[:], ACT.Exp, scale=-0.5,
                                     bias=ln_scale if ln_scale is not None else 0.0).then_inc(rstd_ready, 1)

            def x_tile(n, m):
                if m < X_DVE:
                    act.wait_ge(x_ready, n * X_DVE + m + 1)
                else:
                    act.wait_ge(x_pool, n * X_POOL + m - X_DVE + 1)

            def raw_operand(l, w, wait_x, between=None):
                for m in range(KT):
                    wait_x(m)
                    nc.scalar.activation(h_hi[:, m], xr[:, m], ACT.Identity,
                                         scale=g1(l, f"ffn{w + 1}_pre", m)).then_inc(hi_act, 1)
                    nc.scalar.activation(h32[:, m], xr[:, m], ACT.Square).then_inc(sq_ready, 1)
                    if between:
                        between(m)

            def pre_norm(l, i, g0):
                for m in range(KT):
                    x_tile(l * 3 + i, m)
                    nc.scalar.activation(ya_hi[:, m], xr[:, m], ACT.Identity,
                                         scale=p1("mix_pre", m)).then_inc(raw_act, 1)
                    nc.scalar.activation(h32[:, m], xr[:, m], ACT.Square).then_inc(sq_ready, 1)
                hi_split(*ahead(g0, 0))
                rstd(l * 6 + 2 * i, eps1[:], rs[:], stat)
                for m in range(KT):
                    act.wait_ge(h_ready, l * KT + m + 1)
                    nc.scalar.activation(h_hi[:, m], h32[:, m], ACT.Copy).then_inc(hi_act, 1)
                    if m == 1:
                        hi_split(*ahead(g0, 1))

            def y_tile(yb, m, b, w, slot):
                act.wait_ge(acc_ready, yb * (KT + 1) + m)
                nc.scalar.activation(y_sqr[:, slot], o_tile[b], ACT.Square).then_inc(y_sq, 1)
                nc.scalar.activation(y[:, bass.ds(m, 1)].rearrange("p a t -> p (a t)"), o_tile[b],
                                     ACT.Identity, scale=w).then_inc(y_taken, 1)

            def ffn(l, w, g0):
                i_sub = 2 * w
                f = l * 2 + w

                def up_group(i, first=False):
                    g = g0 + i
                    for p in range(2):
                        hi_split(*ahead(g, 2 * p))
                        if first and p == 0:
                            rstd(l * 6 + 2 * i_sub, eps1[:], rs[:], stat)
                            nc.scalar.preload_act_table_set("silu_and_others")
                        act.wait_ge(gated, f * NF + i * 2 + p + 1)
                        act.wait_ge(gate_scaled, f * NF + i * 2 + p + 3)
                        nc.scalar.activation(silu_g[:, p], cbuf[:, p], ACT.Silu).then_inc(silu_done, 1)
                        hi_split(*ahead(g, 2 * p + 1))

                up_group(0, first=True)
                with act.Fori(1, G_UP) as i:
                    up_group(i)
                exp_set()
                yb = l * 3 + i_sub
                with act.Fori(0, 2) as i:
                    for mm in range(4):
                        for part in range(DOWN_PARTS):
                            q = DOWN_PARTS * mm + part
                            hi_split(*ahead(g0 + G_UP + i * DOWN_PARTS + q // RING, q % RING))
                        act.wait_ge(unit_done, (g0 + G_UP + i * DOWN_PARTS) * RING + DOWN_PARTS * (mm + 1))
                        m = i * 4 + mm
                        y_tile(yb, m, mm, g1(l, f"ffn{w + 1}_post", m), mm % 2)
                rstd(l * 6 + 2 * i_sub + 1, eps1[:], rs[:], stat, ln_half[:])

            def mixer(l, g0):
                pre_norm(l, 1, g0)
                n64 = l * 64
                def attn_exp(h):
                    act.wait_ge(nmax_ready, l * HEADS + h + 1)
                    for k, (m, qt) in enumerate(((0, 0), (0, 1), (1, 0), (1, 1))):
                        s = sm[:, m, 0:P] if qt == 0 else sm[:, m, P:3 * P]
                        i = nc.scalar.activation(s, s, ACT.Exp, bias=nmx[:, 2 * m + qt:2 * m + qt + 1],
                                                 scale=A_SCALE, accum_out=den[:, 2 * m + qt:2 * m + qt + 1])
                    i.then_inc(p_ready, 1)

                def attn_square(h):
                    act.wait_ge(o_ready, l * HEADS + h + 1)
                    nc.scalar.activation(osq[:], side[3][:, 0:T], ACT.Square).then_inc(osq_ready, 1)

                def attn_rstd(h):
                    act.wait_ge(ostat_ready, l * HEADS + h + 1)
                    nc.scalar.activation(lnv[:], side[3][:, T:2 * T], ACT.Ln, bias=eps1[:]).then_inc(oln_ready, 1)
                    act.wait_ge(oln_ready, l * HEADS + h + 1)
                    if h > 0:
                        act.wait_ge(o_normed, l * HEADS + h)
                    nc.scalar.activation(o_rs[:], lnv[:], ACT.Exp, scale=-0.5).then_inc(orstd_ready, 1)

                def gates():
                    act.wait_ge(gates_raw, l + 1)
                    nc.scalar.activation(row_i[:], side[2][0:HEADS, 0:T], ACT.Identity,
                                         bias=p1("igate_b")[0:HEADS]).then_inc(gate_act, 1)
                    nc.scalar.activation(row_abs[:], side[2][32:32 + HEADS, 0:T], ACT.Abs,
                                         bias=p1("fgate_b")[32:32 + HEADS]).then_inc(gate_act, 1)
                    act.wait_ge(gate_act, l * 5 + 2)
                    nc.scalar.activation(row_abs[:], row_abs[:], ACT.Exp, scale=-1.0).then_inc(gate_act, 1)
                    act.wait_ge(gate_act, l * 5 + 3)
                    nc.scalar.activation(row_l1[:], row_abs[:], ACT.Ln, bias=1.0).then_inc(gate_act, 1)

                def gate_e():
                    act.wait_ge(gate_vec, l * 22 + 21)
                    nc.scalar.activation(row_e[:], row_fm[:], ACT.Exp, scale=-1.0).then_inc(gate_act, 1)

                def mlstm_exp(h):
                    act.wait_ge(mz_ready, l * HEADS + h + 1)
                    nc.scalar.activation(zw[:], zw[:], ACT.Exp).then_inc(mw_ready, 1)

                def mlstm_abs(h):
                    act.wait_ge(nd_ready, l * HEADS + h + 1)
                    if h > 0:
                        act.wait_ge(mrec_ready, l * HEADS + h)
                    nc.scalar.activation(mden[:], side[3][:, 0:T], ACT.Abs).then_inc(dabs_ready, 1)

                def mlstm_square(h):
                    act.wait_ge(hn_ready, l * HEADS + h + 1)
                    nc.scalar.activation(osq[:], hn[:], ACT.Square).then_inc(hsq_ready, 1)

                def mlstm_rstd(h):
                    act.wait_ge(hstat_ready, l * HEADS + h + 1)
                    nc.scalar.activation(lnv[:], side[3][:, 0:T], ACT.Ln, bias=eps1[:]).then_inc(hln_ready, 1)
                    act.wait_ge(hln_ready, l * HEADS + h + 1)
                    nc.scalar.activation(o_rs[:], lnv[:], ACT.Exp, scale=-0.5).then_inc(hrstd_ready, 1)

                def evict(i):
                    b = o_tile[i % 3]
                    if i == U_RAW:
                        act.wait_ge(mix_evict, n64 + U_RAW)
                    act.wait_ge(unit_done, g0 * RING + i + 1)
                    if i < U_MO and i % 3 < 2:
                        r = nc.scalar.activation(qk[:, i % 3 * 8 + i // 3], b, ACT.Copy)
                    elif i < U_MO or U_MV <= i < U_GL:
                        n = i // 3 if i < U_MO else i - U_MV + 8
                        act.wait_ge(vt_ready, l * 16 + n + 1)
                        r = nc.scalar.activation(vT[:, n % 2], b, ACT.Copy)
                    elif i < U_MQK:
                        r = nc.scalar.activation(h32[:, i - U_MO], b, ACT.Copy)
                    elif i < U_MV:
                        n = i - U_MQK
                        r = nc.scalar.activation(y[:, n], b, ACT.Identity, scale=p1("conv_w", 3 * 8 + n),
                                                 bias=p1("conv_b", n))
                    else:
                        r = nc.scalar.activation(gl[:, i - U_GL], b, ACT.Identity,
                                                 bias=p1("gate_b", i - U_GL))
                    r.then_inc(mix_evict, 1)

                for i in range(G_MIX * RING):
                    k, h = (i - A0) % 3, (i - A0) // 3
                    if i >= A0:
                        if k == 0 and h < HEADS:
                            attn_exp(h)
                        if k == 2 and 1 <= h <= HEADS:
                            attn_square(h - 1)
                        if k == 0 and 2 <= h <= HEADS + 1:
                            attn_rstd(h - 2)
                    k, h = (i - M0) % 3, (i - M0) // 3
                    if i >= M0:
                        if k == 0 and h < HEADS:
                            mlstm_exp(h)
                        if k == 2 and h < HEADS:
                            mlstm_abs(h)
                        if k == 0 and 1 <= h <= HEADS:
                            mlstm_square(h - 1)
                        if k == 1 and 1 <= h <= HEADS:
                            mlstm_rstd(h - 1)
                    if U_PM <= i < U_OUT:
                        m = i - U_PM
                        act.wait_ge(proj_done, l * 24 + 8 + 2 * (m + 1))
                        nc.scalar.activation(h_hi[:, m], gl[:, m], ACT.Copy).then_inc(hi_act, 1)
                    if i > 1:
                        hi_split(*ahead(g0 + i // RING, i % RING))
                    if i == U_RAW:
                        act.wait_ge(lam_sum, l + 1)
                        nc.scalar.activation(lame[:], side[1][:, 0:2], ACT.Exp).then_inc(lam_exp, 1)
                        gates()
                    if i == U_MQK + 4:
                        gate_e()
                    if U_RAW <= i < U_PA:
                        evict(i)
                    if i == U_MV + 1:
                        act.wait_ge(conv_done, l * 16 + 16)
                        nc.scalar.activation(y[:], y[:], ACT.Silu).then_inc(sig_ready, 1)
                    if i == U_MV + 3:
                        exp_set()
                    if i == U_MQK + 3:
                        act.wait_ge(mix_evict, n64 + U_MQK)
                        nc.scalar.activation(h32[:], h32[:], ACT.Sigmoid).then_inc(sig_ready, 1)
                        exp_set()
                    if i == U_PA:
                        act.wait_ge(mix_evict, n64 + 64)
                        nc.scalar.activation(gl[:], gl[:], ACT.Sigmoid).then_inc(sig_ready, 1)
                        exp_set()
                    if i >= U_OUT:
                        act.wait_ge(unit_done, g0 * RING + i + 1)
                        m = i - U_OUT
                        y_tile(l * 3 + 1, m, i % 3, p1("mix_post", m), m % 2)
                rstd(l * 6 + 3, eps1[:], rs[:], stat)
                raw_operand(l, 1, lambda m: x_tile(l * 3 + 2, m))

            def layer_norm(l, i, g, b):
                e = l * 2 + i
                for m in range(KT):
                    act.wait_ge(centred, e * KT + m + 1)
                    nc.scalar.activation(h32[:, m], y[:, m], ACT.Square).then_inc(sq_ready, 1)
                act.wait_ge(stat_ready, E0 + 2 + 2 * e)
                nc.scalar.activation(lnv[:], side[1][:, 0:T], ACT.Ln, bias=eps2[:]).then_inc(lnv_ready, 1)
                act.wait_ge(lnv_ready, E0 + 1 + e)
                nc.scalar.activation(rs[:], lnv[:], ACT.Exp, scale=-0.5).then_inc(rstd_ready, 1)
                for m in range(KT):
                    act.wait_ge(scaled2, e * KT + m + 1)
                    nc.scalar.activation(xr[:, m], y[:, m], ACT.Identity, bias=g2(l, b, m)).then_inc(x_ready, 1)
                    nc.scalar.activation(h_hi[:, m], y[:, m], ACT.Identity, bias=g2(l, b, m)).then_inc(hi_act, 1)

            def conv_ffn(l, g0):
                f = l + 4
                nc.scalar.preload_act_table_set("silu_and_others")
                with act.Fori(0, G_UP) as i:
                    g = g0 + i
                    for p in range(2):
                        act.wait_ge(gated, f * NF + i * 2 + p + 1)
                        for half in range(2):
                            s = 2 * p + half
                            hi_split(*ahead(g, s))
                            act.wait_ge(unit_done, g * RING + s + 1)
                            w = par[:, bass.ds(i * 2 + (C2["conv_w"] + 2 * 2 * NF + half * NF + p), 1)]
                            b = par[:, bass.ds(i * 2 + (C2["conv_b"] + half * NF + p), 1)]
                            nc.scalar.activation(cbuf[:, s], o_tile[s], ACT.Identity, scale=w,
                                                 bias=b).then_inc(conv2_base, 1)
                        act.wait_ge(conv2_done, l * (2 * NF) + i * 4 + 2 * p + 5)
                        nc.scalar.activation(silu_g[:, p], cbuf[:, 2 * p], ACT.Silu).then_inc(silu_done, 1)
                exp_set()
                with act.Fori(0, 2) as i:
                    for q in range(4 * DOWN_PARTS):
                        hi_split(*ahead(g0 + G_UP + i * DOWN_PARTS + q // RING, q % RING))
                layer_norm(l, 1, "ln2_g", "ln2_b")

            def mixer2(l, g0):
                n28 = l * 18

                def forget():
                    act.wait_ge(f_raw, l + 1)
                    nc.scalar.activation(row_abs[0:4], side[1][0:4, 0:T], ACT.Abs,
                                         bias=p2("b_forget")[0:4]).then_inc(f_act, 1)

                def forget_ln():
                    act.wait_ge(f_act, l * 3 + 1)
                    nc.scalar.activation(row_abs[0:4], row_abs[0:4], ACT.Exp, scale=-1.0).then_inc(f_act, 1)
                    act.wait_ge(f_act, l * 3 + 2)
                    nc.scalar.activation(row_l1[0:4], row_abs[0:4], ACT.Ln, bias=1.0).then_inc(f_act, 1)

                def sgu_square():
                    act.wait_ge(sgu_vec, l * 3 + 3)
                    nc.scalar.activation(sqc[:], xc[:], ACT.Square).then_inc(sgu_sq, 1)

                def sgu_rstd():
                    act.wait_ge(sgu_var, l + 1)
                    nc.scalar.activation(v8[:], v8[:], ACT.Ln, bias=eps2[:], scale=1.0 / 64).then_inc(sgu_ln, 1)
                    act.wait_ge(sgu_ln, l + 1)
                    nc.scalar.activation(r8[:], v8[:], ACT.Exp, scale=-0.5).then_inc(sgu_rs, 1)

                def attn_exp(h):
                    act.wait_ge(n2_ready, l * 8 + h + 1)
                    b = h % 2
                    for qt in range(2):
                        s = sm[:, b, 0:P] if qt == 0 else sm[:, b, P:3 * P]
                        k = 2 * b + qt
                        i = nc.scalar.activation(s, s, ACT.Exp, bias=nmx[:, k:k + 1], scale=A_SCALE,
                                                 accum_out=den[:, k:k + 1])
                    i.then_inc(e2_ready, 1)

                def pool_scale():
                    act.wait_ge(d_mixed, l + 1)
                    for ct in range(2):
                        r = nc.scalar.activation(d32[:, ct], side[3][:, ct * T:(ct + 1) * T], ACT.Copy,
                                                 scale=p2("pool_scale", ct))
                    r.then_inc(d_ready, 1)

                def value_hi(j):
                    act.wait_ge(o2_ready, l * 4 + j + 1)
                    nc.scalar.activation(ya_hi[:, j], side[3 if j % 2 == 0 else 0][:, 0:T],
                                         ACT.Copy).then_inc(o2_hi, 1)

                def evict(i):
                    b = o_tile[i % 3]
                    act.wait_ge(unit_done, g0 * RING + i + 1)
                    if i < V_CU:
                        r = nc.scalar.activation(gv[:, i], b, ACT.Gelu)
                    elif i < V_DP:
                        r = nc.scalar.activation(gu[:, (i - V_CU) * T:(i - V_CU + 1) * T], b, ACT.Gelu)
                    elif i < V_AQ:
                        r = nc.scalar.activation(pda[:, i - V_DP, PAD:], b, ACT.Copy)
                    elif i < V_AV:
                        r = nc.scalar.activation(qk[:, i - V_AQ], b, ACT.Copy)
                    else:
                        n = i - V_AV
                        if n >= 2:
                            act.wait_ge(v2_turned, l * 4 + n - 1)
                        r = nc.scalar.activation(vT[:, n % 2], b, ACT.Copy)
                    r.then_inc(m2_evict, 1)

                for i in range(G_MIX2 * RING):
                    if S2 <= i < S2 + 8:
                        attn_exp(i - S2)
                    if V_NONE <= i <= V_NONE + 1:
                        value_hi(i - V_NONE)
                    if i == V_OUT:
                        value_hi(2)
                        value_hi(3)
                    hi_split(*ahead(g0 + i // RING, i % RING))
                    if i == 1:
                        forget()
                    if i < V_NONE:
                        evict(i)
                    if i == 3:
                        exp_set()
                        sgu_square()
                        forget_ln()
                    if i == 4:
                        sgu_rstd()
                    if i == 13:
                        pool_scale()
                layer_norm(l, 0, "ln1_g", "ln1_b")

            for q in range(1, 4):
                act.dma_start(xr[:, 2 * q:2 * q + 2], x[:, 2 * q:2 * q + 2]).then_inc(x_in[q], 16)
            act.dma_start(cst[:, 0:2 * P], consts[:, 0:2 * P]).then_inc(ones_in, 16)
            exp_set()
            act.wait_ge(init, 3)
            act.wait_ge(gains_in, 16)
            raw_operand(0, 0, lambda m: act.wait_ge(x_in[m // 2], 16),
                        lambda m: hi_split(0, 0, first=True) if m == 1 else None)
            for s in range(1, AHEAD):
                hi_split(0, s, first=True)
            with act.Fori(0, DEPTH) as l:
                g = l * G_L1
                ffn(l, 0, g)
                act.wait_ge(par_in, l * 16 + 16)
                mixer(l, g + G_FFN)
                ffn(l, 1, g + G_FFN + G_MIX)
                raw_operand(l + 1, 0, lambda m: x_tile(l * 3 + 3, m))
            with act.Fori(0, DEPTH) as l:
                nc.scalar.preload_act_table_set("gelu_and_others")
                act.wait_ge(par_in, l * 16 + 16 * (DEPTH + 1))
                g = l * G_L2 + G_B2
                mixer2(l, g)
                conv_ffn(l, g + G_MIX2)

        @block.vector
        def _(dve):
            def lo_split(g, s):
                dve.wait_ge(hi_ready, g * RING + s + 1)
                nc.vector.tensor_tensor(w_lo[:, s], w_raw[:, s], w_hi[:, s].bitcast(F32),
                                        ALU.subtract).then_inc(split_done, 1)

            def mix_raw_rest(m):
                nc.vector.scalar_tensor_tensor(out=ya_lo[:, m], in0=xr[:, m], scalar=p1("mix_pre", m),
                                               in1=ya_hi[:, m].bitcast(F32), op0=ALU.mult,
                                               op1=ALU.subtract).then_inc(raw_split, 1)

            def pre_norm(l, i, w, g0):
                lo_split(*ahead(g0, 0))
                dve.wait_ge(rstd_ready, l * 6 + 2 * i + 1)

                def take(i, dst):
                    dve.wait_ge(unit_done, g0 * RING + i + 1)
                    nc.vector.tensor_tensor(dst, o_tile[i], rs[:], ALU.mult).then_inc(mix_evict, 1)

                take(0, qk[:, 0])
                hb = (l * 4 + 1) * KT

                def rest(m):
                    dve.wait_ge(hi_act, hb + m + 1)
                    nc.vector.tensor_tensor(h_lo[:, m], h32[:, m], h_hi[:, m].bitcast(F32),
                                            ALU.subtract).then_inc(h_split, 1)

                for m in range(KT):
                    nc.vector.scalar_tensor_tensor(out=h32[:, m], in0=xr[:, m], scalar=p1(w, m), in1=rs[:],
                                                   op0=ALU.mult, op1=ALU.mult).then_inc(h_ready, 1)
                    if m > 0:
                        rest(m - 1)
                    if m == 4:
                        take(1, qk[:, HEADS])
                        lo_split(*ahead(g0, 1))
                rest(KT - 1)
                take(2, vT[:, 0])

            def clear_acc(yb):
                nc.vector.memset(acc[:], 0.0).then_inc(acc_ready, 1)

            def add_squares(yb, m, slot):
                dve.wait_ge(y_sq, yb * KT + m + 5)
                dve.wait_ge(acc_ready, yb * (KT + 1) + m + 1)
                nc.vector.tensor_tensor(acc[:], acc[:], y_sqr[:, slot], ALU.add).then_inc(acc_ready, 1)

            def post_norm(l, i, rest):
                dve.wait_ge(rstd_ready, l * 6 + 2 * i + 2)
                yb = (l * 3 + i) * X_DVE

                def update(m):
                    dve.wait_ge(y_scaled, yb + m + 1)
                    nc.vector.tensor_tensor(xr[:, m], y[:, m], xr[:, m], ALU.add).then_inc(x_ready, 1)

                for m in range(X_DVE):
                    nc.vector.tensor_tensor(y[:, m], y[:, m], rs[:], ALU.mult).then_inc(y_scaled, 1)
                    if m > 0:
                        update(m - 1)
                    if m > 1:
                        rest(m - 2)
                update(X_DVE - 1)
                for m in range(X_DVE - 2, KT):
                    rest(m)

            def raw_rest(l, w, hb):
                def rest(m):
                    dve.wait_ge(hi_act, hb + m + 1)
                    nc.vector.scalar_tensor_tensor(out=h_lo[:, m], in0=xr[:, m], scalar=g1(l, f"ffn{w + 1}_pre", m),
                                                   in1=h_hi[:, m].bitcast(F32), op0=ALU.mult,
                                                   op1=ALU.subtract).then_inc(h_split, 1)
                return rest

            def ffn(l, w, g0):
                i_sub = 2 * w
                f = l * 2 + w
                with dve.Fori(0, G_UP) as i:
                    g = g0 + i
                    for p in range(2):
                        n = f * NF + i * 2 + p
                        lo_split(*ahead(g, 2 * p))
                        dve.wait_ge(rstd_ready, l * 6 + 2 * i_sub + 1)
                        dve.wait_ge(silu_done, n + 1)
                        dve.wait_ge(unit_done, g * RING + 2 * p + 1)
                        nc.vector.tensor_tensor(cbuf[:, p], o_tile[2 * p], rs[:], ALU.mult).then_inc(gate_scaled, 1)
                        lo_split(*ahead(g, 2 * p + 1))
                        dve.wait_ge(unit_done, g * RING + 2 * p + 2)
                        nc.vector.tensor_tensor(cbuf[:, 2 + p], o_tile[2 * p + 1], rs[:],
                                                ALU.mult).then_inc(up_scaled, 1)
                        dve.wait_ge(act_split, n + 1)
                        dve.wait_ge(silu_done, n + 3)
                        dve.wait_ge(up_scaled, n + 3)
                        nc.vector.tensor_tensor(act32[:, p], silu_g[:, p], cbuf[:, 2 + p],
                                                ALU.mult).then_inc(gated, 1)
                yb = l * 3 + i_sub
                clear_acc(yb)
                with dve.Fori(0, 2) as i:
                    for mm in range(4):
                        for part in range(DOWN_PARTS):
                            q = DOWN_PARTS * mm + part
                            lo_split(*ahead(g0 + G_UP + i * DOWN_PARTS + q // RING, q % RING))
                        add_squares(yb, i * 4 + mm, mm % 2)
                def mixer_rest(m):
                    dve.wait_ge(raw_act, l * KT + m + 1)
                    mix_raw_rest(m)

                if w == 0:
                    dve.wait_ge(par_in, l * 16 + 16)
                post_norm(l, i_sub, raw_rest(l + 1, 0, (l * 4 + 4) * KT) if w else mixer_rest)

            def mixer(l, g0):
                pre_norm(l, 1, "mix_pre", g0)
                n8 = l * HEADS
                nc.vector.tensor_tensor(lamp[:, 0:1], p1("lam", 0), p1("lam", 1), ALU.mult)
                nc.vector.tensor_tensor(lamp[:, 1:2], p1("lam", 2), p1("lam", 3), ALU.mult)
                nc.vector.tensor_tensor(wn[:], p1("attn_norm"), p1("one_minus_lam_init"),
                                        ALU.mult).then_inc(lam_step, 1)

                def gates():
                    dve.wait_ge(gate_act, l * 5 + 4)
                    nc.vector.tensor_scalar(row_min[:], side[2][32:32 + HEADS, 0:T], p1("fgate_b")[32:32 + HEADS],
                                            0.0, ALU.add, ALU.min).then_inc(gate_vec, 1)

                def gate_max(j):
                    k, am = 1 << j, j % 2
                    dve.wait_ge(gate_vec, l * 22 + 12 + j)
                    nc.vector.tensor_tensor(scan_m[:, 1 - am, P:], scan_m[:, am, P:], scan_m[:, am, P - k:P + T - k],
                                            ALU.max).then_inc(gate_vec, 1)
                    if 2 * k == T:
                        dve.wait_ge(gate_vec, l * 22 + 13 + j)
                        nc.vector.tensor_tensor(row_fm[:], scan_m[:, 1 - am, P:], scan_f[:, 1 - am, P:],
                                                ALU.add).then_inc(gate_vec, 1)
                        nc.vector.tensor_scalar(neg_m[:], scan_m[:, 1 - am, P:], -1.0, None,
                                                ALU.mult).then_inc(gate_vec, 1)

                def g_tok():
                    dve.wait_ge(g_turned, l + 1)
                    nc.vector.tensor_copy(gT[:], side[3][:, 0:QT * HEADS].rearrange("p (a h) -> p a h", a=QT)) \
                        .then_inc(g_tok_ready, 1)

                def store_v(n):
                    dve.wait_ge(vt_ready, l * 16 + n + 3)
                    dst = (v_tok if n < 8 else mv_tok)[:, n % 8]
                    nc.vector.tensor_copy(dst, tr[:, 0:T].rearrange("p (a d) -> p a d", a=QT)) \
                        .then_inc(vt_stored, 1)

                def conv(i):
                    n = i - U_MQK
                    b = o_tile[i % 3]
                    dve.wait_ge(mix_evict, l * 64 + i + 1)
                    for back in (1, 2, 3):
                        r = nc.vector.scalar_tensor_tensor(
                            out=y[:, n, back:], in0=b[:, 0:T - back], scalar=p1("conv_w", (3 - back) * 8 + n),
                            in1=y[:, n, back:], op0=ALU.mult, op1=ALU.add)
                        if back == 1:
                            r.then_inc(conv_step, 1)
                            dve.wait_ge(conv_step, (l * 8 + n) * 2 + 1)
                        if back == 2:
                            r.then_inc(conv_step, 1)
                            dve.wait_ge(conv_step, (l * 8 + n) * 2 + 2)
                    r.then_inc(conv_done, 2)

                def attn_mask(h):
                    if h > 0:
                        dve.wait_ge(comb_ready, n8 + h)
                    for m in range(2):
                        dve.wait_ge(sc_ready, (n8 + h) * 2 + m + 1)
                        nc.vector.memset(spare[:, 13 + m:14 + m], 0.0)
                        dve.wait_ge(consts_in, 16)
                        for qt, (a, b) in enumerate(((0, P), (P, 3 * P))):
                            r = nc.vector.tensor_tensor_reduce(
                                out=sm[:, m, a:b], in0=side[m][:, a:b], in1=mask_rows[:, a:b], scale=1.0,
                                scalar=-3e38, op0=ALU.add, op1=ALU.max,
                                accum_out=mx[:, 2 * m + qt:2 * m + qt + 1])
                        r.then_inc(sc_masked, 1)
                    dve.wait_ge(sc_masked, (n8 + h) * 2 + 2)
                    nc.vector.tensor_scalar(nmx[:], mx[:], -A_SCALE, None, ALU.mult).then_inc(nmax_ready, 1)

                def attn_combine(h):
                    dve.wait_ge(p_ready, n8 + h + 1)
                    nc.vector.reciprocal(rden[:], den[:]).then_inc(comb_step, 1)
                    dve.wait_ge(comb_step, (n8 + h) * 3 + 1)
                    nc.vector.tensor_scalar(rden[:, 2:4], rden[:, 2:4], nlam[:, 0:1], None,
                                            ALU.mult).then_inc(comb_step, 1)
                    if h > 0:
                        dve.wait_ge(aT_ready, n8 + h)
                    nc.vector.tensor_scalar(comb[:, 0:P], sm[:, 0, 0:P], rden[:, 0:1], None, ALU.mult)
                    nc.vector.tensor_scalar(comb[:, P:], sm[:, 0, P:], rden[:, 1:2], None,
                                            ALU.mult).then_inc(comb_step, 1)
                    dve.wait_ge(comb_step, (n8 + h) * 3 + 3)
                    nc.vector.scalar_tensor_tensor(out=comb[:, 0:P], in0=sm[:, 1, 0:P], scalar=rden[:, 2:3],
                                                   in1=comb[:, 0:P], op0=ALU.mult, op1=ALU.add)
                    nc.vector.scalar_tensor_tensor(out=comb[:, P:], in0=sm[:, 1, P:], scalar=rden[:, 3:4],
                                                   in1=comb[:, P:], op0=ALU.mult,
                                                   op1=ALU.add).then_inc(comb_ready, 1)

                def attn_store(h):
                    dve.wait_ge(aT_ready, n8 + h + 1)
                    if h > 0:
                        dve.wait_ge(o_ready, n8 + h)
                    nc.vector.tensor_copy(aT[:], side[2][:, 0:3 * P]).then_inc(aT_stored, 1)

                def attn_norm(h):
                    dve.wait_ge(orstd_ready, n8 + h + 1)
                    if h > 0:
                        dve.wait_ge(ya_split, n8 + h)
                    nc.vector.scalar_tensor_tensor(out=ya32[:], in0=side[3][:, 0:T], scalar=wn[:], in1=o_rs[:],
                                                   op0=ALU.mult, op1=ALU.mult).then_inc(o_normed, 1)

                def mlstm_z(h):
                    dve.wait_ge(ms_ready, n8 + h + 1)
                    if h > 0:
                        dve.wait_ge(mp_ready, n8 + h)
                    nc.vector.tensor_scalar(zw[:, 0:T], side[1][:, 0:T], gT[:, 0, h:h + 1], 0.0, ALU.add, ALU.min)
                    nc.vector.tensor_scalar(zw[:, T:], side[1][:, P:T], gT[:, 1, h:h + 1], 0.0, ALU.add,
                                            ALU.min).then_inc(mz_ready, 1)

                def mlstm_p(h):
                    dve.wait_ge(mwm_ready, (n8 + h) * 2 + 2)
                    if h > 0:
                        dve.wait_ge(nd_ready, n8 + h)
                    nc.vector.scalar_tensor_tensor(out=mp[:], in0=side[0][:, 0:3 * P], scalar=A_SCALE, in1=zw[:],
                                                   op0=ALU.mult, op1=ALU.mult).then_inc(mp_ready, 1)

                def mlstm_h(h):
                    dve.wait_ge(dabs_ready, n8 + h + 1)
                    nc.vector.tensor_tensor(mden[:], mden[:], side[1][:, T:2 * T], ALU.max).then_inc(mmax_ready, 1)
                    dve.wait_ge(mmax_ready, n8 + h + 1)
                    nc.vector.reciprocal(mrec[:], mden[:]).then_inc(mrec_ready, 1)
                    dve.wait_ge(mrec_ready, n8 + h + 1)
                    nc.vector.tensor_tensor(hn[:], mrec[:], side[2][:, 0:T], ALU.mult).then_inc(hn_ready, 1)

                def mlstm_norm(h):
                    dve.wait_ge(hrstd_ready, n8 + h + 1)
                    nc.vector.scalar_tensor_tensor(out=hn[:], in0=hn[:], scalar=p1("mlstm_norm", h), in1=o_rs[:],
                                                   op0=ALU.mult, op1=ALU.mult).then_inc(ym_step, 1)
                    dve.wait_ge(ym_step, n8 + h + 1)
                    dve.wait_ge(sig_ready, l * 3 + 1)
                    dve.wait_ge(ym_split if h > 0 else ya_split, n8 + (h or HEADS))
                    nc.vector.tensor_tensor(ya32[:], hn[:], h32[:, h], ALU.mult).then_inc(ym_ready, 1)

                def proj(i):
                    b = o_tile[i % 3]
                    if i == U_PA:
                        dve.wait_ge(sig_ready, l * 3 + 3)
                    dve.wait_ge(unit_done, g0 * RING + i + 1)
                    n = i - U_PA
                    nc.vector.tensor_tensor(gl[:, n], gl[:, n], b, ALU.mult).then_inc(proj_done, 1)
                    if i >= U_PM:
                        m = i - U_PM
                        dve.wait_ge(proj_done, l * 24 + 8 + 2 * m + 1)
                        nc.vector.tensor_tensor(gl[:, m], gl[:, m], gl[:, 8 + m], ALU.add).then_inc(proj_done, 1)
                        dve.wait_ge(hi_act, (l * 4 + 2) * KT + m + 1)
                        nc.vector.tensor_tensor(h_lo[:, m], gl[:, m], h_hi[:, m].bitcast(F32),
                                                ALU.subtract).then_inc(h_split, 1)

                for i in range(G_MIX * RING):
                    if i % 3 == 1 and 1 <= i // 3 <= HEADS:
                        store_v(i // 3 - 1)
                    if U_MV + 1 < i <= U_GL + 1:
                        store_v(i - U_MV - 2 + 8)
                    k, h = (i - A0) % 3, (i - A0) // 3
                    if i >= A0:
                        if k == 0 and h < HEADS:
                            attn_mask(h)
                        if k == 1 and 1 <= h <= HEADS:
                            attn_store(h - 1)
                        if k == 2 and h < HEADS:
                            attn_combine(h)
                        if k == 0 and 2 <= h <= HEADS + 1:
                            attn_norm(h - 2)
                    k, h = (i - M0) % 3, (i - M0) // 3
                    if i >= M0:
                        if k == 0 and h < HEADS:
                            mlstm_z(h)
                        if k == 1 and h < HEADS:
                            mlstm_p(h)
                        if k == 1 and 1 <= h <= HEADS:
                            mlstm_norm(h - 1)
                        if k == 2 and h < HEADS:
                            mlstm_h(h)
                    if U_PA <= i < U_OUT:
                        proj(i)
                    if i > 1:
                        lo_split(*ahead(g0 + i // RING, i % RING))
                    if i == U_RAW:
                        dve.wait_ge(lam_exp, l + 1)
                        nc.vector.scalar_tensor_tensor(out=nlam[:, 0:1], in0=lame[:, 1:2], scalar=lame[:, 0:1],
                                                       in1=p1("lam_init"), op0=ALU.subtract,
                                                       op1=ALU.subtract).then_inc(lam_ready, 1)
                        gates()
                    if U_MO <= i < U_MQK:
                        gate_max(i - U_MO)
                    if i == U_MQK + 4:
                        g_tok()
                    if U_MQK <= i < U_MV:
                        conv(i)
                    if i == U_OUT:
                        clear_acc(l * 3 + 1)
                    if i >= U_OUT:
                        add_squares(l * 3 + 1, i - U_OUT, (i - U_OUT) % 2)
                post_norm(l, 1, raw_rest(l, 1, (l * 4 + 3) * KT))

            def add_residual(l, i, m, b):
                z = xr[:, bass.ds(m, 1)].rearrange("p a t -> p (a t)")
                nc.vector.scalar_tensor_tensor(out=z, in0=z, scalar=ALPHA, in1=b, op0=ALU.mult,
                                               op1=ALU.add).then_inc(z_ready, 1)
                dve.wait_ge(z_ready, l * (2 * KT) + (i * KT + 5) + m)
                dve.wait_ge(acc_ready, (l * 2 + i) * (KT + 1) + (Y0 + 1) + m)
                nc.vector.tensor_tensor(acc[:], acc[:], z, ALU.add).then_inc(acc_ready, 1)

            def layer_norm(l, i, g):
                e = l * 2 + i
                dve.wait_ge(stat_ready, E0 + 1 + 2 * e)
                for m in range(KT):
                    nc.vector.tensor_tensor(y[:, m], xr[:, m], stat, ALU.subtract).then_inc(centred, 1)
                dve.wait_ge(rstd_ready, E0 + 1 + e)

                def rest(m):
                    dve.wait_ge(hi_act, H0 + KT + e * KT + m + 1)
                    nc.vector.tensor_tensor(h_lo[:, m], xr[:, m], h_hi[:, m].bitcast(F32),
                                            ALU.subtract).then_inc(h_split, 1)

                for m in range(KT):
                    nc.vector.scalar_tensor_tensor(out=y[:, m], in0=y[:, m], scalar=g2(l, g, m), in1=rs[:],
                                                   op0=ALU.mult, op1=ALU.mult).then_inc(scaled2, 1)
                    if m > 1:
                        rest(m - 2)
                rest(KT - 2)
                rest(KT - 1)

            def conv_ffn(l, g0):
                f = l + 4
                with dve.Fori(0, G_UP) as i:
                    g = g0 + i
                    for p in range(2):
                        for half in range(2):
                            s = 2 * p + half
                            lo_split(*ahead(g, s))
                            n = l * (2 * NF) + i * 4 + s
                            dve.wait_ge(conv2_base, n + 1)
                            for back in (1, 2):
                                w = par[:, bass.ds(i * 2 + (C2["conv_w"] + (2 - back) * 2 * NF + half * NF + p), 1)]
                                r = nc.vector.scalar_tensor_tensor(
                                    out=cbuf[:, s, back:], in0=o_tile[s][:, 0:T - back], scalar=w,
                                    in1=cbuf[:, s, back:], op0=ALU.mult, op1=ALU.add)
                                if back == 1:
                                    r.then_inc(conv2_step, 1)
                                    dve.wait_ge(conv2_step, n + 1)
                            r.then_inc(conv2_done, 1)
                        dve.wait_ge(act_split, f * NF + i * 2 + p + 1)
                        dve.wait_ge(conv2_done, l * (2 * NF) + i * 4 + 2 * p + 6)
                        dve.wait_ge(silu_done, f * NF + i * 2 + p + 3)
                        nc.vector.tensor_tensor(act32[:, p], silu_g[:, p], cbuf[:, 2 * p + 1],
                                                ALU.mult).then_inc(gated, 1)
                nc.vector.memset(spare[:, 10:11], 0.0).then_inc(par_free, 1)
                nc.vector.memset(acc[:], 0.0).then_inc(acc_ready, 1)
                with dve.Fori(0, 2) as i:
                    for mm in range(4):
                        for part in range(DOWN_PARTS):
                            q = DOWN_PARTS * mm + part
                            lo_split(*ahead(g0 + G_UP + i * DOWN_PARTS + q // RING, q % RING))
                        dve.wait_ge(unit_done, (g0 + G_UP + i * DOWN_PARTS) * RING + DOWN_PARTS * (mm + 1))
                        add_residual(l, 1, i * 4 + mm, o_tile[mm])
                layer_norm(l, 1, "ln2_g")

            def mixer2(l, g0):
                def forget():
                    dve.wait_ge(f_act, l * 3 + 1)
                    nc.vector.tensor_scalar(row_min[0:4], side[1][0:4, 0:T], p2("b_forget")[0:4], 0.0, ALU.add,
                                            ALU.min).then_inc(f_vec, 1)
                    dve.wait_ge(f_act, l * 3 + 3)
                    dve.wait_ge(f_vec, l * 11 + 1)
                    dve.wait_ge(pads_ready, DEPTH + l + 1)
                    nc.vector.tensor_tensor(scan_f[0:4, 0, P:], row_min[0:4], row_l1[0:4],
                                            ALU.subtract).then_inc(f_vec, 1)

                def forget_sum(j):
                    k, at = 1 << j, j % 2
                    dve.wait_ge(f_vec, l * 11 + 2 + j)
                    nc.vector.tensor_tensor(scan_f[0:4, 1 - at, P:], scan_f[0:4, at, P:],
                                            scan_f[0:4, at, P - k:P + T - k], ALU.add).then_inc(f_vec, 1)
                    if 2 * k == T:
                        dve.wait_ge(f_vec, l * 11 + 3 + j)
                        nc.vector.tensor_scalar(neg_m[0:4], scan_f[0:4, 1 - at, P:], -1.0 / A_SCALE, None,
                                                ALU.mult).then_inc(f_vec, 1)

                def groups(ap):
                    return ap.rearrange("p (g c) -> p g c", c=64)

                def sgu_centre():
                    dve.wait_ge(gv_turned, l + 1)
                    nc.vector.tensor_reduce(m8[:], groups(side[3][:, 0:2 * T]), AX.X, ALU.add).then_inc(sgu_vec, 1)
                    dve.wait_ge(sgu_vec, l * 3 + 1)
                    nc.vector.tensor_scalar(m8[:], m8[:], 1.0 / 64, None, ALU.mult).then_inc(sgu_vec, 1)
                    dve.wait_ge(sgu_vec, l * 3 + 2)
                    nc.vector.tensor_tensor(groups(xc[:]), groups(side[3][:, 0:2 * T]),
                                            m8[:].unsqueeze(2).to_broadcast([P, 8, 64]),
                                            ALU.subtract).then_inc(sgu_vec, 1)

                def sgu_variance():
                    dve.wait_ge(sgu_sq, l + 1)
                    nc.vector.tensor_reduce(v8[:], groups(sqc[:]), AX.X, ALU.add).then_inc(sgu_var, 1)

                def sgu_scale():
                    dve.wait_ge(sgu_rs, l + 1)
                    nc.vector.tensor_tensor(groups(xc[:]), groups(xc[:]),
                                            r8[:].unsqueeze(2).to_broadcast([P, 8, 64]),
                                            ALU.mult).then_inc(sgu_xn, 1)

                def sgu_gate():
                    dve.wait_ge(sgu_mixed, l + 1)
                    nc.vector.tensor_tensor(c32[:], gu[:], side[3][:, 0:2 * T], ALU.mult).then_inc(c_ready, 1)

                def rotate(n):
                    dve.wait_ge(swapped, l * 4 + n + 1)
                    t = ya32[:]
                    nc.vector.tensor_tensor(t, cst[:, CC["rot_sin"]:CC["rot_sin"] + T], side[2][:, 0:T], ALU.mult)
                    nc.vector.tensor_tensor(qk[:, n], qk[:, n], cst[:, CC["rot_cos"]:CC["rot_cos"] + T],
                                            ALU.mult).then_inc(rot_step, 1)
                    dve.wait_ge(rot_step, l * 4 + n + 1)
                    nc.vector.tensor_tensor(qk[:, n], qk[:, n], t, ALU.add).then_inc(rot_done, 1)

                def attn_mask(h):
                    b = h % 2
                    dve.wait_ge(s2_ready, l * 8 + h + 1)
                    if h >= 2:
                        dve.wait_ge(a2_turned, l * 8 + h - 1)
                    nc.vector.memset(spare[:, 13 + b:14 + b], 0.0)
                    dve.wait_ge(consts_in, 16)
                    for qt, (lo, hi) in enumerate(((0, P), (P, 3 * P))):
                        r = nc.vector.tensor_tensor_reduce(
                            out=sm[:, b, lo:hi], in0=side[b][:, lo:hi], in1=mask_rows[:, lo:hi], scale=1.0,
                            scalar=-3e38, op0=ALU.add, op1=ALU.max,
                            accum_out=mx[:, 2 * b + qt:2 * b + qt + 1])
                    r.then_inc(s2_masked, 1)
                    dve.wait_ge(s2_masked, l * 8 + h + 1)
                    nc.vector.tensor_scalar(nmx[:, 2 * b:2 * b + 2], mx[:, 2 * b:2 * b + 2], -A_SCALE, None,
                                            ALU.mult).then_inc(n2_ready, 1)

                def attn_scale(h):
                    b = h % 2
                    dve.wait_ge(e2_ready, l * 8 + h + 1)
                    nc.vector.reciprocal(rden[:, 2 * b:2 * b + 2], den[:, 2 * b:2 * b + 2]).then_inc(q2_step, 1)
                    dve.wait_ge(q2_step, l * 8 + h + 1)
                    nc.vector.tensor_scalar(sm[:, b, 0:P], sm[:, b, 0:P], rden[:, 2 * b:2 * b + 1], None, ALU.mult)
                    nc.vector.tensor_scalar(sm[:, b, P:], sm[:, b, P:], rden[:, 2 * b + 1:2 * b + 2], None,
                                            ALU.mult).then_inc(q2_ready, 1)

                def attn_store(h):
                    dve.wait_ge(a2_turned, l * 8 + h + 1)
                    nc.vector.tensor_copy(aT8[:, h], side[2][:, 0:3 * P]).then_inc(a2_stored, 1)

                def store_v(n):
                    dve.wait_ge(v2_turned, l * 4 + n + 1)
                    nc.vector.tensor_copy(v_tok[:, n], tr[:, 0:T].rearrange("p (a d) -> p a d", a=QT)) \
                        .then_inc(v2_stored, 1)

                def value_lo(j):
                    dve.wait_ge(o2_hi, l * 4 + j + 1)
                    nc.vector.tensor_tensor(ya_lo[:, j], side[3 if j % 2 == 0 else 0][:, 0:T],
                                            ya_hi[:, j].bitcast(F32), ALU.subtract).then_inc(ab_split, 1)

                for i in range(G_MIX2 * RING):
                    if V_AQ + 1 <= i <= V_AQ + 4:
                        rotate(i - V_AQ - 1)
                    if S2 <= i < S2 + 8:
                        attn_mask(i - S2)
                    if S2 + 2 <= i < S2 + 10:
                        attn_store(i - S2 - 2)
                    if S2 <= i < S2 + 8:
                        attn_scale(i - S2)
                    if V_AV + 2 <= i < V_AV + 6:
                        store_v(i - V_AV - 2)
                    if V_NONE <= i <= V_NONE + 1:
                        value_lo(i - V_NONE)
                    if i == V_OUT:
                        value_lo(2)
                        value_lo(3)
                    lo_split(*ahead(g0 + i // RING, i % RING))
                    if i == 2:
                        sgu_centre()
                    if i == 4:
                        sgu_variance()
                    if i == 5:
                        forget()
                        sgu_scale()
                    if V_AQ <= i < V_AQ + 4:
                        forget_sum(2 * (i - V_AQ))
                        forget_sum(2 * (i - V_AQ) + 1)
                    if i == 8:
                        sgu_gate()
                    if i == V_OUT:
                        nc.vector.memset(acc[:], 0.0).then_inc(acc_ready, 1)
                    if i >= V_OUT:
                        dve.wait_ge(unit_done, g0 * RING + i + 1)
                        add_residual(l, 0, i - V_OUT, o_tile[i % 3])
                layer_norm(l, 0, "ln1_g")

            nc.vector.memset(spare[:, 19:20], 0.0).then_inc(split_done, 1)
            nc.vector.memset(eps1[:], EPS).then_inc(init, 1)
            nc.vector.memset(eps2[:], LN_EPS).then_inc(init, 1)
            nc.vector.memset(ln_half[:], math.log(0.5)).then_inc(init, 1)
            nc.vector.memset(spare[:, 15:16], 0.0).then_inc(par_free, 1)
            nc.vector.memset(spare[:, 8:9], 0.0).then_inc(y_sq, 4)
            nc.vector.memset(spare[:, 17:18], 0.0).then_inc(y_taken, 4)
            nc.vector.memset(spare[:, 11:12], 0.0).then_inc(z_ready, 4)
            nc.vector.memset(spare[:, 12:13], 0.0).then_inc(conv2_done, 4)
            dve.wait_ge(gains_in, 16)
            rest = raw_rest(0, 0, 0)
            for m in range(KT):
                dve.wait_ge(x_in[m // 2], 16)
                rest(m)
                if m == 1:
                    lo_split(0, 0)
                    dve.wait_ge(x_in[3], 16)
                    nc.vector.memset(spare[:, 18:19], 0.0).then_inc(split_done, RING - 1)
            nc.vector.memset(spare[:, 9:10], 0.0).then_inc(x_ready, X_DVE)
            for s in range(1, AHEAD):
                lo_split(0, s)
            with dve.Fori(0, DEPTH) as l:
                g = l * G_L1
                ffn(l, 0, g)
                mixer(l, g + G_FFN)
                nc.vector.memset(spare[:, 10:11], 0.0).then_inc(par_free, 1)
                ffn(l, 1, g + G_FFN + G_MIX)
            with dve.Fori(0, DEPTH) as l:
                dve.wait_ge(par_in, l * 16 + 16 * (DEPTH + 1))
                g = l * G_L2 + G_B2
                mixer2(l, g)
                conv_ffn(l, g + G_MIX2)

        @block.gpsimd
        def _(pool):
            credits = ((silu_done, 2), (gated, 2), (act_split, 2), (vt_ready, 2), (vt_stored, 1),
                       (gate_scaled, 2), (up_scaled, 2))
            for k, (s, n) in enumerate(credits):
                nc.gpsimd.memset(spare[:, k:k + 1], 0.0).then_inc(s, n)

            def split(src, hi, lo, rounded, n, done):
                nc.gpsimd.tensor_tensor(hi, src, ones_t, ALU.mult).then_inc(rounded, 1)
                pool.wait_ge(rounded, n)
                nc.gpsimd.tensor_tensor(lo, src, hi.bitcast(F32), ALU.subtract).then_inc(done, 1)

            ones_t = ones.unsqueeze(1).to_broadcast([P, 2, P])

            def halves(ap):
                return ap.rearrange("p (a b) -> p a b", a=2)

            def ffn(l, w):
                f = l * 2 + w
                with pool.Fori(0, G_UP) as i:
                    for p in range(2):
                        pool.wait_ge(gated, f * NF + i * 2 + p + 3)
                        j = i * 2 + p
                        hi = act_hi[:, bass.ds(j, 1)].rearrange("p a (b t) -> p (a b) t", b=2)
                        lo = act_lo[:, bass.ds(j, 1)].rearrange("p a (b t) -> p (a b) t", b=2)
                        split(halves(act32[:, p]), hi, lo, act_rounded, f * NF + j + 1, act_split)
                post_norm(l, 2 * w)

            def post_norm(l, i):
                pool.wait_ge(rstd_ready, l * 6 + 2 * i + 2)
                for k, m in enumerate(range(X_DVE, KT)):
                    n = (l * 3 + i) * X_POOL + k + 1
                    nc.gpsimd.tensor_tensor(y[:, m], y[:, m], rs[:], ALU.mult).then_inc(y_pool, 1)
                    pool.wait_ge(y_pool, n)
                    nc.gpsimd.tensor_tensor(xr[:, m], y[:, m], xr[:, m], ALU.add).then_inc(x_pool, 1)

            def mixer(l):
                n8 = l * HEADS
                nc.gpsimd.tensor_tensor(scan_f[:, :, 0:P], ones[0:HEADS].unsqueeze(1).to_broadcast([HEADS, 2, P]),
                                        ones[0:HEADS].unsqueeze(1).to_broadcast([HEADS, 2, P]), ALU.subtract)
                nc.gpsimd.memset(scan_m[:, :, 0:P], 0.0).then_inc(pads_ready, 1)
                pool.wait_ge(pads_ready, l + 1)

                def gates():
                    n = [l * 22, 1]

                    def link(ins):
                        n[1] += 1
                        ins.then_inc(gate_vec, 1)
                        pool.wait_ge(gate_vec, n[0] + n[1])

                    pool.wait_ge(gate_act, l * 5 + 4)
                    pool.wait_ge(gate_vec, l * 22 + 1)
                    link(nc.gpsimd.tensor_tensor(scan_f[:, 0, P:], row_min[:], row_l1[:], ALU.subtract))
                    k, at = 1, 0
                    while k < T:
                        link(nc.gpsimd.tensor_tensor(scan_f[:, 1 - at, P:], scan_f[:, at, P:],
                                                     scan_f[:, at, P - k:P + T - k], ALU.add))
                        k, at = 2 * k, 1 - at
                    link(nc.gpsimd.tensor_tensor(scan_m[:, 0, P:], row_i[:], scan_f[:, at, P:], ALU.subtract))
                    link(nc.gpsimd.tensor_tensor(row_min[:], row_i[:], scan_f[:, at, P:], ALU.subtract))

                gates()
                for h in range(HEADS):
                    pool.wait_ge(o_normed, n8 + h + 1)
                    split(halves(ya32[:]), halves(ya_hi[:, h]), halves(ya_lo[:, h]), side_rounded,
                          n8 * 2 + h + 1, ya_split)
                for h in range(HEADS):
                    pool.wait_ge(mw_ready, n8 + h + 1)
                    nc.gpsimd.tensor_tensor(zw[:, 0:P], zw[:, 0:P], mask_cols, ALU.mult).then_inc(mwm_ready, 1)
                    nc.gpsimd.tensor_tensor(zw[:, T:], zw[:, T:], mask_cols, ALU.mult).then_inc(mwm_ready, 1)
                    if h > 0:
                        ym(n8, h - 1)
                ym(n8, HEADS - 1)
                post_norm(l, 1)

            def ym(n8, h):
                pool.wait_ge(ym_ready, n8 + h + 1)
                split(halves(ya32[:]), halves(yms_hi[:, h]), halves(yms_lo[:, h]), side_rounded,
                      n8 * 2 + HEADS + h + 1, ym_split)

            def conv_ffn(l):
                f = l + 4
                with pool.Fori(0, G_UP) as i:
                    for p in range(2):
                        pool.wait_ge(gated, f * NF + i * 2 + p + 3)
                        j = i * 2 + p
                        hi = act_hi[:, bass.ds(j, 1)].rearrange("p a (b t) -> p (a b) t", b=2)
                        lo = act_lo[:, bass.ds(j, 1)].rearrange("p a (b t) -> p (a b) t", b=2)
                        split(halves(act32[:, p]), hi, lo, act_rounded, f * NF + j + 1, act_split)

            def mixer2(l):
                nc.gpsimd.tensor_tensor(scan_f[0:4, :, 0:P], ones[0:4].unsqueeze(1).to_broadcast([4, 2, P]),
                                        ones[0:4].unsqueeze(1).to_broadcast([4, 2, P]),
                                        ALU.subtract).then_inc(pads_ready, 1)
                nc.gpsimd.memset(pda[:, :, 0:PAD], 0.0)
                nc.gpsimd.memset(pdb[:, :, 0:PAD], 0.0).then_inc(pool_step, 1)
                w = p2("sgu_w", 0, 4 * P).rearrange("p (g t) -> p g t", g=4)
                nc.gpsimd.tensor_tensor(w, w, mask_cols.unsqueeze(1).to_broadcast([P, 4, P]),
                                        ALU.mult).then_inc(sgu_w_masked, 1)
                pool.wait_ge(sgu_xn, l + 1)
                two = xc[:].rearrange("p (a c) -> p a c", a=2)
                out2 = vn[:].rearrange("p (a c) -> p a c", a=2)
                nc.gpsimd.tensor_tensor(two, two, p2("sgu_g", 0, T).unsqueeze(1).to_broadcast([P, 2, T]),
                                        ALU.mult).then_inc(sgu_step, 1)
                pool.wait_ge(sgu_step, l + 1)
                nc.gpsimd.tensor_tensor(out2, two, p2("sgu_b_ln", 0, T).unsqueeze(1).to_broadcast([P, 2, T]),
                                        ALU.add).then_inc(vn_ready, 1)
                n = [l * 10 + 1]

                def link(ins):
                    n[0] = n[0] + 1
                    ins.then_inc(pool_step, 1)
                    pool.wait_ge(pool_step, n[0])

                pool.wait_ge(m2_evict, l * 18 + V_AQ)
                pool.wait_ge(pool_step, l * 10 + 1)

                def doubled(rows, ct, src, dst, back):
                    link(nc.gpsimd.tensor_tensor(dst[rows, ct, PAD:], src[rows, ct, PAD:],
                                                 src[rows, ct, PAD - back:PAD + T - back], ALU.add))

                everything, upper, lower = slice(0, P), slice(64, P), slice(0, 64)
                link(nc.gpsimd.tensor_tensor(pooled[:], pda[:, :, PAD:],
                                             ones[:, 0:1].unsqueeze(1).to_broadcast([P, 2, T]), ALU.mult))
                doubled(everything, 0, pda, pdb, 1)
                doubled(upper, 0, pdb, pda, 2)
                doubled(everything, 1, pda, pdb, 1)
                doubled(everything, 1, pdb, pda, 2)
                doubled(everything, 1, pda, pdb, 4)
                doubled(upper, 1, pdb, pda, 8)
                inv = cst[:, CC["inv_count"]:CC["inv_count"] + 2 * T].rearrange("p (a t) -> p a t", a=2)
                nc.gpsimd.tensor_tensor(pda[upper, :, PAD:], pda[upper, :, PAD:], inv[upper], ALU.mult)
                link(nc.gpsimd.tensor_tensor(pda[lower, :, PAD:], pdb[lower, :, PAD:], inv[lower], ALU.mult))
                link(nc.gpsimd.tensor_tensor(pooled[:], pda[:, :, PAD:], pooled[:], ALU.subtract))
                pool.wait_ge(c_ready, l + 1)
                for ct in range(2):
                    split(halves(c32[:, ct * T:(ct + 1) * T]), halves(ya_hi[:, 4 + ct]), halves(ya_lo[:, 4 + ct]),
                          cd_rounded, l * 4 + ct + 1, cd_split)
                pool.wait_ge(d_ready, l + 1)
                for ct in range(2):
                    split(halves(d32[:, ct]), halves(ya_hi[:, 6 + ct]), halves(ya_lo[:, 6 + ct]),
                          cd_rounded, l * 4 + ct + 3, cd_split)

            pool.wait_ge(x_in[3], 16)
            nc.gpsimd.memset(spare[:, 16:17], 0.0).then_inc(x_pool, X_POOL)
            pool.wait_ge(raw_full[AHEAD - 1], 16)
            pool.dma_start(cst[:, 2 * P:], consts[:, 2 * P:]).then_inc(consts_in, 16)
            pool.wait_ge(ones_in, 16)

            def load_params(k):
                pool.wait_ge(par_free, k + 1)
                pool.dma_start(par[:], params[bass.ds(k, 1)].rearrange("a p n -> (a p) n")).then_inc(par_in, 16)

            def second_layer(l):
                pool.wait_ge(consts_in, 16)
                pool.wait_ge(unit_done, (l * G_L2 + G_B2) * RING)
                pool.wait_ge(par_in, l * 16 + 16 * (DEPTH + 1))
                mixer2(l)
                conv_ffn(l)

            load_params(0)
            with pool.Fori(0, DEPTH) as l:
                ffn(l, 0)
                pool.wait_ge(consts_in, 16)
                pool.wait_ge(unit_done, (l * G_L1 + G_FFN) * RING)
                mixer(l)
                load_params(l + 1)
                ffn(l, 1)
            with pool.Fori(0, DEPTH - 1) as l:
                second_layer(l)
                load_params(l + (DEPTH + 1))
            second_layer(DEPTH - 1)

        @block.tensor
        def _(pe):
            def product(dst, s, k, hi, lo, first, last):
                w = slice(k * P, (k + 1) * P)
                nc.tensor.matmul(dst, w_hi[:, s, w], hi, start=first, stop=False)
                nc.tensor.matmul(dst, w_hi[:, s, w], lo, start=False, stop=False)
                return nc.tensor.matmul(dst, w_lo[:, s, w], hi, start=False, stop=last)

            def unit(g, s):
                pe.wait_ge(split_done, g * RING + (s + 1 + RING))

            def model_unit(dst, s, hi, lo, waits=None):
                for k in range(KT):
                    if waits:
                        waits(k)
                    r = product(dst, s, k, hi[:, k], lo[:, k], k == 0, k == KT - 1)
                r.then_inc(unit_done, 1)

            def squares(n, k):
                pe.wait_ge(sq_ready, n * KT + k + 1)
                r = nc.tensor.matmul(stat, ones_model, h32[:, k], start=(k == 0), stop=(k == KT - 1))
                if k == KT - 1:
                    r.then_inc(stat_ready, 1)

            def paced_unit(s, hi, lo, arrived, hb, n):
                for k in range(KT):
                    pe.wait_ge(arrived, hb + k + 1)
                    r = product(o_tile[0], s, k, hi[:, k], lo[:, k], k == 0, k == KT - 1)
                    if k < KT - 1:
                        squares(n, k)
                r.then_inc(unit_done, 1)
                squares(n, KT - 1)

            def post_norm(yb):
                pe.wait_ge(acc_ready, yb * (KT + 1) + KT + 1)
                nc.tensor.matmul(stat, ones_model, acc[:], start=True, stop=True).then_inc(stat_ready, 1)

            def ffn(l, w, g0):
                i_sub = 2 * w
                f = l * 2 + w
                hb = (l * 4 + 3 * w) * KT

                def up_group(i, first=False):
                    for s in range(RING):
                        unit(g0 + i, s)
                        pe.wait_ge(up_scaled if s % 2 else gate_scaled, f * NF + i * 2 + s // 2 + 1)
                        if first and s == 0:
                            paced_unit(s, h_hi, h_lo, h_split, hb, l * 3 + i_sub)
                        else:
                            model_unit(o_tile[s], s, h_hi, h_lo)

                up_group(0, first=True)
                with pe.Fori(1, G_UP) as i:
                    up_group(i)
                yb = l * 3 + i_sub
                with pe.Fori(0, 2) as i:
                    for mm in range(4):
                        pe.wait_ge(y_taken, yb * KT + i * 4 + mm + 1)
                        pe.wait_ge(up_scaled if mm % 2 else gate_scaled, f * NF + NF + 1 + mm // 2)
                        for part in range(DOWN_PARTS):
                            q = DOWN_PARTS * mm + part
                            s = q % RING
                            unit(g0 + G_UP + i * DOWN_PARTS + q // RING, s)
                            ks = range(KT * part, min(KT * (part + 1), NF))
                            pe.wait_ge(act_split, f * NF + ks[-1] + 3)
                            for k in ks:
                                r = product(o_tile[mm], s, k - KT * part, act_hi[:, k], act_lo[:, k], k == 0,
                                            k == NF - 1)
                            r.then_inc(unit_done, 1)
                post_norm(yb)

            def mixer(l, g0):
                n8 = l * HEADS
                hb = (l * 4 + 1) * KT

                def gates():
                    wg = par[:, C1["w_gates"]:C1["w_gates"] + KT * 64].rearrange("p (k n) -> p k n", k=KT)
                    for k in range(KT):
                        r = nc.tensor.matmul(side[2][0:64, 0:T], wg[:, k], h32[:, k], start=(k == 0),
                                             stop=(k == KT - 1))
                    r.then_inc(gates_raw, 1)

                def g_tok():
                    pe.wait_ge(consts_in, 16)
                    pe.wait_ge(gate_vec, l * 22 + 12)
                    pe.wait_ge(o_normed, n8 + HEADS)
                    for a in range(QT):
                        r = nc.tensor.matmul(side[3][:, a * HEADS:(a + 1) * HEADS], row_min[:, a * P:(a + 1) * P],
                                             ident[0:HEADS, 0:HEADS], start=True, stop=True)
                    r.then_inc(g_turned, 1)

                def turn_v(n):
                    i = 3 * n + 2 if n < 8 else U_MV + n - 8
                    pe.wait_ge(mix_evict, l * 64 + i + 1)
                    pe.wait_ge(vt_stored, l * 16 + n + 1)
                    for a in range(QT):
                        r = nc.tensor.transpose(tr[:, a * P:(a + 1) * P], vT[:, n % 2, a * P:(a + 1) * P], ident)
                    r.then_inc(vt_ready, 1)

                def scores(h):
                    pe.wait_ge(mix_evict, l * 64 + 3 * h + 2)
                    if h == 0:
                        pe.wait_ge(lam_exp, l + 1)
                    for m in range(2):
                        if h > 0:
                            pe.wait_ge(sc_masked, (n8 + h) * 2 - 1 + m)
                        r = slice(64 * m, 64 * m + 64)
                        nc.tensor.matmul(side[m][:, 0:P], qk[r, h, 0:P], qk[r, 8 + h, 0:P], start=True, stop=True)
                        nc.tensor.matmul(side[m][:, P:3 * P], qk[r, h, P:T], qk[r, 8 + h, :], start=True,
                                         stop=True).then_inc(sc_ready, 1)

                def turn_a(h):
                    pe.wait_ge(comb_ready, n8 + h + 1)
                    if h > 0:
                        pe.wait_ge(aT_stored, n8 + h)
                    else:
                        pe.wait_ge(gate_vec, l * 22 + 1)
                    for b in range(3):
                        r = nc.tensor.transpose(side[2][:, b * P:(b + 1) * P], comb[:, blk(b)], ident)
                    r.then_inc(aT_ready, 1)

                def values(h):
                    pe.wait_ge(aT_stored, n8 + h + 1)
                    pe.wait_ge(vt_stored, l * 16 + h + 2)
                    if h > 0:
                        pe.wait_ge(o_normed, n8 + h)
                    nc.tensor.matmul(side[3][:, 0:T], v_tok[:, h, 0], aT[:, 0:T], start=True, stop=False)
                    nc.tensor.matmul(side[3][:, P:T], v_tok[:, h, 1], aT[:, T:], start=False,
                                     stop=True).then_inc(o_ready, 1)

                def head_mean(h):
                    pe.wait_ge(osq_ready, n8 + h + 1)
                    nc.tensor.matmul(side[3][:, T:2 * T], ones_head, osq[:], start=True,
                                     stop=True).then_inc(ostat_ready, 1)

                def row(h):
                    return ident[0:HEADS, h:h + 1].to_broadcast([HEADS, P])

                def mlstm_scores(h):
                    if h == 0:
                        pe.wait_ge(sig_ready, l * 3 + 2)
                        pe.wait_ge(sc_masked, (n8 + HEADS) * 2)
                        pe.wait_ge(gate_act, l * 5 + 5)
                        pe.wait_ge(gate_vec, l * 22 + 22)
                    else:
                        pe.wait_ge(mp_ready, n8 + h)
                        pe.wait_ge(mmax_ready, n8 + h)
                    r = slice(64 * (h % 2), 64 * (h % 2) + 64)
                    q, k = y[r, h // 2], y[r, 4 + h // 2]
                    nc.tensor.matmul(side[0][:, 0:T], k[:, 0:P], q, start=True, stop=True)
                    nc.tensor.matmul(side[0][:, T:3 * P], k[:, P:T], q[:, P:T], start=True, stop=True)
                    nc.tensor.matmul(side[1][:, 0:T], row(h), neg_m[:], start=True, stop=True)
                    nc.tensor.matmul(side[1][:, T:2 * T], row(h), row_e[:], start=True,
                                     stop=True).then_inc(ms_ready, 1)

                def mlstm_values(h):
                    pe.wait_ge(mp_ready, n8 + h + 1)
                    pe.wait_ge(vt_stored, l * 16 + 8 + h + 2)
                    if h == 0:
                        pe.wait_ge(orstd_ready, n8 + HEADS)
                        pe.wait_ge(o_normed, n8 + HEADS)
                    else:
                        pe.wait_ge(hn_ready, n8 + h)
                        pe.wait_ge(hrstd_ready, n8 + h)
                    nc.tensor.matmul(side[2][:, 0:T], mv_tok[:, h, 0], mp[:, 0:T], start=True, stop=False)
                    nc.tensor.matmul(side[2][:, P:T], mv_tok[:, h, 1], mp[:, T:], start=False, stop=True)
                    nc.tensor.matmul(side[3][:, 0:T], ones, mp[:, 0:T], start=True, stop=False)
                    nc.tensor.matmul(side[3][:, P:T], ones, mp[:, T:], start=False, stop=True).then_inc(nd_ready, 1)

                def mlstm_mean(h):
                    pe.wait_ge(hsq_ready, n8 + h + 1)
                    nc.tensor.matmul(side[3][:, 0:T], ones_head, osq[:], start=True,
                                     stop=True).then_inc(hstat_ready, 1)

                def waits(i):
                    if i < 3:
                        pass
                    elif i - 3 < U_PA:
                        pe.wait_ge(mix_evict, l * 64 + i - 2)
                    elif i - 3 < U_PM:
                        pe.wait_ge(proj_done, l * 24 + i - 3 - U_PA + 1)
                    elif i - 3 < U_OUT:
                        pe.wait_ge(proj_done, l * 24 + 8 + 2 * (i - 3 - U_PM) + 1)
                    else:
                        pe.wait_ge(y_taken, (l * 3 + 1) * KT + 4 + i - 3 - U_OUT + 1)
                    if U_MQK <= i - 3 < U_MV:
                        pe.wait_ge(conv_done, l * 16 + 2 * (i - 3 - U_MQK + 1))

                for i in range(G_MIX * RING):
                    k, h = (i - A0) % 3, (i - A0) // 3
                    if i % 3 == 1 and 1 <= i // 3 <= HEADS:
                        turn_v(i // 3 - 1)
                    if U_MV + 1 < i <= U_GL + 1:
                        turn_v(i - U_MV - 2 + 8)
                    if i >= A0:
                        if k == 0 and h < HEADS:
                            scores(h)
                        if k == 1 and 1 <= h <= HEADS:
                            turn_a(h - 1)
                        if k == 2 and 1 <= h <= HEADS:
                            values(h - 1)
                        if k == 0 and 2 <= h <= HEADS + 1:
                            head_mean(h - 2)
                    k, h = (i - M0) % 3, (i - M0) // 3
                    if i >= M0:
                        if k == 0 and h < HEADS:
                            mlstm_scores(h)
                        if k == 1 and 1 <= h <= HEADS:
                            mlstm_mean(h - 1)
                        if k == 2 and h < HEADS:
                            mlstm_values(h)
                    g, s = g0 + i // RING, i % RING
                    unit(g, s)
                    waits(i)
                    if i == 0:
                        paced_unit(s, ya_hi, ya_lo, raw_split, l * KT, l * 3 + 1)
                    elif i < U_RAW:
                        model_unit(o_tile[i % 3], s, ya_hi, ya_lo)
                    elif i < U_PA:
                        model_unit(o_tile[i % 3], s, h_hi, h_lo,
                                   (lambda k: pe.wait_ge(h_split, hb + k + 1)) if i == U_RAW else None)
                    elif i < U_PM:
                        model_unit(o_tile[i % 3], s, ya_hi, ya_lo,
                                   (lambda k: pe.wait_ge(ya_split, n8 + k + 1)) if i == U_PA else None)
                    elif i < U_OUT:
                        model_unit(o_tile[i % 3], s, yms_hi, yms_lo,
                                   (lambda k: pe.wait_ge(ym_split, n8 + k + 1)) if i == U_PM else None)
                    else:
                        model_unit(o_tile[i % 3], s, h_hi, h_lo,
                                   (lambda k: pe.wait_ge(h_split, hb + KT + k + 1)) if i == U_OUT else None)
                    if i == U_RAW:
                        pe.wait_ge(lam_step, l + 1)
                        nc.tensor.matmul(side[1][:, 0:2], ones, lamp[:], start=True, stop=True).then_inc(lam_sum, 1)
                        gates()
                    if i == U_MQK + 4:
                        g_tok()
                post_norm(l * 3 + 1)

            def blk(b):
                return slice(b * P, (b + 1) * P)

            def layer_norm(l, i):
                e = l * 2 + i
                pe.wait_ge(acc_ready, e * (KT + 1) + Y0 + KT + 1)
                nc.tensor.matmul(stat, ones_model, acc[:], start=True, stop=True).then_inc(stat_ready, 1)
                for m in range(KT):
                    pe.wait_ge(sq_ready, Q0 + e * KT + m + 1)
                    r = nc.tensor.matmul(side[1][:, 0:T], ones_model, h32[:, m], start=(m == 0), stop=(m == KT - 1))
                r.then_inc(stat_ready, 1)

            def conv_ffn(l, g0):
                f = l + 4
                hb = H0 + (l * 2 + 1) * KT
                with pe.Fori(0, G_UP) as i:
                    for s in range(RING):
                        unit(g0 + i, s)
                        pe.wait_ge(conv2_done, l * (2 * NF) + i * 4 + s + 1)
                        model_unit(o_tile[s], s, h_hi, h_lo,
                                   (lambda k: pe.wait_ge(h_split, hb + k + 1)) if s == 0 else None)
                with pe.Fori(0, 2) as i:
                    for mm in range(4):
                        pe.wait_ge(z_ready, l * (2 * KT) + KT + i * 4 + mm + 1)
                        pe.wait_ge(conv2_done, l * (2 * NF) + 2 * NF + mm + 1)
                        for part in range(DOWN_PARTS):
                            q = DOWN_PARTS * mm + part
                            s = q % RING
                            unit(g0 + G_UP + i * DOWN_PARTS + q // RING, s)
                            ks = range(KT * part, min(KT * (part + 1), NF))
                            pe.wait_ge(act_split, f * NF + ks[-1] + 3)
                            for k in ks:
                                r = product(o_tile[mm], s, k - KT * part, act_hi[:, k], act_lo[:, k], k == 0,
                                            k == NF - 1)
                            r.then_inc(unit_done, 1)
                layer_norm(l, 1)

            def mixer2(l, g0):
                hb = H0 + l * 2 * KT

                def forget():
                    wf = p2("w_forget", 0, KT * 32).rearrange("p (k n) -> p k n", k=KT)
                    for k in range(KT):
                        r = nc.tensor.matmul(side[1][0:32, 0:T], wf[:, k], xr[:, k], start=(k == 0),
                                             stop=(k == KT - 1))
                    r.then_inc(f_raw, 1)

                def turn_gv():
                    pe.wait_ge(m2_evict, l * 18 + 2)
                    pe.wait_ge(consts_in, 16)
                    for a in range(QT):
                        for ct in range(2):
                            r = nc.tensor.transpose(side[3][:, a * T + ct * P:a * T + (ct + 1) * P],
                                                    gv[:, ct, a * P:(a + 1) * P], ident)
                    r.then_inc(gv_turned, 1)

                def spatial():
                    pe.wait_ge(sgu_w_masked, l + 1)
                    pe.wait_ge(vn_ready, l + 1)
                    for g in range(4):
                        rows, ct = slice(64 * (g % 2), 64 * (g % 2) + 64), g // 2
                        for a in range(QT):
                            dst = side[3][rows, ct * T + a * P:ct * T + (a + 1) * P]
                            nc.tensor.matmul(dst, vn[:, a * T + 64 * g:a * T + 64 * g + 64], p2("sgu_w", g * P, P),
                                             start=True, stop=False)
                            r = nc.tensor.matmul(dst, ident[0:4, g:g + 1].to_broadcast([4, 64]),
                                                 p2("sgu_b", 0, P)[0:4], start=False, stop=True)
                    r.then_inc(sgu_mixed, 1)

                def pooling():
                    pe.wait_ge(pool_step, l * 10 + 10)
                    pe.wait_ge(c_ready, l + 1)
                    for ct in range(2):
                        r = nc.tensor.matmul(side[3][:, ct * T:(ct + 1) * T], p2("pool_w", ct * P, P),
                                             pooled[:, ct], start=True, stop=True)
                    r.then_inc(d_mixed, 1)

                def swap(n):
                    pe.wait_ge(m2_evict, l * 18 + V_AQ + n + 1)
                    if n > 0:
                        pe.wait_ge(rot_done, l * 4 + n)
                    nc.tensor.matmul(side[2][:, 0:T], cst[:, CC["rot_swap"]:CC["rot_swap"] + P], qk[:, n],
                                     start=True, stop=True).then_inc(swapped, 1)

                def scores(h):
                    b = side[h % 2]
                    forgets = h >= 4
                    r = slice(64 * (h % 2), 64 * (h % 2) + 64)
                    q, k = (4 if forgets else 0) + (h % 4) // 2, (6 if forgets else 2) + (h % 4) // 2
                    if h == 0:
                        pe.wait_ge(f_vec, l * 11 + 1)
                    if h >= 2:
                        pe.wait_ge(s2_masked, l * 8 + h - 1)
                    if forgets:
                        pe.wait_ge(m2_evict, l * 18 + V_AQ + k + 1)
                        pe.wait_ge(f_vec, l * 11 + 11)
                    else:
                        pe.wait_ge(rot_done, l * 4 + k + 1)
                    for qs, ks, dst in ((slice(0, P), P, b[:, 0:P]), (slice(P, T), T, b[:, P:3 * P])):
                        i = nc.tensor.matmul(dst, qk[r, q, qs], qk[r, k, 0:ks], start=True, stop=not forgets)
                        if forgets:
                            i = nc.tensor.matmul(dst, ident[0:4, h - 4:h - 3].to_broadcast([4, P]),
                                                 neg_m[0:4, 0:ks], start=False, stop=True)
                    i.then_inc(s2_ready, 1)

                def turn_a(h):
                    pe.wait_ge(q2_ready, l * 8 + h + 1)
                    if h > 0:
                        pe.wait_ge(a2_stored, l * 8 + h)
                    else:
                        pe.wait_ge(rot_done, l * 4 + 4)
                    for b in range(3):
                        r = nc.tensor.transpose(side[2][:, blk(b)], sm[:, h % 2, blk(b)], ident)
                    r.then_inc(a2_turned, 1)

                def turn_v(n):
                    pe.wait_ge(m2_evict, l * 18 + V_AV + n + 1)
                    if n > 0:
                        pe.wait_ge(v2_stored, l * 4 + n)
                    for a in range(QT):
                        r = nc.tensor.transpose(tr[:, a * P:(a + 1) * P], vT[:, n % 2, a * P:(a + 1) * P], ident)
                    r.then_inc(v2_turned, 1)

                def values(j):
                    dst = side[3 if j % 2 == 0 else 0]
                    pe.wait_ge(v2_stored, l * 4 + j + 1)
                    pe.wait_ge(a2_stored, l * 8 + 2 * j + 2)
                    if j == 0:
                        pe.wait_ge(d_ready, l + 1)
                    elif j == 1:
                        pe.wait_ge(s2_masked, l * 8 + 8)
                    else:
                        pe.wait_ge(ab_split, l * 4 + j - 1)
                    for h in (2 * j, 2 * j + 1):
                        r = slice(64 * (h % 2), 64 * (h % 2) + 64)
                        nc.tensor.matmul(dst[r, 0:T], v_tok[:, j, 0, r], aT8[:, h, 0:T], start=True, stop=False)
                        i = nc.tensor.matmul(dst[r, P:T], v_tok[:, j, 1, r], aT8[:, h, T:], start=False, stop=True)
                    i.then_inc(o2_ready, 1)

                for i in range(G_MIX2 * RING):
                    if i == 3:
                        turn_gv()
                    if V_AQ + 1 <= i <= V_AQ + 4:
                        swap(i - V_AQ - 1)
                    if i == 8:
                        spatial()
                    if i == 13:
                        pooling()
                    if S2 + 2 <= i < S2 + 10:
                        turn_a(i - S2 - 2)
                    if S2 <= i < S2 + 8:
                        scores(i - S2)
                    if V_AV + 2 <= i < V_AV + 6:
                        turn_v(i - V_AV - 2)
                    if V_NONE <= i <= V_NONE + 1:
                        values(i - V_NONE)
                    if i == V_OUT:
                        values(2)
                        values(3)
                    if V_NONE <= i < V_OUT:
                        continue
                    g, s = g0 + i // RING, i % RING
                    unit(g, s)
                    if i < V_NONE:
                        if i >= 3:
                            pe.wait_ge(m2_evict, l * 18 + i - 2)
                        for k in range(KT):
                            if i == 0:
                                pe.wait_ge(h_split, hb + k + 1)
                            r = product(o_tile[i % 3], s, k, h_hi[:, k], h_lo[:, k], k == 0, k == KT - 1)
                        r.then_inc(unit_done, V_OUT - V_NONE + 1 if i == V_NONE - 1 else 1)
                        if i == 0:
                            forget()
                    else:
                        m = i - V_OUT
                        if m >= 3:
                            pe.wait_ge(z_ready, l * (2 * KT) + 4 + m - 2)
                        else:
                            pe.wait_ge(m2_evict, l * 18 + 18)
                        for n, k in enumerate(K_OUT):
                            if i == V_OUT:
                                pe.wait_ge(cd_split if k >= 4 else ab_split, l * 4 + k % 4 + 1)
                            r = product(o_tile[i % 3], s, k, ya_hi[:, k], ya_lo[:, k], n == 0, n == KT - 1)
                        r.then_inc(unit_done, 1)
                layer_norm(l, 0)

            pe.wait_ge(ones_in, 16)
            with pe.Fori(0, DEPTH) as l:
                g = l * G_L1
                ffn(l, 0, g)
                pe.wait_ge(consts_in, 16)
                pe.wait_ge(par_in, l * 16 + 16)
                mixer(l, g + G_FFN)
                ffn(l, 1, g + G_FFN + G_MIX)
            with pe.Fori(0, DEPTH) as l:
                pe.wait_ge(par_in, l * 16 + 16 * (DEPTH + 1))
                g = l * G_L2 + G_B2
                mixer2(l, g)
                conv_ffn(l, g + G_MIX2)


def cols(a):
    import numpy as np
    return np.ascontiguousarray(a.reshape(-1, P).T)


def tiles(w):
    import numpy as np
    k, m = w.shape
    return np.ascontiguousarray(w.reshape(k // P, P, m // P, P).transpose(2, 1, 0, 3)).reshape(m // P, P, k)


def down_units(w):
    import numpy as np
    t = tiles(w).reshape(KT, P, NF, P)
    t = np.concatenate([t, np.zeros((KT, P, DOWN_PARTS * KT - NF, P), t.dtype)], axis=2)
    t = t.reshape(KT, P, DOWN_PARTS, KT * P).transpose(0, 2, 1, 3)
    return np.ascontiguousarray(t).reshape(KT * DOWN_PARTS, P, KT * P)


def constants():
    import numpy as np
    c = np.zeros((P, NC), np.float32)

    def put(name, a):
        c[:, CC[name]:CC[name] + a.shape[1]] = a

    put("ident", np.eye(P, dtype=np.float32))
    put("ones_model", np.full((P, P), 1.0 / D, np.float32))
    put("ones_head", np.full((P, P), 1.0 / P, np.float32))
    put("ones", np.ones((P, P), np.float32))
    tri = np.where(np.arange(P)[None, :] <= np.arange(P)[:, None], 0.0, NEG).astype(np.float32)
    put("mask_rows", np.concatenate([tri, np.zeros((P, P), np.float32), tri], axis=1))
    put("mask_cols", (np.arange(P)[:, None] <= np.arange(P)[None, :]).astype(np.float32))
    inv_freq = np.float32(500000.0) ** (-np.arange(0, 16, 2, dtype=np.float32) / np.float32(16))
    ang = np.arange(T, dtype=np.float32)[None, :] * inv_freq[:, None]
    cos, sin, swap = np.ones((P, T), np.float32), np.zeros((P, T), np.float32), np.zeros((P, P), np.float32)
    for head in (0, 64):
        for d in range(8):
            cos[head + d] = cos[head + 8 + d] = np.cos(ang[d])
            sin[head + d] = sin[head + 8 + d] = np.sin(ang[d])
            swap[head + 8 + d, head + d] = -1.0
            swap[head + d, head + 8 + d] = 1.0
    put("rot_cos", cos)
    put("rot_sin", sin)
    put("rot_swap", swap)
    inv = np.stack([np.repeat(1.0 / np.minimum(np.arange(T) + 1, w)[None, :], 64, axis=0) for w in (2, 4, 8, 16)])
    put("inv_count", inv.reshape(2, P, T).transpose(1, 0, 2).reshape(P, 2 * T).astype(np.float32))
    return c


def pack1(v, l):
    import math
    import numpy as np
    c = np.zeros((P, NPAR), np.float32)

    def put(name, a):
        c[:a.shape[0], C1[name]:C1[name] + a.shape[1]] = a

    for name, key in (("mix_pre", "mix_norm_pre"), ("mix_post", "mix_norm_post"), ("attn_norm", "attn_norm_w"),
                      ("mlstm_norm", "mlstm_norm_w"), ("conv_b", "conv_b"), ("gate_b", "gate_b")):
        put(name, cols(v[key][l]))
    lam_init = 0.8 - 0.6 * math.exp(-0.3 * l)
    put("lam_init", np.full((P, 1), lam_init, np.float32))
    put("one_minus_lam_init", np.full((P, 1), 1.0 - lam_init, np.float32))
    put("conv_w", cols(v["conv_w"][l]))
    put("lam", np.stack([v[f"attn_lam_{n}"][l] for n in ("q1", "k1", "q2", "k2")], axis=1))
    c[0:HEADS, C1["igate_b"]] = v["igate_b"][l]
    c[32:32 + HEADS, C1["fgate_b"]] = v["fgate_b"][l]
    at = 6144
    g = v["w_in"][l][:, at:at + 2 * HEADS].reshape(KT, P, 2, HEADS).transpose(1, 0, 2, 3)
    w = np.zeros((P, KT, 2, 32), np.float32)
    w[:, :, :, 0:HEADS] = g
    put("w_gates", w.reshape(P, KT * 64))
    return c


def pack_gains(v):
    import numpy as np
    first = [cols(v[n.replace("_", "_norm_")][l]) for l in range(DEPTH) for n in GAINS1]
    second = [cols(v[n + "_2"][l]) for l in range(DEPTH) for n in GAINS2]
    return np.concatenate(first + [np.ones((P, KT), np.float32)] + second, axis=1)


def mix1(v, l):
    import numpy as np
    w = v["w_in"][l]
    q, k, va, mqk, mv, mo, gl = (w[:, a:b] for a, b in ((0, 1024), (1024, 2048), (2048, 3072), (3072, 4096),
                                                        (4096, 5120), (5120, 6144), (6160, 8208)))
    heads = np.stack([tiles(a) for a in (q, k, va)], axis=1).reshape(3 * HEADS, P, D)
    return np.concatenate([heads] + [tiles(a) for a in (mo, mqk, mv, gl, v["w_proj_a"][l], v["w_proj_m"][l],
                                                        v["w_out"][l])])


def up_units(w):
    import numpy as np
    t = tiles(w).reshape(2, NF, P, D)
    return np.ascontiguousarray(t.transpose(1, 0, 2, 3)).reshape(2 * NF, P, D)


def model_in(x):
    import numpy as np
    return np.ascontiguousarray(x.reshape(T, KT, P).transpose(2, 1, 0))


def model_out(a):
    import numpy as np
    return np.ascontiguousarray(a.transpose(2, 1, 0)).reshape(1, T, D)


def pack2(v, l):
    import numpy as np
    c = np.zeros((P, NPAR), np.float32)

    def put(name, a):
        c[:a.shape[0], C2[name]:C2[name] + a.shape[1]] = a

    for name, key in (("conv_w", "conv_w_2"), ("conv_b", "conv_b_2"), ("pool_scale", "pool_scale_2")):
        put(name, cols(v[key][l]))
    put("b_forget", v["b_forget_2"][l][:, None])
    w = np.zeros((P, KT, 32), np.float32)
    w[:, :, 0:4] = v["w_in_2"][l][:, 1536:1540].reshape(KT, P, 4).transpose(1, 0, 2)
    put("w_forget", w.reshape(P, KT * 32))
    put("sgu_w", v["sgu_w_2"][l].transpose(2, 0, 1).reshape(P, 4 * P))
    w = np.zeros((P, 2, P), np.float32)
    for g in range(4):
        r = slice(64 * (g % 2), 64 * (g % 2) + 64)
        w[r, g // 2, r] = v["pool_w_2"][l][g]
    put("pool_w", w.reshape(P, 2 * P))
    put("sgu_g", np.broadcast_to(v["sgu_ln_g_2"][l], (P, T)))
    put("sgu_b_ln", np.broadcast_to(v["sgu_ln_b_2"][l], (P, T)))
    put("sgu_b", v["sgu_b_2"][l])
    return c


def mix2(v, l):
    import numpy as np
    w = v["w_in_2"][l]
    aq, ak, av, bq, bk, bv, cu, cv, dp = (w[:, a:a + 256] for a in (0, 256, 512, 768, 1024, 1280, 1540, 1796, 2052))
    none = np.zeros((2, P, D), np.float32)
    return np.concatenate([tiles(a) for a in (cv, cu, dp, aq, ak, bq, bk, av, bv)] + [none, tiles(v["w_o_2"][l])])


_INS = ["x", "consts", "gains", "params", "w_up1", "w_down1", "w_mix1", "w_mix2", "w_up2", "w_down2"]


def layout(v):
    import numpy as np
    ffns = [(v[n + "_w_gu"][l], v[n + "_w_down"][l]) for l in range(DEPTH) for n in ("ffn1", "ffn2")]
    both = range(DEPTH)
    return {
        "x": model_in(v["x"][0]),
        "consts": constants(),
        "gains": pack_gains(v),
        "params": np.stack([pack1(v, l) for l in both] + [pack2(v, l) for l in both]),
        "w_up1": np.concatenate([up_units(a) for a, _ in ffns]),
        "w_down1": np.concatenate([down_units(b) for _, b in ffns]),
        "w_mix1": np.concatenate([mix1(v, l) for l in both]),
        "w_mix2": np.concatenate([mix2(v, l) for l in both]),
        "w_up2": np.concatenate([up_units(v["w_up_2"][l]) for l in both]),
        "w_down2": np.concatenate([down_units(v["w_down_2"][l]) for l in both]),
    }


def kernel(**inputs):
    import numpy as np
    import concourse.bacc as bacc
    from concourse.bass_utils import run_bass_kernel_spmd

    arrays = layout({k: np.asarray(a) for k, a in inputs.items()})
    nc = bacc.Bacc("TRN2", target_bir_lowering=False, num_devices=1)
    args = [nc.dram_tensor("in_" + n, arrays[n].shape, F32, kind="ExternalInput").ap() for n in _INS]
    args.append(nc.dram_tensor("out_x", (P, KT, T), F32, kind="ExternalOutput").ap())
    build(nc, *args)
    r = run_bass_kernel_spmd(nc, [{"in_" + n: arrays[n] for n in _INS}], core_ids=[0])
    return model_out(r.results[0]["out_x"])
```
